# Optimizing a Trainium2 kernel written in Bass

```python
import math
import jax, jax.numpy as jnp
from jax import lax
import numpy as np

D_MODEL = 1024
BATCH = 1
SEQ = 128
DEPTH = 2
DEC_BATCH = 1
DEC_SEQ = 512
PAST_LEN = 128

GRID_W = 64
BLOCK = 128
WINDOW = 128
N_HEADS = 8
N_KV = 2
HEAD_DIM = 64
Q_GROUP = N_HEADS // N_KV
ATTN_W = N_HEADS * HEAD_DIM
KV_W = N_KV * HEAD_DIM
HY_W = 256
GM_W = 256
GM_HEADS = 4
GM_HEAD_DIM = GM_W // GM_HEADS
GM_CHUNK = 128
MIX_W = ATTN_W + HY_W + GM_W
IN_W = ATTN_W + 2 * KV_W + 3 * HY_W + 2 * GM_W
SHORT_CONV = 3
FILTER_EMB = 33
FILTER_HID = 64
HY_DECAY_HI_PCT = 0.3
HY_DECAY_LO_PCT = 1.5
HY_DECAY_TARGET = 1e-2
N_EXPERTS = 16
EC_CAPACITY = 2
D_EXPERT = 1024
ROPE_THETA = 10000.0
EPS = 1e-6
NEG = -1e30

kernel_name = 'hybrid_prefix_diffusion_step'

def _rmsnorm(x, g):
    xf = x.astype(jnp.float32)
    y = xf * lax.rsqrt(jnp.mean(xf * xf, axis=-1, keepdims=True) + EPS)
    return (y * g.astype(jnp.float32)).astype(x.dtype)

def _modulate(x, g, shift, scale):
    return _rmsnorm(x, g) * (1 + scale) + shift

def _axial_rope(x):
    L = x.shape[1]
    t = jnp.arange(L)
    half = HEAD_DIM // 2
    nf = half // 2
    inv = ROPE_THETA ** (-jnp.arange(nf, dtype=jnp.float32) / nf)

    def rot(xa, pos):
        ang = pos.astype(jnp.float32)[:, None] * inv[None, :]
        cos = jnp.cos(ang)[None, :, None, :].astype(x.dtype)
        sin = jnp.sin(ang)[None, :, None, :].astype(x.dtype)
        x1, x2 = xa[..., :nf], xa[..., nf:]
        return jnp.concatenate([x1 * cos - x2 * sin, x2 * cos + x1 * sin], axis=-1)

    return jnp.concatenate([rot(x[..., :half], t // GRID_W), rot(x[..., half:], t % GRID_W)], axis=-1)

def _attend(q, k, v, bias, sink):
    s = jnp.einsum('bqkgd,bskd->bkgqs', q, k).astype(jnp.float32) * (1.0 / math.sqrt(HEAD_DIM))
    if bias is not None:
        s = s + bias
    sk = jnp.broadcast_to(sink.astype(jnp.float32).reshape(1, N_KV, Q_GROUP, 1, 1), s.shape[:-1] + (1,))
    p = jax.nn.softmax(jnp.concatenate([s, sk], axis=-1), axis=-1)[..., :-1]
    return jnp.einsum('bkgqs,bskd->bqkgd', p.astype(v.dtype), v)

def _ctx_attention(q, k, v, sink):
    B, L = q.shape[:2]
    nb = L // BLOCK
    qb = q.reshape(B, nb, BLOCK, N_KV, Q_GROUP, HEAD_DIM).transpose(1, 0, 2, 3, 4, 5)
    out = lax.map(lambda qi: _attend(qi, k, v, None, sink), qb)
    return out.transpose(1, 0, 2, 3, 4, 5).reshape(B, L, ATTN_W)

def _latent_attention(q, k, v, ck, cv, sink):
    B, L = q.shape[:2]
    nb = L // BLOCK
    P = ck.shape[1]
    pad = ((0, 0), (BLOCK, BLOCK), (0, 0), (0, 0))
    kp, vp = jnp.pad(k, pad), jnp.pad(v, pad)
    ck, cv = ck.astype(k.dtype), cv.astype(v.dtype)
    qb = q.reshape(B, nb, BLOCK, N_KV, Q_GROUP, HEAD_DIM).transpose(1, 0, 2, 3, 4, 5)
    rel = jnp.arange(3 * BLOCK)[None, :] - BLOCK - jnp.arange(BLOCK)[:, None]
    band = jnp.abs(rel) <= WINDOW
    ctx_bias = jnp.zeros((BLOCK, P), jnp.float32)

    def block(args):
        i, qi = args
        start = i * BLOCK
        kw = lax.dynamic_slice_in_dim(kp, start, 3 * BLOCK, axis=1)
        vw = lax.dynamic_slice_in_dim(vp, start, 3 * BLOCK, axis=1)
        kpos = start - BLOCK + jnp.arange(3 * BLOCK)
        valid = band & ((kpos >= 0) & (kpos < L))[None, :]
        bias = jnp.concatenate([jnp.where(valid, 0.0, NEG).astype(jnp.float32), ctx_bias], axis=1)
        return _attend(qi, jnp.concatenate([kw, ck], axis=1), jnp.concatenate([vw, cv], axis=1), bias, sink)

    out = lax.map(block, (jnp.arange(nb), qb))
    return out.transpose(1, 0, 2, 3, 4, 5).reshape(B, L, ATTN_W)

def _hyena_filter(L, w1, b1, w2, b2, w3, freq):
    f32 = jnp.float32
    t = jnp.linspace(0.0, 1.0, L, dtype=f32)[:, None]
    bands = (FILTER_EMB - 1) // 2
    fb = jnp.linspace(1e-4, bands - 1, bands, dtype=f32)[None, :]
    w = 2.0 * math.pi * jnp.arange(L, dtype=f32)[:, None] / L
    feats = jnp.concatenate([t, jnp.cos(fb * w), -jnp.sin(fb * w)], axis=-1)
    fr = freq.astype(f32)
    h = jnp.sin(fr * (feats @ w1.astype(f32) + b1.astype(f32)))
    h = jnp.sin(fr * (h @ w2.astype(f32) + b2.astype(f32)))
    h = h @ w3.astype(f32)
    decay_hi = math.log(HY_DECAY_TARGET) / HY_DECAY_HI_PCT
    decay_lo = math.log(HY_DECAY_TARGET) / HY_DECAY_LO_PCT
    deltas = jnp.abs(jnp.linspace(decay_lo, decay_hi, HY_W, dtype=f32))
    window = jnp.exp(-t * deltas[None, :])
    h_fwd = h[:, :HY_W] * window
    h_bwd = h[:, HY_W:] * window
    return jnp.concatenate([h_fwd, jnp.zeros((1, HY_W), f32), h_bwd[1:][::-1]], axis=0)

def _hyena(z, conv_w, conv_b, w1, b1, w2, b2, w3, freq, d_bias):
    L = z.shape[1]
    r = SHORT_CONV // 2
    zp = jnp.pad(z, ((0, 0), (r, r), (0, 0)))
    z = sum(zp[:, j:j + L] * conv_w[j] for j in range(SHORT_CONV)) + conv_b
    x0, x1, v = jnp.split(z, 3, axis=-1)
    u = (x1 * v).astype(jnp.float32)
    hc = _hyena_filter(L, w1, b1, w2, b2, w3, freq)
    uf = jnp.fft.rfft(u, n=2 * L, axis=1)
    hf = jnp.fft.rfft(hc, n=2 * L, axis=0)
    y = jnp.fft.irfft(uf * hf[None], n=2 * L, axis=1)[:, :L] + u * d_bias.astype(jnp.float32)
    return (x0.astype(jnp.float32) * y).astype(z.dtype)

def _gmlp(z, ws, b):
    B, L = z.shape[:2]
    u, v = jnp.split(jax.nn.gelu(z), 2, axis=-1)
    vc = v.reshape(B, L // GM_CHUNK, GM_CHUNK, GM_HEADS, GM_HEAD_DIM)
    s = jnp.einsum('hpq,bnqhc->bnphc', ws, vc) + b.T[None, None, :, :, None]
    return u * s.reshape(B, L, GM_W)

def _expert_choice(h, router_w, w1, w3, w2):
    B, L, D = h.shape
    xs = h.reshape(B * L, D)
    N = B * L
    C = max(1, EC_CAPACITY * N // N_EXPERTS)
    aff = jax.nn.softmax((xs @ router_w).astype(jnp.float32), axis=-1)
    gate, idx = lax.top_k(aff.T, C)
    xe = xs[idx]
    he = jax.nn.silu(jnp.einsum('ecd,edf->ecf', xe, w1)) * jnp.einsum('ecd,edf->ecf', xe, w3)
    ye = jnp.einsum('ecf,efd->ecd', he, w2) * gate[..., None].astype(h.dtype)
    out = jnp.zeros_like(xs).at[idx.reshape(-1)].add(ye.reshape(-1, D))
    return out.reshape(B, L, D)

def _layer(x, mod, lp, ctx_k=None, ctx_v=None):
    shift1, scale1, gate1, shift2, scale2, gate2 = jnp.split(mod, 6, axis=-1)
    B, L, _ = x.shape
    h = _modulate(x, lp['norm1_g'], shift1, scale1)
    z = h @ lp['w_in']
    o = 0
    q = z[..., o:o + ATTN_W].reshape(B, L, N_HEADS, HEAD_DIM)
    o += ATTN_W
    k = z[..., o:o + KV_W].reshape(B, L, N_KV, HEAD_DIM)
    o += KV_W
    v = z[..., o:o + KV_W].reshape(B, L, N_KV, HEAD_DIM)
    o += KV_W
    zh = z[..., o:o + 3 * HY_W]
    o += 3 * HY_W
    zg = z[..., o:o + 2 * GM_W]
    if ctx_k is None:
        a = _ctx_attention(q, k, v, lp['attn_sink'])
    else:
        a = _latent_attention(_axial_rope(q), _axial_rope(k), v, ctx_k, ctx_v, lp['attn_sink'])
    yh = _hyena(zh, lp['hy_conv_w'], lp['hy_conv_b'], lp['hy_f_w1'], lp['hy_f_b1'], lp['hy_f_w2'],
                lp['hy_f_b2'], lp['hy_f_w3'], lp['hy_freq'], lp['hy_bias'])
    yg = _gmlp(zg, lp['gm_ws'], lp['gm_b'])
    g = lp['out_norm_g']
    mixed = jnp.concatenate([_rmsnorm(a, g[:ATTN_W]),
                             _rmsnorm(yh, g[ATTN_W:ATTN_W + HY_W]),
                             _rmsnorm(yg, g[ATTN_W + HY_W:])], axis=-1) @ lp['w_out']
    x = x + gate1 * mixed
    h = _modulate(x, lp['norm2_g'], shift2, scale2)
    x = x + gate2 * _expert_choice(h, lp['router_w'], lp['exp_w1'], lp['exp_w3'], lp['exp_w2'])
    return x, k, v

def setup_inputs(seed: int = 0) -> dict:
    key = jax.random.key(seed)
    ks = jax.random.split(key, 32)

    def nrm(k, shape, scale):
        return jax.random.normal(k, shape, jnp.float32) * scale

    D, NL = D_MODEL, DEPTH
    return {
        'x_prompt': nrm(ks[0], (BATCH, SEQ, D), 1.0),
        'x_sample': nrm(ks[1], (DEC_BATCH, DEC_SEQ, D), 1.0),
        'c': nrm(ks[2], (DEC_BATCH, D), 1.0),
        'cache_k': nrm(ks[3], (DEC_BATCH, DEPTH, PAST_LEN, N_KV, HEAD_DIM), 1.0),
        'cache_v': nrm(ks[4], (DEC_BATCH, DEPTH, PAST_LEN, N_KV, HEAD_DIM), 1.0),
        'c_ctx': nrm(ks[5], (D,), 1.0),
        'norm1_g': 1.0 + nrm(ks[6], (NL, D), 0.02),
        'norm2_g': 1.0 + nrm(ks[7], (NL, D), 0.02),
        'ada_w': nrm(ks[8], (NL, D, 6 * D), D ** -0.5),
        'ada_b': nrm(ks[9], (NL, 6 * D), 0.01),
        'w_in': nrm(ks[10], (NL, D, IN_W), D ** -0.5),
        'attn_sink': nrm(ks[11], (NL, N_HEADS), 0.5),
        'hy_conv_w': nrm(ks[12], (NL, SHORT_CONV, 3 * HY_W), SHORT_CONV ** -0.5),
        'hy_conv_b': nrm(ks[13], (NL, 3 * HY_W), 0.01),
        'hy_f_w1': nrm(ks[14], (NL, FILTER_EMB, FILTER_HID), FILTER_EMB ** -0.5),
        'hy_f_b1': nrm(ks[15], (NL, FILTER_HID), 0.1),
        'hy_f_w2': nrm(ks[16], (NL, FILTER_HID, FILTER_HID), FILTER_HID ** -0.5),
        'hy_f_b2': nrm(ks[17], (NL, FILTER_HID), 0.1),
        'hy_f_w3': nrm(ks[18], (NL, FILTER_HID, 2 * HY_W), FILTER_HID ** -0.5),
        'hy_freq': 1.0 + nrm(ks[19], (NL, FILTER_HID), 0.1),
        'hy_bias': nrm(ks[20], (NL, HY_W), 0.1),
        'gm_ws': nrm(ks[21], (NL, GM_HEADS, GM_CHUNK, GM_CHUNK), GM_CHUNK ** -0.5),
        'gm_b': 1.0 + nrm(ks[22], (NL, GM_HEADS, GM_CHUNK), 0.01),
        'out_norm_g': 1.0 + nrm(ks[23], (NL, MIX_W), 0.02),
        'w_out': nrm(ks[24], (NL, MIX_W, D), MIX_W ** -0.5),
        'router_w': nrm(ks[25], (NL, D, N_EXPERTS), D ** -0.5),
        'exp_w1': nrm(ks[26], (NL, N_EXPERTS, D, D_EXPERT), D ** -0.5),
        'exp_w3': nrm(ks[27], (NL, N_EXPERTS, D, D_EXPERT), D ** -0.5),
        'exp_w2': nrm(ks[28], (NL, N_EXPERTS, D_EXPERT, D), D_EXPERT ** -0.5),
        'final_g': 1.0 + nrm(ks[29], (D,), 0.02),
    }

def reference(x_prompt, x_sample, c, cache_k, cache_v, c_ctx, norm1_g, norm2_g, ada_w, ada_b, w_in,
              attn_sink, hy_conv_w, hy_conv_b, hy_f_w1, hy_f_b1, hy_f_w2, hy_f_b2, hy_f_w3, hy_freq,
              hy_bias, gm_ws, gm_b, out_norm_g, w_out, router_w, exp_w1, exp_w3, exp_w2, final_g):
    xp, xs = x_prompt, x_sample
    ks, vs = [], []
    for l in range(DEPTH):
        lp = {
            'norm1_g': norm1_g[l], 'norm2_g': norm2_g[l], 'w_in': w_in[l], 'attn_sink': attn_sink[l],
            'hy_conv_w': hy_conv_w[l], 'hy_conv_b': hy_conv_b[l], 'hy_f_w1': hy_f_w1[l],
            'hy_f_b1': hy_f_b1[l], 'hy_f_w2': hy_f_w2[l], 'hy_f_b2': hy_f_b2[l], 'hy_f_w3': hy_f_w3[l],
            'hy_freq': hy_freq[l], 'hy_bias': hy_bias[l], 'gm_ws': gm_ws[l], 'gm_b': gm_b[l],
            'out_norm_g': out_norm_g[l], 'w_out': w_out[l], 'router_w': router_w[l],
            'exp_w1': exp_w1[l], 'exp_w3': exp_w3[l], 'exp_w2': exp_w2[l],
        }
        mod_ctx = (jax.nn.silu(c_ctx) @ ada_w[l] + ada_b[l])[None, None, :]
        mod_lat = (jax.nn.silu(c) @ ada_w[l] + ada_b[l])[:, None, :]
        xp, k_l, v_l = _layer(xp, mod_ctx, lp)
        xs, _, _ = _layer(xs, mod_lat, lp, cache_k[:, l], cache_v[:, l])
        ks.append(k_l)
        vs.append(v_l)
    y_prompt = _rmsnorm(xp, final_g)
    y_sample = _rmsnorm(xs, final_g)
    new_cache_k = jnp.stack(ks, axis=1)
    new_cache_v = jnp.stack(vs, axis=1)
    return (y_prompt, y_sample, new_cache_k, new_cache_v)


_drawn_inputs = setup_inputs


def setup_inputs(seed=0):
    import zlib

    import numpy as np

    out = dict(_drawn_inputs(seed))
    spreads = {}
    factors = {'attn_sink': 8.0,
     'gm_b': 52.997,
     'final_g': 25.049,
     'hy_conv_b': 4.095,
     'out_norm_g': 2.694,
     'norm2_g': 2.975}
    for name, (base, spread) in spreads.items():
        noise = np.random.default_rng([zlib.crc32(name.encode()), seed]).standard_normal(out[name].shape)
        drawn = base * np.exp(spread * noise) if base else spread * noise
        out[name] = __import__('jax').numpy.asarray(drawn.astype(out[name].dtype))
    for name, factor in factors.items():
        out[name] = (out[name] * factor).astype(out[name].dtype)
    return out
```

```python
from contextlib import ExitStack

import concourse.bass as bass
from concourse import mybir

ALU = mybir.AluOpType
ACT = mybir.ActivationFunctionType
F32 = mybir.dt.float32
F32R = mybir.dt.float32r
U32 = mybir.dt.uint32
AX_X = mybir.AxisListType.X

P = 128
D = 1024
DEPTH = 2
LAT, CTX = 512, 128
NT = (LAT + CTX) // P
TOK = LAT + CTX
KC = D // P
HEADS, KV, HD = 8, 2, 64
ATT, KVW = HEADS * HD, KV * HD
HY, GM = 256, 256
GH = 4
TAPS = 3
EMB, FH = 33, 64
EXPERTS = 16
CAP_L, CAP_C = 2 * LAT // EXPERTS, 2 * CTX // EXPERTS
CAP = CAP_L + CAP_C
EPS = 1e-6
SLOTS = 3
ADA = 6
ROUNDS = ADA // SLOTS + 1
PAIRS = EXPERTS // 2
HALF = KC // 2
MATS = 3 * EXPERTS
AHEAD = 4 * KC
SCALE = HD ** -0.5
NEG = -1e30
TWO_PI_HI, TWO_PI_LO = 6.28125, 6.283185307179586 - 6.28125
ROUND = 1.5 * 2.0 ** 23
PI_IN = 3.1415925

G1, G2, GO, CW, CB, GB, SK, FB1, FB2, FQ, NPRM = 0, 8, 16, 24, 42, 48, 52, 60, 61, 62, 64
C_ID, C_MASK, C_COS, C_SIN, C_ONE, NCST = 0, 128, 640, 896, 1024, 1152

V_LAYER, V_LAST = 138, 5
A_LAYER = 8


def hold(eng, s, value, done):
    value = eng.to_reg(value)
    eng.wait_ge(done, 32)
    eng.wait_ge(s, value)


def w3_at(e):
    return e * 3 + 1


def w1_next_at(e):
    return e * 3 + 2


def w2_at(e):
    return MATS - 1 if isinstance(e, int) and e == EXPERTS - 1 else e * 3 + 3


class Chain:

    def __init__(self, eng, sem, name, base, expect):
        self.eng, self.sem, self.base, self.n, self.expect, self.name = eng, sem, base, 0, expect, name

    def held(self, ins, done):
        self.n += 1
        ins.then_inc(self.sem, 1)
        hold(self.eng, self.sem, self.base + self.n, done)

    def __call__(self, ins):
        self.n += 1
        ins.then_inc(self.sem, 1)
        self.eng.wait_ge(self.sem, self.base + self.n)

    def close(self):
        assert self.n == self.expect, f"{self.name} has {self.n} links"


def hybrid_prefix_diffusion_step(nc, i, o):
    x_res = nc.dram_tensor("x_res", [TOK, D], F32).ap()
    xn_dram = nc.dram_tensor("xn_dram", [TOK, D], F32).ap()

    with ExitStack() as ctx:
        def sb(name, shape, dt=F32):
            return ctx.enter_context(nc.sbuf_tensor(name, shape, dt))

        def sb_twice(name, shape):
            with nc.sbuf_tensor(name, shape, F32) as plain:
                pass
            return plain, sb(name + "_r", shape, F32R)

        def sem(name):
            return ctx.enter_context(nc.semaphore(name))

        bank = [ctx.enter_context(nc.psum_tensor(f"bank{n}", [P, 512], F32)) for n in range(8)]
        ring, ring_r = sb_twice("ring", [P, SLOTS, KC * D])
        slot = [ring[:, s, :].rearrange("p (c n) -> p c n", c=KC) for s in range(SLOTS)]
        slot_r = [ring_r[:, s, :].rearrange("p (c n) -> p c n", c=KC) for s in range(SLOTS)]
        hy = ring[:, 2, :]
        zhT = hy[:, 0:3840].rearrange("p (m t) -> p m t", m=6)
        dftc = hy[:, 3840:5888].rearrange("p (a k) -> p a k", a=4)
        dfts = hy[:, 5888:7936].rearrange("p (a k) -> p a k", a=4)
        dftcx, dftsx = hy[:, 7936:8064], hy[:, 8064:8192]
        arena_h, arena_hr = sb_twice("arena_h", [P, KC * TOK])
        hT = arena_h[:, :].rearrange("p (c t) -> p c t", c=KC)
        filc = arena_h[:, 0:2048].rearrange("p (a k) -> p a k", a=4)
        fils = arena_h[:, 2048:4096].rearrange("p (a k) -> p a k", a=4)
        filcx, filsx = arena_h[:, 4096:4224], arena_h[:, 4224:4352]
        feats = arena_h[0:EMB, 4352:4992]
        final_g = arena_h[:, 0:D]
        arena_z, arena_zr = sb_twice("arena_z", [P, NT * 1280])
        zt = arena_z[:, :].rearrange("p (t n) -> p t n", t=NT)
        win = arena_z[:, 0:1280].rearrange("p (t n) -> p t n", t=NT)
        fsum = arena_z[:, 1280:2560].rearrange("p (t n) -> p t n", t=NT)
        fdif = arena_z[:, 2560:3840].rearrange("p (t n) -> p t n", t=NT)
        hfw, hbw = arena_z[:, 3840:4096], arena_z[:, 4096:4352]
        pre, turns, hid = (arena_z[0:FH, a:a + TOK] for a in (4352, 4992, 5632))
        fw1, fw2 = arena_z[0:EMB, 6272:6336], arena_z[0:FH, 6336:6400]
        xe = [arena_z[0:CAP, a:a + D] for a in (0, 1024)]
        ye = [arena_z[0:CAP, a:a + D] for a in (2048, 3072)]
        he = arena_z[0:CAP, 4096:5120]
        heT = [arena_zr[:, a:a + KC * CAP].rearrange("p (c t) -> p c t", c=KC) for a in (5120, 5760)]
        arena_u, arena_ur = sb_twice("arena_u", [P, 6400])
        adab = [arena_u[0:2, a:a + D] for a in (0, 1024)]
        mrow = [arena_u[0:2, a:a + D] for a in (2048, 3072)]
        fw3 = arena_u[0:FH, 4096:4608]
        junk = arena_u[:, 5120:6144]
        x0c = arena_u[:, 0:1280].rearrange("p (m t) -> p m t", m=2)
        spec = [arena_u[:, 1280 * a:1280 * a + 1280] for a in range(5)]
        uT = spec[1].rearrange("p (m t) -> p m t", m=2)
        utok = spec[2].rearrange("p (t n) -> p t n", t=NT)
        cvt = spec[3][:, 0:TOK]
        prod = [spec[n].rearrange("p (j n) -> p j n", j=NT) for n in (1, 2, 3, 4)]
        yh = spec[2].rearrange("p (m t) -> p m t", m=2)
        ysq = spec[4].rearrange("p (m t) -> p m t", m=2)
        hms, hrc, hy_y, hya = spec[3][:, 0:TOK], spec[3][:, TOK:2 * TOK], spec[0][:, 0:TOK], spec[0][:, TOK:2 * TOK]
        qT = arena_u[:, 0:2560].rearrange("p (i t) -> p i t", i=4)
        kT = arena_u[:, 2560:3328]
        sbuf_s = [arena_u[:, 3328 + 512 * n:3840 + 512 * n] for n in range(2)]
        prob = [arena_u[:, 4352 + 512 * n:4864 + 512 * n] for n in range(2)]
        probT = [arena_u[:, 5376 + 512 * n:5888 + 512 * n] for n in range(2)]
        xn = arena_u[:, 0:5120].rearrange("p (t n) -> p t n", t=NT)
        xeT = [[arena_ur[:, a:a + KC * CAP].rearrange("p (c t) -> p c t", c=KC) for a in (b, b + 640)]
               for b in (0, 1280)]
        high = [arena_hr[:, c * D:(c + 1) * D] if c < 5 else arena_ur[:, 2560 + (c - 5) * D:2560 + (c - 4) * D]
                for c in range(KC)]
        spectrum = sb("spectrum", [P, 2, NT, HY])
        sflat = spectrum[:, :, :, :].rearrange("p a t n -> p (a t n)")
        g2e, s2e, xt = (sflat[:, a:a + KC * CAP].rearrange("p (c t) -> p c t", c=KC) for a in (640, 1280, 1920))
        affT = spectrum[0:EXPERTS, 0, 0:3, :].rearrange("p t n -> p (t n)")[:, 0:TOK]
        gate1 = sb("gate1", [P, 2, D])
        gate2 = sb("gate2", [CAP, D])
        cst = sb("cst", [P, NCST])
        ident = cst[:, C_ID:C_ID + P]
        mask = cst[:, C_MASK:C_MASK + 512]
        ones = cst[:, C_ONE:C_ONE + P]
        cos_t = cst[:, C_COS:C_COS + 256].rearrange("p (t n) -> p t n", t=4)
        sin_t = cst[:, C_SIN:C_SIN + 128].rearrange("p (t h n) -> p t h n", t=4, h=2)
        sel = sb("sel", [2, 2 * P + CAP])
        prm = sb("prm", [P, NPRM])
        wsT = sb("wsT", [P, GH, P])
        rw = sb("rw", [P, KC, EXPERTS])
        ck, cv = sb("ck", [P, KVW]), sb("cv", [P, KVW])
        rtmp = sb("rtmp", [P, 640])
        jk = sb("jk", [P, 512])
        dbias = rtmp[0:1, 0:HY]
        cvec = sb("cvec", [P, 2, KC])
        cs = sb("cs", [P, KC, 2])
        mod = sb("mod", [P, 4, KC, 2])
        nsink = sb("nsink", [P, HEADS])
        ssum, sms, srec, sroot, stmp = (sb(n, [P, 10]) for n in ("ssum", "sms", "srec", "sroot", "stmp"))
        negmax, rsum, esink, denom = (sb(n, [P, NT, HEADS]) for n in ("negmax", "rsum", "esink", "denom"))
        aff = sb("aff", [P, NT, EXPERTS])
        anm, asum, arec = (sb(n, [P, NT]) for n in ("anm", "asum", "arec"))
        topv = sb("topv", [EXPERTS, CAP])
        topi = sb("topi", [EXPERTS, CAP], U32)
        topf = sb("topf", [EXPERTS, CAP])
        idxT = sb("idxT", [CAP, EXPERTS + 1], U32)
        gateT = sb("gateT", [CAP, EXPERTS])
        icur = [sb(f"icur{n}", [CAP, 1], U32) for n in range(2)]
        iscat = [sb(f"iscat{n}", [CAP, 1], U32) for n in range(2)]

        arrived = [sem(f"arrived{s}") for s in range(SLOTS)]
        used = [sem(f"used{s}") for s in range(SLOTS)]
        dft_in = sem("dft_in")
        const_in = sem("const_in")
        c_in = sem("c_in")
        x_copied = sem("x_copied")
        cs_done = sem("cs_done")
        prm_in = sem("prm_in")
        fil_in = sem("fil_in")
        adab_in = [sem("adab_in0"), sem("adab_in1")]
        mrow_done = sem("mrow_done")
        mod_mm = sem("mod_mm")
        mod_out = sem("mod_out")
        f_mm = sem("f_mm")
        f_pre = sem("f_pre")
        f_sin = sem("f_sin")
        f3_mm = sem("f3_mm")
        f3_out = sem("f3_out")
        spec_mm = sem("spec_mm")
        spec_out = sem("spec_out")
        x_in = sem("x_in")
        sq1 = sem("sq1")
        rec1 = sem("rec1")
        root1 = sem("root1")
        xn1 = sem("xn1")
        t1_mm = sem("t1_mm")
        h1_v, h1_a = sem("h1_v"), sem("h1_a")
        z_mm = sem("z_mm")
        z_v, z_a = sem("z_v"), sem("z_a")
        kv_out = sem("kv_out")
        gm_mm = sem("gm_mm")
        gm_out = sem("gm_out")
        gm_sq = sem("gm_sq")
        u_done = sem("u_done")
        ut_mm = sem("ut_mm")
        ut_out = sem("ut_out")
        fwd_mm = sem("fwd_mm")
        y_done = sem("y_done")
        inv_mm = sem("inv_mm")
        yh_done = sem("yh_done")
        ysq_done = sem("ysq_done")
        yss_mm = sem("yss_mm")
        hrec = sem("hrec")
        hroot = sem("hroot")
        hy_done = sem("hy_done")
        rope_done = sem("rope_done")
        qk_mm = sem("qk_mm")
        qk_a = sem("qk_a")
        sc_mm = sem("sc_mm")
        sc_out = sem("sc_out")
        p_done = sem("p_done")
        pt_mm = sem("pt_mm")
        pt_v, pt_a = sem("pt_v"), sem("pt_a")
        pv_mm = sem("pv_mm")
        es_in = sem("es_in")
        es_out = sem("es_out")
        a_done = sem("a_done")
        a_sq = sem("a_sq")
        mrec = sem("mrec")
        mroot = sem("mroot")
        mixn = sem("mixn")
        mx_mm = sem("mx_mm")
        mx_out = sem("mx_out")
        xr_in = [sem(f"xr_in{t}") for t in range(NT)]
        wo_mm = sem("wo_mm")
        x1_done = sem("x1_done")
        sq2 = sem("sq2")
        rec2 = sem("rec2")
        root2 = sem("root2")
        xn2 = sem("xn2")
        x1_out = sem("x1_out")
        xn_out = sem("xn_out")
        t2_mm = sem("t2_mm")
        h2_v, h2_a = sem("h2_v"), sem("h2_a")
        lg_mm = sem("lg_mm")
        anm_done = sem("anm_done")
        aexp = sem("aexp")
        aff_done = sem("aff_done")
        affT_mm = sem("affT_mm")
        affT_out = sem("affT_out")
        top_done = sem("top_done")
        top_mm = sem("top_mm")
        top_out = sem("top_out")
        half_in = [[sem(f"half_in{n}_{h}") for h in range(2)] for n in range(SLOTS)]
        high_ready = sem("high_ready")
        low_ready = sem("low_ready")
        chunk_used = sem("chunk_used")
        icur_done = sem("icur_done")
        xe_in = [sem("xe_in0"), sem("xe_in1")]
        xeT_mm = sem("xeT_mm")
        xt_scaled = sem("xt_scaled")
        xt_done = sem("xt_done")
        xh_done = sem("xh_done")
        xeT_out = sem("xeT_out")
        silu = sem("silu")
        he_done = sem("he_done")
        heT_mm = sem("heT_mm")
        hh_done = sem("hh_done")
        heT_out = sem("heT_out")
        ye_done = sem("ye_done")
        scattered = sem("scattered")
        rows_free = sem("rows_free")
        fin_in = sem("fin_in")
        fsq, frec, froot, y_out_done = sem("fsq"), sem("frec"), sem("froot"), sem("y_out_done")
        y_out = sem("y_out")
        v_link, v_flink, a_link = sem("v_link"), sem("v_flink"), sem("a_link")

        proj = ([("q", t, "v") for t in range(NT)] + [("kv", t, "a") for t in range(NT)]
                + [("zh", 0, "v"), ("zh", 1, "v"), ("zhc", 0, "v")]
                + [("zh", m, "v") for m in range(2, 6)] + [("zhc", 2, "v")]
                + [("zg", t, "a") for t in range(NT)])
        NP_ = len(proj)
        Z_V, Z_A = (sum(p[2] == e for p in proj) for e in "va")

        def taken(n):
            e = proj[n][2]
            return (z_v if e == "v" else z_a), (Z_V if e == "v" else Z_A), sum(p[2] == e for p in proj[:n + 1])

        def multiplied(n):
            if n in (LAST_SLOT0, NP_ - 1):
                return used[0 if n == LAST_SLOT0 else 1], ROUNDS, 4
            return z_mm, NP_ - 2, n + 1 - (n > LAST_SLOT0)

        def proj_at(kind, t):
            return proj.index(next(p for p in proj if p[:2] == (kind, t)))

        LAST_SLOT0 = proj_at("zhc", 0)

        att = [(b, h) for b in range(NT) for h in range(HEADS)]

        def keys(b):
            if b == NT - 1:
                return [(LAT, P)], P
            blocks = [((b - 1) * P, P)] if b else []
            blocks += [(TOK, P), (b * P, 2 * P if b < 3 else P)]
            return blocks, 0 if b else P

        def values(b):
            if b == NT - 1:
                return [zt[:, b, 640:768]]
            v = [zt[:, b - 1, 640:768]] if b else []
            v += [cv[:, :], zt[:, b, 640:768]]
            return v + ([zt[:, b + 1, 640:768]] if b < 3 else [])

        MOD = [(0, "col"), (1, "col"), (2, "lat"), (2, "ctx"), (3, "col"), (4, "col"), (5, "cap")]
        spread = [1, 2, 4, 5, 6, 7]
        FWD = [6, 7, 0, 1, 2]

        def affinity_T(pe, l, t):
            pe.wait_ge(aff_done, l * NT + t + 1)
            if t:
                pe.wait_ge(affT_out, l * NT + t)
            pe.transpose(bank[7][0:EXPERTS, 0:P], aff[:, t, :], ident).then_inc(affT_mm, 1)

        def width(b):
            return sum(n for _, n in keys(b)[0])

        def chunks(l, m, c):
            return l * (MATS * KC) + m * KC + c + 1

        block = ctx.enter_context(nc.Block())

        @block.sync
        def _(sp):
            with sp.Fori(0, DEPTH) as l:
                for r in range(2):
                    for s in range(SLOTS):
                        j = SLOTS * r + s
                        if r == 0:
                            through = sp.to_reg(l * (MATS * KC) + AHEAD - (3, 1, 0)[s] * KC)
                        sp.wait_ge(used[s], l * ROUNDS + r + 1)
                        if r == 0:
                            sp.wait_ge(chunk_used, through)
                        sp.dma_start(slot[s], i["ada_w"][bass.ds(l, 1), :, j * D:(j + 1) * D]
                                     .rearrange("a (p c) n -> (a p) c n", p=P)).then_inc(arrived[s], 16)
                for s in range(2):
                    sp.wait_ge(used[s], l * ROUNDS + 3)
                    sp.dma_start(slot[s], i["w_in"][bass.ds(l, 1), :, s * D:(s + 1) * D]
                                 .rearrange("a (p c) n -> (a p) c n", p=P)).then_inc(arrived[s], 16)
                sp.wait_ge(used[2], l * ROUNDS + 3)
                sp.dma_start(dftc, i["dft_cos"].rearrange("(a p) k -> p a k", p=P)).then_inc(dft_in, 16)
                sp.dma_start(dfts, i["dft_sin"].rearrange("(a p) k -> p a k", p=P)).then_inc(dft_in, 16)
                sp.dma_start(dftcx, i["dftx_cos"]).then_inc(dft_in, 16)
                sp.dma_start(dftsx, i["dftx_sin"]).then_inc(dft_in, 16)
                sp.wait_ge(inv_mm, l + 1)
                sp.wait_ge(u_done, l + 1)
                sp.dma_start(slot[2], i["w_out"][bass.ds(l, 1)]
                             .rearrange("a (c p) n -> (a p) c n", p=P)).then_inc(arrived[2], 16)

                def fill(s, name, e, before):
                    for h in range(2):
                        if before is None:
                            sp.wait_ge(used[s], l * ROUNDS + 4)
                        else:
                            sp.wait_ge(chunk_used, AHEAD + chunks(l, before, h * HALF + HALF - 1))
                        sp.dma_start(slot[s][:, h * HALF:(h + 1) * HALF, :],
                                     i[name][bass.ds(l, 1), bass.ds(e, 1)]
                                     .rearrange("a b (p c) n -> (a b p) c n", p=P)[:, h * HALF:(h + 1) * HALF, :])\
                            .then_inc(half_in[s][h], 16)

                fill(0, "exp_w1", 0, None)
                fill(1, "exp_w3", 0, None)
                fill(0, "exp_w1", 1, 0)
                fill(2, "exp_w2", 0, None)
                fill(1, "exp_w3", 1, w3_at(0))
                with sp.Fori(1, EXPERTS - 1) as e:
                    fill(0, "exp_w1", e + 1, w1_next_at(e) - 3)
                    fill(2, "exp_w2", e, w2_at(e) - 3)
                    fill(1, "exp_w3", e + 1, w3_at(e))
                fill(2, "exp_w2", EXPERTS - 1, w2_at(EXPERTS - 2))

        @block.gpsimd
        def _(pool):
            pool.sem_inc(rows_free, 2)
            pool.dma_start(cvec[:, 0, :], i["c"].rearrange("a (p k) -> (a p) k", k=KC)).then_inc(c_in, 16)
            pool.dma_start(cvec[:, 1, :], i["c_ctx"].rearrange("(p k) -> p k", k=KC)).then_inc(c_in, 16)
            pool.dma_start(cst[:, :], i["consts"]).then_inc(const_in, 16)
            pool.dma_start(sel[:, :], i["sel"]).then_inc(const_in, 16)
            pool.dma_start(x_res[0:LAT], i["x_sample"].rearrange("a t d -> (a t) d")).then_inc(x_copied, 16)
            pool.dma_start(x_res[LAT:TOK], i["x_prompt"].rearrange("a t d -> (a t) d")).then_inc(x_copied, 16)

            with pool.Fori(0, DEPTH) as l:
                def layer(name):
                    return i[name][bass.ds(l, 1)]

                def ada_bias(j):
                    src = layer("ada_b")[:, j * D:(j + 1) * D].broadcast_to([2, D])
                    pool.dma_start(adab[j % 2], src).then_inc(adab_in[j % 2], 16)

                ada_bias(0)
                ada_bias(1)
                pool.dma_start(prm[:, :], layer("params").rearrange("a p n -> (a p) n")).then_inc(prm_in, 16)
                pool.dma_start(fw1, layer("hy_f_w1").rearrange("a p n -> (a p) n")).then_inc(prm_in, 16)
                pool.dma_start(fw2, layer("hy_f_w2").rearrange("a p n -> (a p) n")).then_inc(prm_in, 16)
                pool.dma_start(fw3, layer("hy_f_w3").rearrange("a p n -> (a p) n")).then_inc(prm_in, 16)
                pool.dma_start(feats, i["feats"]).then_inc(fil_in, 16)
                pool.dma_start(win, i["window"].rearrange("(t p) n -> p t n", p=P)).then_inc(fil_in, 16)
                pool.dma_start(filc, i["fil_cos"].rearrange("(a p) k -> p a k", p=P)).then_inc(fil_in, 16)
                pool.dma_start(fils, i["fil_sin"].rearrange("(a p) k -> p a k", p=P)).then_inc(fil_in, 16)
                pool.dma_start(filcx, i["filx_cos"]).then_inc(fil_in, 16)
                pool.dma_start(filsx, i["filx_sin"]).then_inc(fil_in, 16)
                pool.dma_start(dbias, layer("hy_bias")).then_inc(prm_in, 16)
                pool.dma_start(wsT[:, :, :], layer("ws_t").rearrange("a p (h n) -> (a p) h n", h=GH)).then_inc(prm_in, 16)
                pool.dma_start(rw[:, :, :], layer("router_w").rearrange("a (p c) n -> (a p) c n", p=P)).then_inc(prm_in, 16)
                pool.dma_start(ck[:, :], i["cache_k"][0, bass.ds(l, 1)].rearrange("a p h d -> (a p) (h d)")).then_inc(prm_in, 16)
                pool.dma_start(cv[:, :], i["cache_v"][0, bass.ds(l, 1)].rearrange("a p h d -> (a p) (h d)")).then_inc(prm_in, 16)
                for j in range(2, ADA):
                    hold(pool, mrow_done, l * ADA + j - 1, const_in)
                    ada_bias(j)
                hold(pool, spec_mm, l * 5 + 5, const_in)
                pool.wait_ge(x_copied, 32)
                pool.dma_start(zt[:, :, 0:D], x_res.rearrange("(t p) d -> p t d", p=P)).then_inc(x_in, 16)
                s, per, n = taken(proj_at("kv", NT - 1))
                hold(pool, s, l * per + n, const_in)
                for name, a in (("new_k", 512), ("new_v", 640)):
                    pool.dma_start(o[name][0, bass.ds(l, 1)].rearrange("a p h d -> (a p) (h d)"),
                                   zt[:, NT - 1, a:a + KVW]).then_inc(kv_out, 16)
                for t in range(NT):
                    hold(pool, mx_mm, l * NT + t + 1, const_in)
                    if t == NT - 1:
                        hold(pool, kv_out, l * 32 + 32, const_in)
                    pool.dma_start(zt[:, t, 0:D], x_res[t * P:(t + 1) * P]).then_inc(xr_in[t], 16)
                for t in range(NT):
                    hold(pool, x1_done, l * NT + t + 1, const_in)
                    pool.dma_start(x_res[t * P:(t + 1) * P], zt[:, t, 0:D]).then_inc(x1_out, 16)
                    hold(pool, xn2, l * NT + t + 1, const_in)
                    pool.dma_start(xn_dram[t * P:(t + 1) * P], xn[:, t, :]).then_inc(xn_out, 16)
                hold(pool, x1_out, l * 80 + 80, const_in)
                hold(pool, xn_out, l * 80 + 80, const_in)

                def gather(u):
                    pool.indirect_dma_start(xe[u], None, xn_dram,
                                            bass.IndirectOffsetOnAxis(ap=icur[u][:, :], axis=0))\
                        .then_inc(xe_in[u], 16)

                def scatter(u, e):
                    hold(pool, ye_done, e + 1, const_in)
                    pool.indirect_dma_start(x_res, bass.IndirectOffsetOnAxis(ap=iscat[u][:, :], axis=0),
                                            ye[u], None, compute_op=ALU.add).then_inc(scattered, 16)
                    pool.wait_ge(scattered, e * 16 + 16)
                    pool.sem_inc(rows_free, 1)

                hold(pool, icur_done, l * (EXPERTS + 1) + 2, const_in)
                gather(0)
                gather(1)
                with pool.Fori(0, PAIRS - 1) as k:
                    for u in range(2):
                        e = k * 2 + u
                        hold(pool, icur_done, l * (EXPERTS + 1) + e + 3, const_in)
                        hold(pool, xeT_mm, l * EXPERTS + e + 1, const_in)
                        gather(u)
                        scatter(u, l * EXPERTS + e)
                scatter(0, l * EXPERTS + EXPERTS - 2)
                scatter(1, l * EXPERTS + EXPERTS - 1)

            pool.dma_start(zt[:, :, 0:D], x_res.rearrange("(t p) d -> p t d", p=P)).then_inc(fin_in, 16)
            pool.dma_start(final_g, i["final_g"].rearrange("(a d) -> a d", a=1).broadcast_to([P, D])).then_inc(fin_in, 16)
            pool.wait_ge(y_out_done, 1)
            pool.dma_start(o["y_sample"].rearrange("a (t p) d -> p (a t) d", p=P), zt[:, 0:4, 0:D]).then_inc(y_out, 16)
            pool.dma_start(o["y_prompt"].rearrange("a p d -> (a p) d"), zt[:, 4, 0:D]).then_inc(y_out, 16)
            pool.wait_ge(y_out, 32)
            pool.wait_ge(kv_out, 32 * DEPTH)

        @block.tensor
        def _(pe):
            for s in range(SLOTS):
                pe.sem_inc(used[s], 1)
            pe.sem_inc(chunk_used, AHEAD)
            pe.wait_ge(const_in, 32)
            pe.wait_ge(cs_done, 1)

            with pe.Fori(0, DEPTH) as l:
                def ada(j):
                    if j >= 2:
                        pe.wait_ge(mrow_done, l * ADA + j - 1)
                    pe.wait_ge(arrived[j % SLOTS], (l * ROUNDS + j // SLOTS + 1) * 16)
                    for n in range(2):
                        for c in range(KC):
                            mm = pe.matmul(bank[2 * (j % 2) + n][0:2, :], cs[:, c, :],
                                           slot[j % SLOTS][:, c, n * 512:(n + 1) * 512],
                                           start=(c == 0), stop=(c == KC - 1))
                    mm.then_inc(used[j % SLOTS], 1)

                def mod_step(q):
                    j, what = MOD[q]
                    if q:
                        pe.wait_ge(mod_out, l * len(MOD) + q)
                    hold(pe, mrow_done, l * ADA + j + 1, const_in)
                    if what == "col":
                        for k in range(KC):
                            mm = pe.transpose(bank[4][:, 2 * k:2 * k + 2], mrow[j % 2][:, k:D:KC], ident[0:2, 0:2])
                    else:
                        a, m = {"lat": (0, P), "ctx": (P, P), "cap": (2 * P, CAP)}[what]
                        for n in range(2):
                            mm = pe.matmul(bank[4 + n][0:m, :], sel[:, a:a + m],
                                           mrow[j % 2][:, n * 512:(n + 1) * 512], start=True, stop=True)
                    mm.then_inc(mod_mm, 1)

                def filter_layer(n):
                    if n == 0:
                        pe.wait_ge(prm_in, l * 144 + 144)
                        hold(pe, fil_in, l * 96 + 96, const_in)
                    else:
                        hold(pe, f_sin, l * 2 + 1, const_in)
                    w, x = (fw1, feats) if n == 0 else (fw2, hid)
                    pe.matmul(bank[6][0:FH, :], w, x[:, 0:LAT], start=True, stop=True)
                    pe.matmul(bank[7][0:FH, 0:CTX], w, x[:, LAT:TOK], start=True, stop=True).then_inc(f_mm, 1)

                def filter_taps():
                    pe.wait_ge(f_sin, l * 2 + 2)
                    for t in range(NT):
                        if t >= 2:
                            pe.wait_ge(f3_out, l * NT + t - 1)
                        pe.matmul(bank[6 + t % 2][:, :], hid[:, t * P:(t + 1) * P], fw3, start=True, stop=True)\
                            .then_inc(f3_mm, 1)

                def filter_spectrum():
                    pe.wait_ge(f3_out, l * NT + NT)
                    for n in range(4):
                        if n >= 2:
                            pe.wait_ge(spec_out, l * 5 + n - 1)
                        table, taps = (filc, fsum) if n < 2 else (fils, fdif)
                        for j in range(2):
                            jj = 2 * (n % 2) + j
                            for a in range(4):
                                mm = pe.matmul(bank[6 + n % 2][:, j * HY:(j + 1) * HY],
                                               table[:, a, jj * P:(jj + 1) * P], taps[:, a, :],
                                               start=(a == 0), stop=(a == 3))
                        mm.then_inc(spec_mm, 1)
                    pe.wait_ge(spec_out, l * 5 + 3)
                    pe.matmul(bank[6][:, 0:HY], filcx, fsum[:, 4, :], start=True, stop=True)
                    pe.matmul(bank[6][:, HY:2 * HY], filsx, fdif[:, 4, :], start=True, stop=True).then_inc(spec_mm, 1)

                ada(0)
                filter_layer(0)
                ada(1)
                mod_step(0)
                filter_layer(1)
                ada(2)
                mod_step(1)
                filter_taps()
                ada(3)
                mod_step(2)
                mod_step(3)
                filter_spectrum()
                ada(4)
                mod_step(4)
                ada(5)
                mod_step(5)
                mod_step(6)

                pe.wait_ge(mod_out, l * len(MOD) + len(MOD))
                pe.wait_ge(spec_out, l * 5 + 5)
                pe.wait_ge(mrow_done, l * ADA + ADA)
                for t in range(NT):
                    pe.wait_ge(xn1, l * NT + t + 1)
                    if t == 4:
                        pe.wait_ge(h1_v, l * NT + 1)
                        pe.wait_ge(h1_a, l * NT + 1)
                    for k in range(KC):
                        mm = pe.transpose(bank[2 * (t % 4) + k // 4][:, (k % 4) * P:(k % 4 + 1) * P],
                                          zt[:, t, k:D:KC], ident)
                    mm.then_inc(t1_mm, 1)

                pe.wait_ge(h1_v, l * NT + NT)
                pe.wait_ge(h1_a, l * NT + NT)
                pe.wait_ge(arrived[0], (l * ROUNDS + 3) * 16)
                for n, (kind, t, _) in enumerate(proj):
                    if n == LAST_SLOT0 + 1:
                        pe.wait_ge(arrived[1], (l * ROUNDS + 3) * 16)
                    if n >= 8:
                        s, per, v = taken(n - 8)
                        pe.wait_ge(s, l * per + v)
                    out = bank[n % 8]
                    if kind in ("q", "kv", "zg"):
                        a, m = {"q": (0, 512), "kv": (512, 256), "zg": (512, 512)}[kind]
                        w = slot[1] if kind == "zg" else slot[0]
                        for c in range(KC):
                            wc = w[:, c, a:a + m]
                            if kind == "q":
                                wc = wc.rearrange("p (g i d) -> p i g d", g=KV, i=4)
                            mm = pe.matmul(out[:, 0:m], hT[:, c, t * P:(t + 1) * P], wc,
                                           start=(c == 0), stop=(c == KC - 1))
                    else:
                        ms = [t] if kind == "zh" else list(range(t, 2 if t == 0 else 6))
                        a, b = (0, LAT) if kind == "zh" else (LAT, TOK)
                        for x, m in enumerate(ms):
                            w = slot[0][:, :, 768 + m * P:896 + m * P] if m < 2 else \
                                slot[1][:, :, (m - 2) * P:(m - 1) * P]
                            for c in range(KC):
                                mm = pe.matmul(out[:, x * (b - a):(x + 1) * (b - a)], w[:, c, :], hT[:, c, a:b],
                                               start=(c == 0), stop=(c == KC - 1))
                    mm.then_inc(multiplied(n)[0], 1)

                for e in "av":
                    s, per, v = taken(max(n for n in range(NP_) if proj[n][2] == e))
                    pe.wait_ge(s, l * per + v)
                pe.wait_ge(prm_in, l * 144 + 144)
                for t in range(NT):
                    for h in range(GH):
                        mm = pe.matmul(bank[t // 2][:, (t % 2) * GM + h * 64:(t % 2) * GM + h * 64 + 64],
                                       wsT[:, h, :], zt[:, t, 1024 + h * 64:1088 + h * 64], start=True, stop=True)
                    if t % 2 or t == NT - 1:
                        mm.then_inc(gm_mm, 1)

                pe.wait_ge(u_done, l + 1)
                for t in range(NT):
                    for m in range(2):
                        mm = pe.transpose(bank[3 + t // 2][:, (t % 2) * HY + m * P:(t % 2) * HY + (m + 1) * P],
                                          uT[:, m, t * P:(t + 1) * P], ident)
                    if t % 2 or t == NT - 1:
                        mm.then_inc(ut_mm, 1)
                pe.wait_ge(dft_in, l * 64 + 64)
                pe.wait_ge(ut_out, l * 3 + 3)
                for n in range(4):
                    if n == 2:
                        pe.wait_ge(gm_out, l * 3 + 3)
                    table = dftc if n < 2 else dfts
                    for j in range(2):
                        jj = 2 * (n % 2) + j
                        for a in range(4):
                            pe.matmul(bank[FWD[n]][:, j * HY:(j + 1) * HY], table[:, a, jj * P:(jj + 1) * P],
                                      utok[:, a, :], start=(a == 0), stop=(a == 3))
                pe.matmul(bank[FWD[4]][:, 0:HY], dftcx, utok[:, 4, :], start=True, stop=True)
                pe.matmul(bank[FWD[4]][:, HY:2 * HY], dftsx, utok[:, 4, :], start=True, stop=True).then_inc(fwd_mm, 1)
                pe.wait_ge(y_done, l + 1)
                for m in range(2):
                    for n in range(8):
                        pe.matmul(bank[3 + m][:, :], prod[0 if n < 4 else 2][:, n % 4, m * P:(m + 1) * P],
                                  (dftc if n < 4 else dfts)[:, n % 4, :], start=(n == 0), stop=(n == 7))
                for m in range(2):
                    for n in range(2):
                        mm = pe.matmul(bank[5][:, m * P:(m + 1) * P], prod[2 * n][:, 4, m * P:(m + 1) * P],
                                       dftsx if n else dftcx, start=(n == 0), stop=(n == 1))
                mm.then_inc(inv_mm, 1)
                pe.wait_ge(ysq_done, l + 1)
                for m in range(2):
                    pe.matmul(bank[6][:, :], ones, ysq[:, m, 0:LAT], start=(m == 0), stop=(m == 1))
                for m in range(2):
                    mm = pe.matmul(bank[7][:, 0:CTX], ones, ysq[:, m, LAT:TOK], start=(m == 0), stop=(m == 1))
                mm.then_inc(yss_mm, 1)

                pe.wait_ge(hy_done, l + 1)
                for t in range(NT):
                    if t < 4:
                        pe.wait_ge(rope_done, l * 4 + t + 1)
                    if t >= 2:
                        pe.wait_ge(qk_a, l * 7 + t - 1)
                    for n in range(4):
                        mm = pe.transpose(bank[t % 2][:, n * P:(n + 1) * P], zt[:, t, n * P:(n + 1) * P], ident)
                    mm.then_inc(qk_mm, 1)
                for t in range(4):
                    mm = pe.transpose(bank[2][:, t * P:(t + 1) * P], zt[:, t, 512:640], ident)
                mm.then_inc(qk_mm, 1)
                pe.transpose(bank[3][:, 0:P], zt[:, 4, 512:640], ident)
                pe.transpose(bank[3][:, P:2 * P], ck[:, :], ident).then_inc(qk_mm, 1)

                pe.wait_ge(qk_a, l * 7 + 7)
                for n in range(len(att) + 3):
                    if n < len(att):
                        b, h = att[n]
                        if n >= 2:
                            pe.wait_ge(sc_out, l * len(att) + n - 1)
                        g = slice(h // 4 * HD, h // 4 * HD + HD)
                        at = 0
                        for col, w in keys(b)[0]:
                            mm = pe.matmul(bank[4 + n % 2][:, at:at + w], qT[g, h % 4, b * P:(b + 1) * P],
                                           kT[g, col:col + w], start=True, stop=True)
                            at += w
                        mm.then_inc(sc_mm, 1)
                    m = n - 2
                    if 0 <= m < len(att):
                        pe.wait_ge(p_done, l * len(att) + m + 1)
                        if m >= 2:
                            pe.wait_ge(pt_v if m % 2 else pt_a, l * 20 + m // 2)
                        for x in range(width(att[m][0]) // P):
                            mm = pe.transpose(bank[6 + m % 2][:, x * P:(x + 1) * P],
                                              prob[m % 2][:, x * P:(x + 1) * P], ident)
                        mm.then_inc(pt_mm, 1)
                    m = n - 3
                    if 0 <= m < len(att):
                        b, h = att[m]
                        pe.wait_ge(pt_v if m % 2 else pt_a, l * 20 + m // 2 + 1)
                        if b == 4 and h == 0:
                            pe.wait_ge(a_done, l * NT + 1)
                        vs = values(b)
                        for x, v in enumerate(vs):
                            mm = pe.matmul(bank[b % 4][:, h * HD:(h + 1) * HD], probT[m % 2][:, x * P:(x + 1) * P],
                                           v[:, h // 4 * HD:h // 4 * HD + HD],
                                           start=(x == 0), stop=(x == len(vs) - 1))
                        mm.then_inc(pv_mm, 1)

                for t in range(NT):
                    pe.wait_ge(mixn, l * NT + t + 1)
                    if t >= 2:
                        pe.wait_ge(mx_out, l * NT + t - 1)
                    for n in range(6):
                        a = n * P if n < 4 else 768 + (n - 4) * P
                        mm = pe.transpose(bank[4 + 2 * (t % 2) + n // 4][:, (n % 4) * P:(n % 4 + 1) * P],
                                          zt[:, t, a:a + P], ident)
                    mm.then_inc(mx_mm, 1)
                pe.wait_ge(mx_out, l * NT + NT)

                pe.wait_ge(arrived[2], (l * ROUNDS + 3) * 16)
                for n in range(NT + 3):
                    if n < NT:
                        if n >= 2:
                            pe.wait_ge(x1_done, l * NT + n - 1)
                        for x in range(2):
                            for c in range(KC):
                                mm = pe.matmul(bank[2 * (n % 2) + x][:, :], hT[:, c, n * P:(n + 1) * P],
                                               slot[2][:, c, x * 512:(x + 1) * 512],
                                               start=(c == 0), stop=(c == KC - 1))
                        mm.then_inc(wo_mm if n < NT - 1 else used[2], 1)
                    t = n - 1
                    if 0 <= t < NT:
                        pe.wait_ge(xn2, l * NT + t + 1)
                        if t:
                            pe.wait_ge(h2_v, l * NT + t)
                            pe.wait_ge(h2_a, l * NT + t)
                        for k in range(KC):
                            mm = pe.transpose(bank[4 + k // 4][:, (k % 4) * P:(k % 4 + 1) * P], xn[:, t, k:D:KC], ident)
                        mm.then_inc(t2_mm, 1)
                    t = n - 2
                    if 0 <= t < NT:
                        pe.wait_ge(h2_v, l * NT + t + 1)
                        pe.wait_ge(h2_a, l * NT + t + 1)
                        if t:
                            pe.wait_ge(aff_done, l * NT + t)
                        for c in range(KC):
                            mm = pe.matmul(bank[6][:, t * EXPERTS:(t + 1) * EXPERTS], hT[:, c, t * P:(t + 1) * P],
                                           rw[:, c, :], start=(c == 0), stop=(c == KC - 1))
                        mm.then_inc(lg_mm, 1)
                    t = n - 3
                    if 0 <= t < NT:
                        affinity_T(pe, l, t)
                hold(pe, top_done, l + 1, const_in)
                pe.transpose(bank[6][0:CAP, 0:EXPERTS], topf[:, :], ident[0:EXPERTS, 0:EXPERTS])
                pe.transpose(bank[6][0:CAP, EXPERTS:2 * EXPERTS], topv[:, :], ident[0:EXPERTS, 0:EXPERTS])\
                    .then_inc(top_mm, 1)

                def product(m, s, out, x, between=(None, None)):
                    for c in range(KC):
                        pe.wait_ge(low_ready, chunks(l, m, c))
                        parts = ((x[0], high[c]), (x[0], slot_r[s][:, c, :]), (x[1], high[c]))
                        for part, (xs, w) in enumerate(parts):
                            for n in range(2):
                                mm = pe.matmul(bank[out + n][0:CAP, :], xs[:, c, :], w[:, n * 512:(n + 1) * 512],
                                               start=(c == 0 and part == 0), stop=(c == KC - 1 and part == 2))
                        mm.then_inc(chunk_used, 1)
                        if c == between[0]:
                            between[1]()

                def rows_T(u, k):
                    pe.wait_ge(xe_in[u], (l * PAIRS + k) * 16 + 16)
                    for c in range(KC):
                        mm = pe.transpose(bank[6 + c // 4][:, (c % 4) * CAP:(c % 4 + 1) * CAP], xe[u][:, c:D:KC],
                                          ident[0:CAP, 0:CAP])
                    mm.then_inc(xeT_mm, 1)

                def hidden_T(e):
                    pe.wait_ge(he_done, l * EXPERTS + e + 1)
                    for c in range(KC):
                        mm = pe.transpose(bank[6 + c // 4][:, (c % 4) * CAP:(c % 4 + 1) * CAP], he[:, c:D:KC],
                                          ident[0:CAP, 0:CAP])
                    mm.then_inc(heT_mm, 1)

                def expert(e, u, k, last=False):
                    product(w3_at(e), 1, 2, xeT[u], (None, None) if last else (1, lambda: rows_T(1 - u, k + u)))
                    if last:
                        hidden_T(e)
                    else:
                        pe.wait_ge(xeT_out, l * EXPERTS + e + 2)
                        product(w1_next_at(e), 0, 0, xeT[1 - u], (3, lambda: hidden_T(e)))
                    pe.wait_ge(heT_out, l * EXPERTS + e + 1)
                    product(w2_at(e), 2, 4, heT)

                pe.wait_ge(top_out, l + 1)
                rows_T(0, 0)
                pe.wait_ge(xeT_out, l * EXPERTS + 1)
                product(0, 0, 0, xeT[0])
                with pe.Fori(0, PAIRS - 1) as k:
                    for u in range(2):
                        expert(k * 2 + u, u, k)
                expert(EXPERTS - 2, 0, PAIRS - 1)
                expert(EXPERTS - 1, 1, PAIRS - 1, last=True)
                pe.wait_ge(ye_done, l * EXPERTS + EXPERTS)

        @block.scalar
        def _(act):
            act.wait_ge(c_in, 32)
            act.activation(cs[:, :, :].rearrange("p k s -> p s k"), cvec[:, :, :], ACT.Silu).then_inc(cs_done, 1)

            with act.Fori(0, DEPTH) as l:
                link = Chain(act, a_link, "A_LAYER", l * A_LAYER, A_LAYER)
                for n in range(2):
                    act.wait_ge(f_pre, l * 2 + n + 1)
                    act.activation(hid, pre, ACT.Sin).then_inc(f_sin, 1)
                for n in range(5):
                    act.wait_ge(spec_mm, l * 5 + n + 1)
                    if n < 4:
                        dst, src = spectrum[:, n // 2, 2 * (n % 2):2 * (n % 2) + 2, :], bank[6 + n % 2][:, :]
                    else:
                        dst, src = spectrum[:, :, 4, :], bank[6][:, :]
                    act.activation(dst, src.rearrange("p (j n) -> p j n", j=2), ACT.Copy,
                                   scale=1.0 / (LAT if n < 4 else CTX)).then_inc(spec_out, 1)

                act.wait_ge(x_in, l * 16 + 16)
                act.wait_ge(mod_mm, l * len(MOD) + len(MOD))
                for t in range(NT):
                    ins = act.activation(junk, zt[:, t, 0:D], ACT.Square, accum_out=ssum[:, t:t + 1])
                    link(ins) if t < NT - 1 else ins.then_inc(sq1, 1)
                act.wait_ge(rec1, l + 1)
                act.activation(sroot[:, 0:NT], srec[:, 0:NT], ACT.Sqrt).then_inc(root1, 1)
                act.wait_ge(mod_out, l * len(MOD) + len(MOD))

                def modulated(t, src, s0, done):
                    s = t // 4
                    for k in range(4, KC):
                        ins = act.activation(hT[:, k, t * P:(t + 1) * P], src[:, (k - 4) * P:(k - 3) * P], ACT.Identity,
                                             bias=mod[:, s0, k, s:s + 1], scale=mod[:, s0 + 1, k, s:s + 1])
                    ins.then_inc(done, 1)

                for t in range(NT):
                    act.wait_ge(t1_mm, l * NT + t + 1)
                    modulated(t, bank[2 * (t % 4) + 1], 0, h1_a)

                for n, (kind, t, e) in enumerate(proj):
                    if e == "a":
                        s, per, at = multiplied(n)
                        act.wait_ge(s, l * per + at)
                        if kind == "kv":
                            act.activation(zt[:, t, 512:768], bank[n % 8][:, 0:256], ACT.Copy).then_inc(z_a, 1)
                        else:
                            act.activation(zt[:, t, 768:1280], bank[n % 8][:, :], ACT.Gelu_apprx_tanh).then_inc(z_a, 1)

                for g in range(3):
                    act.wait_ge(ut_mm, l * 3 + g + 1)
                    w = 2 if g < 2 else 1
                    act.activation(utok[:, 2 * g:2 * g + w, :], bank[3 + g][:, 0:w * HY].rearrange("p (t n) -> p t n", t=w),
                                   ACT.Copy).then_inc(ut_out, 1)
                act.wait_ge(gm_out, l * 3 + 3)
                for t in range(NT):
                    ins = act.activation(jk[:, 0:GM], zt[:, t, 768:1024], ACT.Square, accum_out=ssum[:, 5 + t:6 + t])
                    link(ins) if t < NT - 1 else ins.then_inc(gm_sq, 1)
                act.wait_ge(yh_done, l + 1)
                act.activation(ysq, yh, ACT.Square).then_inc(ysq_done, 1)
                act.wait_ge(hrec, l + 1)
                act.activation(hy_y, hrc, ACT.Sqrt).then_inc(hroot, 1)

                for n in range(7):
                    act.wait_ge(qk_mm, l * 7 + n + 1)
                    if n < 5:
                        dst, src = qT[:, :, n * P:(n + 1) * P], bank[n % 2][:, :].rearrange("p (i t) -> p i t", i=4)
                    else:
                        dst, src = (kT[:, 0:512], bank[2][:, :]) if n == 5 else (kT[:, 512:768], bank[3][:, 0:256])
                    act.activation(dst, src, ACT.Copy).then_inc(qk_a, 1)

                for n in range(len(att) + 8):
                    if n < len(att):
                        b, h = att[n]
                        act.wait_ge(sc_out, l * len(att) + n + 1)
                        if n >= 2:
                            act.wait_ge(pt_mm, l * len(att) + n - 1)
                        w = width(b)
                        act.activation(prob[n % 2][:, 0:w], sbuf_s[n % 2][:, 0:w], ACT.Exp,
                                       bias=negmax[:, b, h:h + 1], scale=-1.0,
                                       accum_out=rsum[:, b, h:h + 1]).then_inc(p_done, 1)
                    m = n - 2
                    if 0 <= m < len(att) and m % 2 == 0:
                        act.wait_ge(pt_mm, l * len(att) + m + 1)
                        if m >= 2:
                            act.wait_ge(pv_mm, l * len(att) + m - 1)
                        w = width(att[m][0])
                        act.activation(probT[0][:, 0:w], bank[6][:, 0:w], ACT.Copy).then_inc(pt_a, 1)
                    if n >= 8 and n % 8 == 0:
                        b = n // 8 - 1
                        act.wait_ge(es_in, l * NT + b + 1)
                        act.activation(esink[:, b, :], denom[:, b, :], ACT.Exp).then_inc(es_out, 1)
                    if n >= 14 and n % 8 == 6:
                        b = n // 8 - 1
                        act.wait_ge(a_done, l * NT + b + 1)
                        ins = act.activation(jk[:, :], zt[:, b, 0:ATT], ACT.Square, accum_out=ssum[:, b:b + 1])
                        ins.then_inc(a_sq, 1)
                act.wait_ge(mrec, l + 1)
                act.activation(sroot[:, :], srec[:, :], ACT.Sqrt).then_inc(mroot, 1)

                for n in range(NT + 2):
                    if n < NT:
                        act.wait_ge(x1_done, l * NT + n + 1)
                        act.activation(junk, zt[:, n, 0:D], ACT.Square, accum_out=ssum[:, n:n + 1]).then_inc(sq2, 1)
                        act.wait_ge(rec2, l * NT + n + 1)
                        act.activation(sroot[:, n:n + 1], srec[:, n:n + 1], ACT.Sqrt).then_inc(root2, 1)
                    t = n - 1
                    if 0 <= t < NT:
                        act.wait_ge(t2_mm, l * NT + t + 1)
                        modulated(t, bank[5], 2, h2_a)
                    t = n - 2
                    if 0 <= t < NT:
                        act.wait_ge(anm_done, l * NT + t + 1)
                        act.activation(aff[:, t, :], bank[6][:, t * EXPERTS:(t + 1) * EXPERTS], ACT.Exp,
                                       bias=anm[:, t:t + 1], accum_out=asum[:, t:t + 1]).then_inc(aexp, 1)

                def rounded(m, s, e, after=(None, None)):
                    for c in range(KC):
                        if c % HALF == 0:
                            act.wait_ge(half_in[s][c // HALF], (l * EXPERTS + e) * 16 + 16)
                        act.wait_ge(chunk_used, AHEAD - KC + chunks(l, m, c))
                        act.activation(high[c], slot[s][:, c, :], ACT.Copy).then_inc(high_ready, 1)
                        if c == after[0]:
                            after[1]()

                def rows(x):
                    act.wait_ge(xt_done, l * EXPERTS + x + 1)
                    act.activation(xeT[x % 2 if isinstance(x, int) else 1 - u][0], xt, ACT.Copy).then_inc(xh_done, 1)

                def hidden(e):
                    act.wait_ge(heT_mm, l * EXPERTS + e + 1)
                    for n in range(2):
                        ins = act.activation(heT[0][:, 4 * n:4 * n + 4, :],
                                             bank[6 + n][:, 0:4 * CAP].rearrange("p (c t) -> p c t", c=4), ACT.Copy)
                    ins.then_inc(hh_done, 1)

                def gated(m, e):
                    act.wait_ge(chunk_used, AHEAD + chunks(l, m, KC - 1))
                    act.activation(he[:, 0:512], bank[0][0:CAP, :], ACT.Silu)
                    act.activation(he[:, 512:D], bank[1][0:CAP, :], ACT.Silu).then_inc(silu, 1)

                act.wait_ge(lg_mm, l * NT + NT)
                act.wait_ge(xn_out, l * 80 + 80)
                act.wait_ge(t2_mm, l * NT + NT)
                rounded(0, 0, 0)
                u = 1
                rows(0)
                rounded(w3_at(0), 1, 0)
                gated(0, 0)

                def prepare(e):
                    rounded(w1_next_at(e), 0, e + 1, (4, lambda: rows(e + 1)))
                    rounded(w2_at(e), 2, e, (5, lambda: hidden(e)))
                    gated(w1_next_at(e), e + 1)
                    rounded(w3_at(e + 1), 1, e + 1)

                with act.Fori(0, PAIRS - 1) as k:
                    for u in range(2):
                        prepare(k * 2 + u)
                u = 0
                prepare(EXPERTS - 2)
                rounded(w2_at(EXPERTS - 1), 2, EXPERTS - 1)
                hidden(EXPERTS - 1)
                link.close()

            act.wait_ge(fin_in, 32)
            for t in range(NT):
                act.activation(arena_u[:, t * D:(t + 1) * D], zt[:, t, 0:D], ACT.Square, accum_out=ssum[:, t:t + 1])\
                    .then_inc(fsq, 1)
            act.wait_ge(frec, 1)
            act.activation(sroot[:, 0:NT], srec[:, 0:NT], ACT.Sqrt).then_inc(froot, 1)

        @block.vector
        def _(v):
            def newton(link, root, ms, tmp):
                link(v.tensor_tensor(tmp, root, root, ALU.mult))
                link(v.tensor_tensor(tmp, tmp, ms, ALU.mult))
                link(v.tensor_scalar(tmp, tmp, -0.5, 1.5, ALU.mult, ALU.add))
                link(v.tensor_tensor(root, root, tmp, ALU.mult))

            v.wait_ge(const_in, 32)
            with v.Fori(0, DEPTH) as l:
                link = Chain(v, v_link, "V_LAYER", l * V_LAYER, V_LAYER)

                def row(j):
                    v.wait_ge(used[j % SLOTS], l * ROUNDS + j // SLOTS + 2)
                    v.wait_ge(adab_in[j % 2], l * 48 + 16 * (j // 2 + 1))
                    if j >= 2:
                        v.wait_ge(mod_mm, l * len(MOD) + spread[j - 2])
                    for n in range(2):
                        ins = v.tensor_tensor(mrow[j % 2][:, n * 512:(n + 1) * 512], bank[2 * (j % 2) + n][0:2, :],
                                              adab[j % 2][:, n * 512:(n + 1) * 512], ALU.add)
                    ins.then_inc(mrow_done, 1)

                def mod_taken(q):
                    j, what = MOD[q]
                    v.wait_ge(mod_mm, l * len(MOD) + q + 1)
                    cols = bank[4][:, 0:2 * KC].rearrange("p (k s) -> p k s", s=2)
                    if j in (0, 3):
                        v.tensor_copy(mod[:, 0 if j == 0 else 2, :, :], cols).then_inc(mod_out, 1)
                    elif what == "col":
                        g = prm[:, (G1 if j == 1 else G2):(G1 if j == 1 else G2) + KC]
                        v.scalar_tensor_tensor(out=mod[:, 1 if j == 1 else 3, :, :], in0=cols, scalar=1.0,
                                               in1=g.unsqueeze(2).broadcast_to([P, KC, 2]),
                                               op0=ALU.add, op1=ALU.mult).then_inc(mod_out, 1)
                    else:
                        dst, m = {"lat": (gate1[:, 0, :], P), "ctx": (gate1[:, 1, :], P), "cap": (gate2[:, :], CAP)}[what]
                        for n in range(2):
                            ins = v.tensor_copy(dst[:, n * 512:(n + 1) * 512], bank[4 + n][0:m, :])
                        ins.then_inc(mod_out, 1)

                def phase(n):
                    v.wait_ge(f_mm, l * 2 + n + 1)
                    b1, fq = prm[0:FH, FB1 + n:FB1 + n + 1], prm[0:FH, FQ:FQ + 1]
                    v.tensor_scalar(pre[:, 0:LAT], bank[6][0:FH, :], b1, fq, ALU.add, ALU.mult)
                    link(v.tensor_scalar(pre[:, LAT:TOK], bank[7][0:FH, 0:CTX], b1, fq, ALU.add, ALU.mult))
                    link(v.tensor_scalar(turns, pre, 1.0 / (TWO_PI_HI + TWO_PI_LO), ROUND, ALU.mult, ALU.add))
                    link(v.tensor_scalar(turns, turns, ROUND, None, ALU.subtract))
                    link(v.scalar_tensor_tensor(out=pre, in0=turns, scalar=-TWO_PI_HI, in1=pre, op0=ALU.mult, op1=ALU.add))
                    link(v.scalar_tensor_tensor(out=pre, in0=turns, scalar=-TWO_PI_LO, in1=pre, op0=ALU.mult, op1=ALU.add))
                    v.tensor_scalar(pre, pre, PI_IN, -PI_IN, ALU.min, ALU.max).then_inc(f_pre, 1)

                def taps(t):
                    v.wait_ge(f3_mm, l * NT + t + 1)
                    src = bank[6 + t % 2]
                    v.tensor_tensor(hfw, src[:, 0:HY], win[:, t, :], ALU.mult)
                    link(v.tensor_tensor(hbw, src[:, HY:2 * HY], win[:, t, :], ALU.mult))
                    if t in (0, 4):
                        v.tensor_tensor(hfw[0:1, :], hfw[0:1, :], dbias, ALU.add)
                        link(v.memset(hbw[0:1, :], 0.0))
                    v.tensor_tensor(fsum[:, t, :], hfw, hbw, ALU.add)
                    ins = v.tensor_tensor(fdif[:, t, :], hfw, hbw, ALU.subtract)
                    ins.then_inc(f3_out, 1)
                    v.wait_ge(f3_out, l * NT + t + 1)

                v.wait_ge(prm_in, l * 144 + 144)
                v.tensor_scalar(nsink[:, :], prm[:, SK:SK + HEADS], -1.0, None, ALU.mult)
                row(0)
                v.wait_ge(fil_in, l * 96 + 96)
                phase(0)
                row(1)
                mod_taken(0)
                phase(1)
                row(2)
                mod_taken(1)
                for t in range(NT):
                    taps(t)
                row(3)
                mod_taken(2)
                mod_taken(3)
                row(4)
                mod_taken(4)
                row(5)
                mod_taken(5)
                mod_taken(6)

                v.wait_ge(sq1, l + 1)
                link(v.tensor_scalar(sms[:, 0:NT], ssum[:, 0:NT], 1.0 / D, EPS, ALU.mult, ALU.add))
                v.reciprocal(srec[:, 0:NT], sms[:, 0:NT]).then_inc(rec1, 1)
                v.wait_ge(root1, l + 1)
                newton(link, sroot[:, 0:NT], sms[:, 0:NT], stmp[:, 0:NT])
                for t in range(NT):
                    v.tensor_scalar(zt[:, t, 0:D], zt[:, t, 0:D], sroot[:, t:t + 1], None, ALU.mult).then_inc(xn1, 1)

                def modulated(t, src, s0, done):
                    s = t // 4
                    for k in range(4):
                        ins = v.tensor_scalar(hT[:, k, t * P:(t + 1) * P], src[:, k * P:(k + 1) * P],
                                              mod[:, s0 + 1, k, s:s + 1], mod[:, s0, k, s:s + 1], ALU.mult, ALU.add)
                    ins.then_inc(done, 1)

                v.wait_ge(mod_out, l * len(MOD) + len(MOD))
                for t in range(NT):
                    v.wait_ge(t1_mm, l * NT + t + 1)
                    modulated(t, bank[2 * (t % 4)], 0, h1_v)

                for n, (kind, t, e) in enumerate(proj):
                    if e == "v":
                        s, per, at = multiplied(n)
                        v.wait_ge(s, l * per + at)
                        if kind == "q":
                            dst, src = zt[:, t, 0:512], bank[n % 8][:, :]
                        elif kind == "zh":
                            dst, src = zhT[:, t, 0:LAT], bank[n % 8][:, :]
                        else:
                            m = 2 if t == 0 else 4
                            dst = zhT[:, t:t + m, LAT:TOK]
                            src = bank[n % 8][:, 0:m * CTX].rearrange("p (m t) -> p m t", m=m)
                        v.tensor_copy(dst, src).then_inc(z_v, 1)
                v.wait_ge(z_v, l * Z_V + Z_V)

                for m in range(6):
                    dst = x0c[:, m, :] if m < 2 else uT[:, m - 2, :] if m < 4 else cvt
                    w = [prm[:, CW + 6 * j + m:CW + 6 * j + m + 1] for j in range(TAPS)]
                    link(v.tensor_scalar(dst, zhT[:, m, :], w[1], prm[:, CB + m:CB + m + 1], ALU.mult, ALU.add))
                    for j, (to, fr) in enumerate(((1, 0), (0, 1))):
                        for a, b in ((0, LAT), (LAT, TOK)):
                            ins = v.scalar_tensor_tensor(out=dst[:, a + to:b - fr], in0=zhT[:, m, a + fr:b - to],
                                                         scalar=w[2 * j], in1=dst[:, a + to:b - fr],
                                                         op0=ALU.mult, op1=ALU.add)
                        link(ins)
                    if m >= 4:
                        ins = v.tensor_tensor(uT[:, m - 4, :], uT[:, m - 4, :], cvt, ALU.mult)
                        link(ins) if m == 4 else ins.then_inc(u_done, 1)

                for t in range(4):
                    s, per, n = taken(proj_at("kv", t))
                    v.wait_ge(s, l * per + n)
                    x = zt[:, t, 0:640].rearrange("p (h a b n) -> p h a b n", h=10, a=2, b=2)
                    r = rtmp[:, :].rearrange("p (h a b n) -> p h a b n", h=10, a=2, b=2)
                    sn = sin_t[:, t].unsqueeze(1).broadcast_to([P, 10, 2, 16])
                    v.scalar_tensor_tensor(out=r[:, :, :, 0, :], in0=x[:, :, :, 1, :], scalar=-1.0, in1=sn,
                                           op0=ALU.mult, op1=ALU.mult)
                    link(v.tensor_tensor(r[:, :, :, 1, :], x[:, :, :, 0, :], sn, ALU.mult))
                    x3 = zt[:, t, 0:640].rearrange("p (h d) -> p h d", h=10)
                    link(v.tensor_tensor(x3, x3, cos_t[:, t].unsqueeze(1).broadcast_to([P, 10, 64]), ALU.mult))
                    v.tensor_tensor(zt[:, t, 0:640], zt[:, t, 0:640], rtmp[:, :], ALU.add).then_inc(rope_done, 1)
                    v.wait_ge(rope_done, l * 4 + t + 1)

                for g in range(3):
                    v.wait_ge(gm_mm, l * 3 + g + 1)
                    ts = [t for t in (2 * g, 2 * g + 1) if t < NT]
                    for x, t in enumerate(ts):
                        ins = v.tensor_tensor(zt[:, t, 1024:1280].rearrange("p (h c) -> p h c", h=GH),
                                              bank[g][:, x * GM:(x + 1) * GM].rearrange("p (h c) -> p h c", h=GH),
                                              prm[:, GB:GB + GH].unsqueeze(2).broadcast_to([P, GH, 64]), ALU.add)
                    link(ins)
                    for t in ts:
                        ins = v.tensor_tensor(zt[:, t, 768:1024], zt[:, t, 768:1024], zt[:, t, 1024:1280], ALU.mult)
                    ins.then_inc(gm_out, 1)

                v.wait_ge(fwd_mm, l + 1)
                v.wait_ge(spec_out, l * 5 + 5)
                for n, (x, f) in enumerate(((0, 0), (1, 1), (0, 1), (1, 0))):
                    for j in range(2):
                        v.tensor_tensor(prod[n][:, 2 * j:2 * j + 2, :],
                                        bank[FWD[2 * x + j]][:, :].rearrange("p (j n) -> p j n", j=2),
                                        spectrum[:, f, 2 * j:2 * j + 2, :], ALU.mult)
                    ins = v.tensor_tensor(prod[n][:, 4, :], bank[FWD[4]][:, x * HY:(x + 1) * HY],
                                          spectrum[:, f, 4, :], ALU.mult)
                link(ins)
                v.tensor_tensor(spec[1], spec[1], spec[2], ALU.subtract)
                v.tensor_tensor(spec[3], spec[3], spec[4], ALU.add).then_inc(y_done, 1)

                v.wait_ge(inv_mm, l + 1)
                for m in range(2):
                    v.tensor_tensor(yh[:, m, 0:LAT], bank[3 + m][:, :], x0c[:, m, 0:LAT], ALU.mult)
                v.tensor_tensor(yh[:, :, LAT:TOK], bank[5][:, 0:2 * CTX].rearrange("p (m t) -> p m t", m=2),
                                x0c[:, :, LAT:TOK], ALU.mult).then_inc(yh_done, 1)
                v.wait_ge(yss_mm, l + 1)
                v.tensor_scalar(hms[:, 0:LAT], bank[6][:, :], 1.0 / HY, EPS, ALU.mult, ALU.add)
                link(v.tensor_scalar(hms[:, LAT:TOK], bank[7][:, 0:CTX], 1.0 / HY, EPS, ALU.mult, ALU.add))
                v.reciprocal(hrc, hms).then_inc(hrec, 1)
                v.wait_ge(hroot, l + 1)
                newton(link, hy_y, hms, hya)
                for m in range(2):
                    ins = v.scalar_tensor_tensor(out=hT[:, 4 + m, :], in0=yh[:, m, :], scalar=prm[:, GO + 4 + m:GO + 5 + m],
                                                 in1=hy_y, op0=ALU.mult, op1=ALU.mult)
                ins.then_inc(hy_done, 1)

                for n in range(len(att) + 4):
                    if n < len(att):
                        b, h = att[n]
                        if n >= 2:
                            v.wait_ge(p_done, l * len(att) + n - 1)
                        hold(v, sc_mm, l * len(att) + n + 1, const_in)
                        w, m0 = width(b), keys(b)[1]
                        v.tensor_tensor_reduce(out=sbuf_s[n % 2][:, 0:w], in0=bank[4 + n % 2][:, 0:w],
                                               in1=mask[:, m0:m0 + w], scale=-SCALE, scalar=nsink[:, h:h + 1],
                                               op0=ALU.add, op1=ALU.min,
                                               accum_out=negmax[:, b, h:h + 1]).then_inc(sc_out, 1)
                    m = n - 2
                    if 0 <= m < len(att) and m % 2:
                        v.wait_ge(pt_mm, l * len(att) + m + 1)
                        if m >= 2:
                            v.wait_ge(pv_mm, l * len(att) + m - 1)
                        w = width(att[m][0])
                        v.tensor_copy(probT[1][:, 0:w], bank[7][:, 0:w]).then_inc(pt_v, 1)
                    if n >= 8 and n % 8 == 0:
                        b = n // 8 - 1
                        v.wait_ge(sc_out, l * len(att) + n)
                        v.tensor_tensor(denom[:, b, :], negmax[:, b, :], nsink[:, :], ALU.subtract).then_inc(es_in, 1)
                    if n >= 11 and n % 8 == 3:
                        b = n // 8 - 1
                        v.wait_ge(es_out, l * NT + b + 1)
                        v.wait_ge(pv_mm, l * len(att) + 8 * b + 8)
                        link(v.tensor_tensor(denom[:, b, :], rsum[:, b, :], esink[:, b, :], ALU.add))
                        link(v.reciprocal(denom[:, b, :], denom[:, b, :]))
                        v.tensor_tensor(zt[:, b, 0:ATT].rearrange("p (h d) -> p h d", h=HEADS),
                                        bank[b % 4][:, :].rearrange("p (h d) -> p h d", h=HEADS),
                                        denom[:, b, :].unsqueeze(2).broadcast_to([P, HEADS, HD]), ALU.mult)\
                            .then_inc(a_done, 1)

                v.wait_ge(a_sq, l * NT + NT)
                v.wait_ge(gm_sq, l + 1)
                v.tensor_scalar(sms[:, 0:5], ssum[:, 0:5], 1.0 / ATT, EPS, ALU.mult, ALU.add)
                link(v.tensor_scalar(sms[:, 5:10], ssum[:, 5:10], 1.0 / GM, EPS, ALU.mult, ALU.add))
                v.reciprocal(srec[:, :], sms[:, :]).then_inc(mrec, 1)
                v.wait_ge(mroot, l + 1)
                newton(link, sroot[:, :], sms[:, :], stmp[:, :])
                v.wait_ge(a_done, l * NT + NT)
                v.wait_ge(gm_out, l * 3 + 3)
                for t in range(NT):
                    v.tensor_scalar(zt[:, t, 0:ATT], zt[:, t, 0:ATT], sroot[:, t:t + 1], None, ALU.mult)
                    v.tensor_scalar(zt[:, t, 768:1024], zt[:, t, 768:1024], sroot[:, 5 + t:6 + t], None, ALU.mult)\
                        .then_inc(mixn, 1)
                for t in range(NT):
                    v.wait_ge(mx_mm, l * NT + t + 1)
                    for x, (c, w) in enumerate(((0, 4), (6, 2))):
                        ins = v.tensor_tensor(hT[:, c:c + w, t * P:(t + 1) * P],
                                              bank[4 + 2 * (t % 2) + x][:, 0:w * P].rearrange("p (c t) -> p c t", c=w),
                                              prm[:, GO + c:GO + c + w].unsqueeze(2).broadcast_to([P, w, P]), ALU.mult)
                    ins.then_inc(mx_out, 1)

                for n in range(NT + 3):
                    if n < NT:
                        if n < NT - 1:
                            v.wait_ge(wo_mm, l * (NT - 1) + n + 1)
                        else:
                            v.wait_ge(used[2], l * ROUNDS + 4)
                        halves = (rtmp[:, 0:512], jk[:, :])
                        for x in range(2):
                            ins = v.tensor_tensor(halves[x], bank[2 * (n % 2) + x][:, :],
                                                  gate1[:, n // 4, x * 512:(x + 1) * 512], ALU.mult)
                        link(ins)
                        v.wait_ge(xr_in[n], l * 16 + 16)
                        for x in range(2):
                            a = zt[:, n, x * 512:(x + 1) * 512]
                            ins = v.tensor_tensor(a, a, halves[x], ALU.add)
                        ins.then_inc(x1_done, 1)
                        v.wait_ge(sq2, l * NT + n + 1)
                        c = slice(n, n + 1)
                        link(v.tensor_scalar(sms[:, c], ssum[:, c], 1.0 / D, EPS, ALU.mult, ALU.add))
                        v.reciprocal(srec[:, c], sms[:, c]).then_inc(rec2, 1)
                        v.wait_ge(root2, l * NT + n + 1)
                        newton(link, sroot[:, c], sms[:, c], stmp[:, c])
                        v.wait_ge(x1_done, l * NT + n + 1)
                        v.tensor_scalar(xn[:, n, :], zt[:, n, 0:D], sroot[:, c], None, ALU.mult).then_inc(xn2, 1)
                    t = n - 1
                    if 0 <= t < NT:
                        v.wait_ge(t2_mm, l * NT + t + 1)
                        modulated(t, bank[4], 2, h2_v)
                    t = n - 2
                    if 0 <= t < NT:
                        v.wait_ge(lg_mm, l * NT + t + 1)
                        v.tensor_reduce(anm[:, t:t + 1], bank[6][:, t * EXPERTS:(t + 1) * EXPERTS], AX_X, ALU.max,
                                        negate=True).then_inc(anm_done, 1)
                        v.wait_ge(aexp, l * NT + t + 1)
                        link(v.reciprocal(arec[:, t:t + 1], asum[:, t:t + 1]))
                        v.tensor_scalar(aff[:, t, :], aff[:, t, :], arec[:, t:t + 1], None, ALU.mult).then_inc(aff_done, 1)
                    t = n - 3
                    if 0 <= t < NT:
                        v.wait_ge(affT_mm, l * NT + t + 1)
                        v.tensor_copy(affT[:, t * P:(t + 1) * P], bank[7][0:EXPERTS, 0:P]).then_inc(affT_out, 1)
                hold(v, affT_out, l * NT + NT, const_in)
                for a, b, c0, c1 in ((0, LAT, 0, CAP_L), (LAT, TOK, CAP_L, CAP)):
                    for c in range(c0, c1, 8):
                        link.held(v.max(topv[:, c:c + 8], affT[:, a:b]), const_in)
                        link.held(v.max_index(topi[:, c:c + 8], topv[:, c:c + 8], affT[:, a:b]), const_in)
                        if c + 8 < c1:
                            link.held(v.match_replace(affT[:, a:b], topv[:, c:c + 8], affT[:, a:b], -1.0), const_in)
                v.tensor_copy(topf[:, 0:CAP_L], topi[:, 0:CAP_L])
                v.tensor_scalar(topf[:, CAP_L:CAP], topi[:, CAP_L:CAP], float(LAT), None, ALU.add).then_inc(top_done, 1)
                v.wait_ge(top_mm, l + 1)
                link(v.tensor_copy(idxT[:, 0:EXPERTS], bank[6][0:CAP, 0:EXPERTS]))
                v.tensor_copy(idxT[:, EXPERTS:EXPERTS + 1], idxT[:, 0:1])
                v.tensor_copy(icur[0][:, :], idxT[:, 0:1]).then_inc(icur_done, 1)
                v.tensor_copy(icur[1][:, :], idxT[:, 1:2]).then_inc(icur_done, 1)
                v.tensor_copy(gateT[:, :], bank[6][0:CAP, EXPERTS:2 * EXPERTS]).then_inc(top_out, 1)
                for dst, n in ((g2e, 3), (s2e, 2)):
                    v.tensor_copy(dst[:, :, 0:CAP_L], mod[:, n, :, 0:1].broadcast_to([P, KC, CAP_L]))
                    ins = v.tensor_copy(dst[:, :, CAP_L:CAP], mod[:, n, :, 1:2].broadcast_to([P, KC, CAP_C]))
                link(ins)

                def rest(m, s, after={}):
                    for c in range(KC):
                        v.wait_ge(high_ready, chunks(l, m, c))
                        v.tensor_tensor(slot_r[s][:, c, :], slot[s][:, c, :], high[c], ALU.subtract).then_inc(low_ready, 1)
                        if c in after:
                            after[c]()

                def rows(x, u):
                    v.wait_ge(xeT_mm, l * EXPERTS + x + 1)
                    if not (isinstance(x, int) and x == EXPERTS - 1):
                        v.tensor_copy(icur[u][:, :], idxT[:, bass.ds(x + 2, 1)]).then_inc(icur_done, 1)
                    for n in range(2):
                        ins = v.tensor_tensor(xt[:, 4 * n:4 * n + 4, :],
                                              bank[6 + n][:, 0:4 * CAP].rearrange("p (c t) -> p c t", c=4),
                                              g2e[:, 4 * n:4 * n + 4, :], ALU.mult)
                    ins.then_inc(xt_scaled, 1)
                    v.wait_ge(xt_scaled, l * EXPERTS + x + 1)
                    v.tensor_tensor(xt, xt, s2e, ALU.add).then_inc(xt_done, 1)

                def rows_rest(x, u):
                    v.wait_ge(xh_done, l * EXPERTS + x + 1)
                    v.tensor_tensor(xeT[u][1], xt, xeT[u][0], ALU.subtract).then_inc(xeT_out, 1)

                def hidden(e):
                    v.wait_ge(chunk_used, AHEAD + chunks(l, w3_at(e), KC - 1))
                    v.wait_ge(silu, l * EXPERTS + e + 1)
                    for n in range(2):
                        a = he[:, n * 512:(n + 1) * 512]
                        ins = v.tensor_tensor(a, a, bank[2 + n][0:CAP, :], ALU.mult)
                    ins.then_inc(he_done, 1)

                def hidden_rest(e):
                    v.wait_ge(hh_done, l * EXPERTS + e + 1)
                    for n in range(2):
                        c = slice(4 * n, 4 * n + 4)
                        ins = v.tensor_tensor(heT[1][:, c, :], bank[6 + n][:, 0:4 * CAP].rearrange("p (c t) -> p c t", c=4),
                                              heT[0][:, c, :], ALU.subtract)
                    ins.then_inc(heT_out, 1)

                def result(e, u):
                    v.wait_ge(rows_free, l * EXPERTS + e + 1)
                    v.tensor_copy(iscat[u][:, :], idxT[:, bass.ds(e, 1)])
                    v.wait_ge(chunk_used, AHEAD + chunks(l, w2_at(e), KC - 1))
                    for n in range(2):
                        ins = v.scalar_tensor_tensor(out=ye[u][:, n * 512:(n + 1) * 512], in0=bank[4 + n][0:CAP, :],
                                                     scalar=gateT[:, bass.ds(e, 1)],
                                                     in1=gate2[:, n * 512:(n + 1) * 512],
                                                     op0=ALU.mult, op1=ALU.mult)
                    ins.then_inc(ye_done, 1)

                def expert(e, u):
                    rest(w1_next_at(e), 0, {2: lambda: rows(e + 1, 1 - u), 4: lambda: rows_rest(e + 1, 1 - u)})
                    hidden(e)
                    rest(w2_at(e), 2, {6: lambda: hidden_rest(e)})
                    rest(w3_at(e + 1), 1)
                    result(e, u)

                rest(0, 0)
                rows(0, 0)
                rows_rest(0, 0)
                rest(w3_at(0), 1)
                with v.Fori(0, PAIRS - 1) as k:
                    for u in range(2):
                        expert(k * 2 + u, u)
                expert(EXPERTS - 2, 0)
                hidden(EXPERTS - 1)
                rest(w2_at(EXPERTS - 1), 2)
                hidden_rest(EXPERTS - 1)
                result(EXPERTS - 1, 1)
                link.close()

            flink = Chain(v, v_flink, "V_LAST", 0, V_LAST)
            v.wait_ge(fsq, NT)
            flink(v.tensor_scalar(sms[:, 0:NT], ssum[:, 0:NT], 1.0 / D, EPS, ALU.mult, ALU.add))
            v.reciprocal(srec[:, 0:NT], sms[:, 0:NT]).then_inc(frec, 1)
            v.wait_ge(froot, 1)
            newton(flink, sroot[:, 0:NT], sms[:, 0:NT], stmp[:, 0:NT])
            for t in range(NT):
                ins = v.scalar_tensor_tensor(out=zt[:, t, 0:D], in0=zt[:, t, 0:D], scalar=sroot[:, t:t + 1],
                                             in1=final_g, op0=ALU.mult, op1=ALU.mult)
            ins.then_inc(y_out_done, 1)
            flink.close()


def tables():
    import numpy as np

    c = {}
    for name, n in (("", LAT), ("x", CTX)):
        k = np.arange(n, dtype=np.float64)
        half = np.pi / n * np.outer(k + 0.5, k + 0.5)
        whole = np.pi / n * np.outer(k, k + 0.5)
        c[f"dft{name}_cos"], c[f"dft{name}_sin"] = np.cos(half), np.sin(half)
        c[f"fil{name}_cos"], c[f"fil{name}_sin"] = np.cos(whole), np.sin(whole)
    feats, window = [], []
    lo, hi = np.log(1e-2) / 1.5, np.log(1e-2) / 0.3
    deltas = np.abs(np.linspace(lo, hi, HY))
    for n in (LAT, CTX):
        t = np.linspace(0.0, 1.0, n)[:, None]
        bands = (EMB - 1) // 2
        fb = np.linspace(1e-4, bands - 1, bands)[None, :]
        w = 2.0 * np.pi * np.arange(n)[:, None] / n
        feats.append(np.concatenate([t, np.cos(fb * w), -np.sin(fb * w)], axis=-1).T)
        window.append(np.exp(-t * deltas[None, :]))
    c["feats"] = np.concatenate(feats, axis=1)
    c["window"] = np.concatenate(window, axis=0)
    m = np.zeros((P, NCST))
    m[:, C_ID:C_ID + P] = np.eye(P)
    q, j = np.arange(P)[:, None], np.arange(P)[None, :]
    m[:, C_MASK:C_MASK + P] = np.where(j >= q, 0.0, NEG)
    m[:, C_MASK + 3 * P:C_MASK + 4 * P] = np.where(j <= q, 0.0, NEG)
    m[:, C_ONE:C_ONE + P] = 1.0
    inv = 10000.0 ** (-np.arange(16) / 16)
    for t in range(4):
        pos = t * P + np.arange(P)
        for h, at in enumerate((pos // 64, pos % 64)):
            ang = at[:, None] * inv[None, :]
            a = C_COS + t * 64 + h * 32
            m[:, a:a + 16] = m[:, a + 16:a + 32] = np.cos(ang)
            a = C_SIN + t * 32 + h * 16
            m[:, a:a + 16] = np.sin(ang)
    c["consts"] = m
    s = np.zeros((2, 2 * P + CAP))
    s[0, 0:P] = s[1, P:2 * P] = 1.0
    s[0, 2 * P:2 * P + CAP_L] = s[1, 2 * P + CAP_L:] = 1.0
    c["sel"] = s
    return {n: a.astype(np.float32) for n, a in c.items()}


_PLAIN = ["x_prompt", "x_sample", "c", "c_ctx", "cache_k", "cache_v", "ada_w", "ada_b", "w_in", "hy_f_w1", "hy_f_w2",
          "hy_f_w3", "hy_bias", "w_out", "router_w", "exp_w1", "exp_w3", "exp_w2", "final_g"]
_OUTS = [("y_prompt", (1, CTX, D)), ("y_sample", (1, LAT, D)),
         ("new_k", (1, DEPTH, CTX, KV, HD)), ("new_v", (1, DEPTH, CTX, KV, HD))]


def kernel(**inputs):
    import numpy as _np
    import concourse.bacc as _bacc
    from concourse import mybir as _mybir
    from concourse.bass_utils import run_bass_kernel_spmd as _run

    arrays = {n: _np.ascontiguousarray(inputs[n]) for n in _PLAIN}
    arrays.update(tables())
    prm = _np.zeros((DEPTH, P, NPRM), _np.float32)
    prm[:, :, G1:G1 + KC] = _np.asarray(inputs["norm1_g"]).reshape(DEPTH, P, KC)
    prm[:, :, G2:G2 + KC] = _np.asarray(inputs["norm2_g"]).reshape(DEPTH, P, KC)
    prm[:, :, GO:GO + KC] = _np.asarray(inputs["out_norm_g"]).reshape(DEPTH, KC, P).transpose(0, 2, 1)
    prm[:, :, CW:CW + 18] = _np.asarray(inputs["hy_conv_w"]).reshape(DEPTH, 18, P).transpose(0, 2, 1)
    prm[:, :, CB:CB + 6] = _np.asarray(inputs["hy_conv_b"]).reshape(DEPTH, 6, P).transpose(0, 2, 1)
    prm[:, :, GB:GB + GH] = _np.asarray(inputs["gm_b"]).transpose(0, 2, 1)
    prm[:, :, SK:SK + HEADS] = _np.asarray(inputs["attn_sink"])[:, None, :]
    prm[:, 0:FH, FB1] = _np.asarray(inputs["hy_f_b1"])
    prm[:, 0:FH, FB2] = _np.asarray(inputs["hy_f_b2"])
    prm[:, 0:FH, FQ] = _np.asarray(inputs["hy_freq"])
    arrays["params"] = prm
    arrays["ws_t"] = _np.ascontiguousarray(_np.asarray(inputs["gm_ws"]).transpose(0, 3, 1, 2).reshape(DEPTH, P, GH * P))

    nc = _bacc.Bacc("TRN2", target_bir_lowering=False, num_devices=1)
    ins, outs, feed = {}, {}, {}
    for n, a in arrays.items():
        feed[f"in_{n}"] = a
        ins[n] = nc.dram_tensor(f"in_{n}", a.shape, _mybir.dt.from_np(a.dtype), kind="ExternalInput").ap()
    for n, shape in _OUTS:
        outs[n] = nc.dram_tensor(f"out_{n}", shape, _mybir.dt.float32, kind="ExternalOutput").ap()
    hybrid_prefix_diffusion_step(nc, ins, outs)
    r = _run(nc, [feed], core_ids=[0])
    return tuple(r.results[0][f"out_{n}"] for n, _ in _OUTS)
```

```python
from contextlib import ExitStack

import concourse.bass as bass
from concourse import mybir

ALU = mybir.AluOpType
ACT = mybir.ActivationFunctionType
F32 = mybir.dt.float32
F32R = mybir.dt.float32r
U32 = mybir.dt.uint32
AX_X = mybir.AxisListType.X

P = 128
D = 1024
DEPTH = 2
LAT, CTX = 512, 128
NT = (LAT + CTX) // P
TOK = LAT + CTX
KC = D // P
HEADS, KV, HD = 8, 2, 64
ATT, KVW = HEADS * HD, KV * HD
HY, GM = 256, 256
GH = 4
TAPS = 3
EMB, FH = 33, 64
EXPERTS = 16
CAP_L, CAP_C = 2 * LAT // EXPERTS, 2 * CTX // EXPERTS
CAP = CAP_L + CAP_C
EPS = 1e-6
SLOTS = 3
ADA = 6
ROUNDS = ADA // SLOTS + 1
PAIRS = EXPERTS // 2
HALF = KC // 2
ASPLIT = 3
SPLIT0 = HALF - 1
MATS = 3 * EXPERTS
AHEAD = 4 * KC
SCALE = HD ** -0.5
NEG = -1e30
TWO_PI_HI, TWO_PI_LO = 6.28125, 6.283185307179586 - 6.28125
ROUND = 1.5 * 2.0 ** 23
PI_IN = 3.1415925

G1, G2, GO, CW, CB, GB, SK, FB1, FB2, FQ, AB, NPRM = 0, 8, 16, 24, 42, 48, 52, 60, 61, 62, 63, 96
C_ID, C_MASK, C_COS, C_SIN, C_ONE, NCST = 0, 128, 640, 896, 1024, 1152

V_LAYER, V_LAST = 140, 5
A_LAYER = 8


def hold(eng, s, value, done):
    value = eng.to_reg(value)
    eng.wait_ge(done, 32)
    eng.wait_ge(s, value)


def w3_at(e):
    return e * 3 + 1


def w1_next_at(e):
    return e * 3 + 2


def w2_at(e):
    return MATS - 1 if isinstance(e, int) and e == EXPERTS - 1 else e * 3 + 3


class Chain:

    def __init__(self, eng, sem, name, base, expect):
        self.eng, self.sem, self.base, self.n, self.expect, self.name = eng, sem, base, 0, expect, name

    def held(self, ins, done):
        self.n += 1
        ins.then_inc(self.sem, 1)
        hold(self.eng, self.sem, self.base + self.n, done)

    def __call__(self, ins):
        self.n += 1
        ins.then_inc(self.sem, 1)
        self.eng.wait_ge(self.sem, self.base + self.n)

    def close(self):
        assert self.n == self.expect, f"{self.name} has {self.n} links"


def hybrid_prefix_diffusion_step(nc, i, o):
    x_res = nc.dram_tensor("x_res", [TOK, D], F32).ap()
    xn_dram = nc.dram_tensor("xn_dram", [TOK, D], F32).ap()

    with ExitStack() as ctx:
        def sb(name, shape, dt=F32):
            return ctx.enter_context(nc.sbuf_tensor(name, shape, dt))

        def sb_twice(name, shape):
            with nc.sbuf_tensor(name, shape, F32) as plain:
                pass
            return plain, sb(name + "_r", shape, F32R)

        def sem(name):
            return ctx.enter_context(nc.semaphore(name))

        bank = [ctx.enter_context(nc.psum_tensor(f"bank{n}", [P, 512], F32)) for n in range(8)]
        ring, ring_r = sb_twice("ring", [P, SLOTS, KC * D])
        slot = [ring[:, s, :].rearrange("p (c n) -> p c n", c=KC) for s in range(SLOTS)]
        slot_r = [ring_r[:, s, :].rearrange("p (c n) -> p c n", c=KC) for s in range(SLOTS)]
        dft = ring[:, 2, :]
        dftc = dft[:, 3840:5888].rearrange("p (a k) -> p a k", a=4)
        dfts = dft[:, 5888:7936].rearrange("p (a k) -> p a k", a=4)
        dftcx, dftsx = dft[:, 7936:8064], dft[:, 8064:8192]
        hy = ring[:, 0, :]
        mixed_high = ring_r[:, 0, 0:KC * TOK].rearrange("p (c t) -> p c t", c=KC)
        arena_h, arena_hr = sb_twice("arena_h", [P, KC * TOK])
        hT = arena_h[:, :].rearrange("p (c t) -> p c t", c=KC)
        h_low = arena_hr[:, :].rearrange("p (c t) -> p c t", c=KC)
        filc = arena_h[:, 0:2048].rearrange("p (a k) -> p a k", a=4)
        fils = arena_h[:, 2048:4096].rearrange("p (a k) -> p a k", a=4)
        filcx, filsx = arena_h[:, 4096:4224], arena_h[:, 4224:4352]
        feats = arena_h[0:EMB, 4352:4992]
        final_g = arena_h[:, 0:D]
        arena_z, arena_zr = sb_twice("arena_z", [P, NT * 1280])
        zt = arena_z[:, :].rearrange("p (t n) -> p t n", t=NT)
        win = arena_z[:, 0:1280].rearrange("p (t n) -> p t n", t=NT)
        fsum = arena_z[:, 1280:2560].rearrange("p (t n) -> p t n", t=NT)
        fdif = arena_z[:, 2560:3840].rearrange("p (t n) -> p t n", t=NT)
        hfw, hbw = arena_z[:, 3840:4096], arena_z[:, 4096:4352]
        pre, turns, hid = (arena_z[0:FH, a:a + TOK] for a in (4352, 4992, 5632))
        fw1, fw2 = arena_z[0:EMB, 6272:6336], arena_z[0:FH, 6336:6400]
        xe = [arena_z[0:CAP, a:a + D] for a in (0, 1024)]
        ye = [arena_z[0:CAP, a:a + D] for a in (2048, 3072)]
        he = arena_z[0:CAP, 4096:5120]
        heT = [arena_zr[:, a:a + KC * CAP].rearrange("p (c t) -> p c t", c=KC) for a in (5120, 5760)]
        arena_u, arena_ur = sb_twice("arena_u", [P, 6400])
        mrow = [arena_u[0:5, a:a + D] for a in (1024, 2048)]
        ahigh = [arena_ur[:, 3072 + n * D:3072 + (n + 1) * D] for n in range(ASPLIT)]
        junk = arena_u[:, 5120:6144]
        h_high = arena_ur[:, 0:2560].rearrange("p (c t) -> p c t", c=4)
        h_high_z = arena_zr[:, :].rearrange("p (t n) -> p t n", t=NT)
        zhT = arena_u[:, 2560:6400].rearrange("p (m t) -> p m t", m=6)
        x0c = hy[:, 0:1280].rearrange("p (m t) -> p m t", m=2)
        spec = [hy[:, 1280 * a:1280 * a + 1280] for a in range(5)]
        uT = spec[1].rearrange("p (m t) -> p m t", m=2)
        utok = spec[2].rearrange("p (t n) -> p t n", t=NT)
        cvt = spec[3][:, 0:TOK]
        prod = [spec[n].rearrange("p (j n) -> p j n", j=NT) for n in (1, 2, 3, 4)]
        yh = spec[2].rearrange("p (m t) -> p m t", m=2)
        ysq = spec[4].rearrange("p (m t) -> p m t", m=2)
        hms, hrc, hy_y, hya = spec[3][:, 0:TOK], spec[3][:, TOK:2 * TOK], spec[0][:, 0:TOK], spec[0][:, TOK:2 * TOK]
        qT = [a[:, 0:2560].rearrange("p (i t) -> p i t", i=4) for a in (arena_u, arena_h)]
        kT = arena_u[:, 2560:3328]
        sbuf_s = [arena_u[:, 3328 + 512 * n:3840 + 512 * n] for n in range(2)]
        prob = [arena_u[:, 4352 + 512 * n:4864 + 512 * n] for n in range(2)]
        probT = [arena_u[:, 5376 + 512 * n:5888 + 512 * n] for n in range(2)]
        xn = arena_u[:, 0:5120].rearrange("p (t n) -> p t n", t=NT)
        xeT = [[arena_ur[:, a:a + KC * CAP].rearrange("p (c t) -> p c t", c=KC) for a in (b, b + 640)]
               for b in (0, 1280)]
        high = [arena_hr[:, c * D:(c + 1) * D] if c < 5 else arena_ur[:, 2560 + (c - 5) * D:2560 + (c - 4) * D]
                for c in range(KC)]
        spectrum = sb("spectrum", [P, 2, NT, HY])
        sflat = spectrum[:, :, :, :].rearrange("p a t n -> p (a t n)")
        g2e, s2e, xt = (sflat[:, a:a + KC * CAP].rearrange("p (c t) -> p c t", c=KC) for a in (640, 1280, 1920))
        affT = spectrum[0:EXPERTS, 0, 0:3, :].rearrange("p t n -> p (t n)")[:, 0:TOK]
        gate1 = sb("gate1", [P, 2, D])
        gate2 = sb("gate2", [CAP, D])
        cst = sb("cst", [P, NCST])
        ident = cst[:, C_ID:C_ID + P]
        mask = cst[:, C_MASK:C_MASK + 512]
        ones = cst[:, C_ONE:C_ONE + P]
        cos_t = cst[:, C_COS:C_COS + 256].rearrange("p (t n) -> p t n", t=4)
        sin_t = cst[:, C_SIN:C_SIN + 128].rearrange("p (t h n) -> p t h n", t=4, h=2)
        sel = sb("sel", [5, 2 * P + CAP + 2])
        join = sel[:, 2 * P + CAP:]
        prm = sb("prm", [P, NPRM])
        wsT = sb("wsT", [P, GH, P])
        rw = sb("rw", [P, KC, EXPERTS])
        ck, cv = sb("ck", [P, KVW]), sb("cv", [P, KVW])
        rtmp = sb("rtmp", [P, 640])
        jk = sb("jk", [P, 512])
        dbias = rtmp[0:1, 0:HY]
        fw3 = jk[0:FH, :]
        cvec = sb("cvec", [P, 2, KC])
        cs_r = sb("cs_r", [P, KC, 4], F32R)
        cs = sb("cs", [P, KC, 4])
        mod = sb("mod", [P, 4, KC, 2])
        nsink = sb("nsink", [P, HEADS])
        ssum, sms, srec, sroot, stmp = (sb(n, [P, 10]) for n in ("ssum", "sms", "srec", "sroot", "stmp"))
        negmax, rsum, esink, denom = (sb(n, [P, NT, HEADS]) for n in ("negmax", "rsum", "esink", "denom"))
        aff = sb("aff", [P, NT, EXPERTS])
        anm, asum, arec = (sb(n, [P, NT]) for n in ("anm", "asum", "arec"))
        topv = sb("topv", [EXPERTS, CAP])
        topi = sb("topi", [EXPERTS, CAP], U32)
        topf = sb("topf", [EXPERTS, CAP])
        idxT = sb("idxT", [CAP, EXPERTS + 1], U32)
        gateT = sb("gateT", [CAP, EXPERTS])
        icur = [sb(f"icur{n}", [CAP, 1], U32) for n in range(2)]
        iscat = [sb(f"iscat{n}", [CAP, 1], U32) for n in range(2)]

        arrived = [sem(f"arrived{s}") for s in range(SLOTS)]
        ada_in = [[sem(f"ada_in{n}_{h}") for h in range(2)] for n in range(SLOTS)]
        ahigh_ready = sem("ahigh_ready")
        alow_ready = sem("alow_ready")
        achunk_used = sem("achunk_used")
        used = [sem(f"used{s}") for s in range(SLOTS)]
        dft_in = sem("dft_in")
        const_in = sem("const_in")
        c_in = sem("c_in")
        x_copied = sem("x_copied")
        cs_done = sem("cs_done")
        cs_zero = sem("cs_zero")
        cs_parts = sem("cs_parts")
        prm_in = sem("prm_in")
        fil_in = sem("fil_in")
        bias_in = sem("bias_in")
        mrow_done = sem("mrow_done")
        mod_mm = sem("mod_mm")
        mod_out = sem("mod_out")
        f_mm = sem("f_mm")
        f_pre = sem("f_pre")
        f_sin = sem("f_sin")
        f3_mm = sem("f3_mm")
        f3_out = sem("f3_out")
        spec_mm = sem("spec_mm")
        spec_out = sem("spec_out")
        x_in = sem("x_in")
        sq1 = sem("sq1")
        rec1 = sem("rec1")
        root1 = sem("root1")
        xn1 = sem("xn1")
        t1_mm = sem("t1_mm")
        h1_v, h1_a = sem("h1_v"), sem("h1_a")
        h_hi, h_lo = sem("h_hi"), sem("h_lo")
        w_hi, w_lo = sem("w_hi"), sem("w_lo")
        z_mm = sem("z_mm")
        z_v, z_a = sem("z_v"), sem("z_a")
        kv_out = sem("kv_out")
        gm_mm = sem("gm_mm")
        gm_out = sem("gm_out")
        gm_sq = sem("gm_sq")
        u_done = sem("u_done")
        ut_mm = sem("ut_mm")
        ut_out = sem("ut_out")
        fwd_mm = sem("fwd_mm")
        y_done = sem("y_done")
        inv_mm = sem("inv_mm")
        yh_done = sem("yh_done")
        ysq_done = sem("ysq_done")
        yss_mm = sem("yss_mm")
        hrec = sem("hrec")
        hroot = sem("hroot")
        hy_done = sem("hy_done")
        rope_done = sem("rope_done")
        q_zero = sem("q_zero")
        qk_mm = sem("qk_mm")
        qk_a = sem("qk_a")
        sc_mm = sem("sc_mm")
        sc_out = sem("sc_out")
        p_done = sem("p_done")
        pt_mm = sem("pt_mm")
        pt_v, pt_a = sem("pt_v"), sem("pt_a")
        pv_mm = sem("pv_mm")
        es_in = sem("es_in")
        es_out = sem("es_out")
        a_done = sem("a_done")
        a_sq = sem("a_sq")
        mrec = sem("mrec")
        mroot = sem("mroot")
        mixn = sem("mixn")
        mx_mm = sem("mx_mm")
        mx_out = sem("mx_out")
        wo_hi, wo_lo = sem("wo_hi"), sem("wo_lo")
        m_hi, m_lo = sem("m_hi"), sem("m_lo")
        xr_in = [sem(f"xr_in{t}") for t in range(NT)]
        wo_mm = sem("wo_mm")
        x1_done = sem("x1_done")
        sq2 = sem("sq2")
        rec2 = sem("rec2")
        root2 = sem("root2")
        xn2 = sem("xn2")
        x1_out = sem("x1_out")
        xn_out = sem("xn_out")
        t2_mm = sem("t2_mm")
        h2_v, h2_a = sem("h2_v"), sem("h2_a")
        lg_mm = sem("lg_mm")
        anm_done = sem("anm_done")
        aexp = sem("aexp")
        aff_done = sem("aff_done")
        affT_mm = sem("affT_mm")
        affT_out = sem("affT_out")
        top_done = sem("top_done")
        top_mm = sem("top_mm")
        top_out = sem("top_out")
        half_in = [[sem(f"half_in{n}_{h}") for h in range(2)] for n in range(SLOTS)]
        high_ready = sem("high_ready")
        low_ready = sem("low_ready")
        chunk_used = sem("chunk_used")
        icur_done = sem("icur_done")
        xe_in = [sem("xe_in0"), sem("xe_in1")]
        xeT_mm = sem("xeT_mm")
        xt_scaled = sem("xt_scaled")
        xt_done = sem("xt_done")
        xh_done = sem("xh_done")
        xeT_out = sem("xeT_out")
        silu = sem("silu")
        he_done = sem("he_done")
        heT_mm = sem("heT_mm")
        hh_done = sem("hh_done")
        heT_out = sem("heT_out")
        ye_done = sem("ye_done")
        scattered = sem("scattered")
        rows_free = sem("rows_free")
        fin_in = sem("fin_in")
        fsq, frec, froot, y_out_done = sem("fsq"), sem("frec"), sem("froot"), sem("y_out_done")
        y_out = sem("y_out")
        v_link, v_flink, a_link = sem("v_link"), sem("v_flink"), sem("a_link")

        proj = ([("q", t, "v") for t in range(NT)] + [("kv", t, "a") for t in range(NT)]
                + [("zh", (m, half), "v") for m in range(6) for half in range(2)]
                + [("zg", t, "a") for t in range(NT)])
        NP_ = len(proj)
        Z_V, Z_A = (sum(p[2] == e for p in proj) for e in "va")

        def taken(n):
            e = proj[n][2]
            return (z_v if e == "v" else z_a), (Z_V if e == "v" else Z_A), sum(p[2] == e for p in proj[:n + 1])

        def multiplied(n):
            if n in (LAST_SLOT0, NP_ - 1):
                return used[0 if n == LAST_SLOT0 else 1], ROUNDS, 3
            return z_mm, NP_ - 2, n + 1 - (n > LAST_SLOT0)

        def proj_at(kind, t):
            return proj.index(next(p for p in proj if p[:2] == (kind, t)))

        LAST_SLOT0 = proj_at("zh", (1, 1))
        GROUPS = [0, NT, LAST_SLOT0 + 1, proj_at("zg", 0)]

        def w_group(w, g, c):
            cols = slice((g % 2) * 512, (g % 2) * 512 + 512)
            return w[g // 2][:, c:c + 2, cols], slot_r[2][:, c:c + 2, cols]

        def token_half(h):
            return (0, 3) if h == 0 else (3, NT)

        def high_of(c, a, b):
            if c < 4:
                return h_high[:, c, a * P:b * P]
            return h_high_z[:, a:b, 768 + (c - 4) * P:768 + (c - 3) * P]

        att = [(b, h) for b in range(NT) for h in range(HEADS)]

        def keys(b):
            if b == NT - 1:
                return [(LAT, P)], P
            blocks = [((b - 1) * P, P)] if b else []
            blocks += [(TOK, P), (b * P, 2 * P if b < 3 else P)]
            return blocks, 0 if b else P

        def values(b):
            if b == NT - 1:
                return [zt[:, b, 640:768]]
            v = [zt[:, b - 1, 640:768]] if b else []
            v += [cv[:, :], zt[:, b, 640:768]]
            return v + ([zt[:, b + 1, 640:768]] if b < 3 else [])

        MOD = [(0, "col"), (1, "col"), (2, "lat"), (2, "ctx"), (3, "col"), (4, "col"), (5, "cap")]
        spread = [1, 2, 4, 5, 6, 7]
        FWD = [6, 7, 0, 1, 2]

        def affinity_T(pe, l, t):
            pe.wait_ge(aff_done, l * NT + t + 1)
            if t:
                pe.wait_ge(affT_out, l * NT + t)
            pe.transpose(bank[7][0:EXPERTS, 0:P], aff[:, t, :], ident).then_inc(affT_mm, 1)

        def width(b):
            return sum(n for _, n in keys(b)[0])

        def chunks(l, m, c):
            return l * (MATS * KC) + m * KC + c + 1

        block = ctx.enter_context(nc.Block())

        @block.sync
        def _(sp):
            sp.dma_start(cvec[:, 0, :], i["c"].rearrange("a (p k) -> (a p) k", k=KC)).then_inc(c_in, 16)
            sp.dma_start(cvec[:, 1, :], i["c_ctx"].rearrange("(p k) -> p k", k=KC)).then_inc(c_in, 16)
            sp.dma_start(sel[:, :], i["sel"]).then_inc(const_in, 16)
            sp.dma_start(cst[:, :], i["consts"]).then_inc(const_in, 16)
            with sp.Fori(0, DEPTH) as l:
                for r in range(2):
                    for s in range(SLOTS):
                        j = SLOTS * r + s
                        if j == 1:
                            sp.wait_ge(prm_in, 160)
                        for h in range(2):
                            if r == 0:
                                sp.wait_ge(chunk_used, l * (MATS * KC) + AHEAD - (3, 1, 0)[s] * KC)
                            elif h == 0:
                                sp.wait_ge(achunk_used, ASPLIT + (l * ADA + s) * ASPLIT + 1)
                            else:
                                sp.wait_ge(used[s], l * ROUNDS + 1)
                            sp.dma_start(slot[s][:, h * HALF:(h + 1) * HALF, :],
                                         i["ada_w"][bass.ds(l, 1), :, j * D:(j + 1) * D]
                                         .rearrange("a (p c) n -> (a p) c n", p=P)[:, h * HALF:(h + 1) * HALF, :])\
                                .then_inc(ada_in[s][h], 16)
                for s in range(2):
                    sp.wait_ge(used[s], l * ROUNDS + 2)
                    sp.dma_start(slot[s], i["w_in"][bass.ds(l, 1), :, s * D:(s + 1) * D]
                                 .rearrange("a (p c) n -> (a p) c n", p=P)).then_inc(arrived[s], 16)
                sp.wait_ge(used[1], l * ROUNDS + 3)
                sp.dma_start(dftc, i["dft_cos"].rearrange("(a p) k -> p a k", p=P)).then_inc(dft_in, 16)
                sp.dma_start(dfts, i["dft_sin"].rearrange("(a p) k -> p a k", p=P)).then_inc(dft_in, 16)
                sp.dma_start(dftcx, i["dftx_cos"]).then_inc(dft_in, 16)
                sp.dma_start(dftsx, i["dftx_sin"]).then_inc(dft_in, 16)
                sp.wait_ge(inv_mm, l + 1)
                sp.dma_start(slot[2], i["w_out"][bass.ds(l, 1)]
                             .rearrange("a (c p) n -> (a p) c n", p=P)).then_inc(arrived[2], 16)

                def fill(s, name, e, before):
                    for h in range(2):
                        if before is None:
                            sp.wait_ge(used[2], l * ROUNDS + 3)
                        else:
                            sp.wait_ge(chunk_used, AHEAD + chunks(l, before, h * HALF + HALF - 1))
                        sp.dma_start(slot[s][:, h * HALF:(h + 1) * HALF, :],
                                     i[name][bass.ds(l, 1), bass.ds(e, 1)]
                                     .rearrange("a b (p c) n -> (a b p) c n", p=P)[:, h * HALF:(h + 1) * HALF, :])\
                            .then_inc(half_in[s][h], 16)

                fill(0, "exp_w1", 0, None)
                fill(1, "exp_w3", 0, None)
                fill(0, "exp_w1", 1, 0)
                fill(2, "exp_w2", 0, None)
                fill(1, "exp_w3", 1, w3_at(0))
                with sp.Fori(1, EXPERTS - 1) as e:
                    fill(0, "exp_w1", e + 1, w1_next_at(e) - 3)
                    fill(2, "exp_w2", e, w2_at(e) - 3)
                    fill(1, "exp_w3", e + 1, w3_at(e))
                fill(2, "exp_w2", EXPERTS - 1, w2_at(EXPERTS - 2))

        @block.gpsimd
        def _(pool):
            pool.sem_inc(rows_free, 2)

            with pool.Fori(0, DEPTH) as l:
                def layer(name):
                    return i[name][bass.ds(l, 1)]

                hold(pool, chunk_used, AHEAD + l * (MATS * KC), const_in)
                for j in (2, 5):
                    pool.dma_start(mrow[j % 2][4:5, :], layer("ada_b")[:, j * D:(j + 1) * D]).then_inc(bias_in, 16)
                pool.dma_start(prm[:, :], layer("params").rearrange("a p n -> (a p) n")).then_inc(prm_in, 16)
                pool.dma_start(fw1, layer("hy_f_w1").rearrange("a p n -> (a p) n")).then_inc(prm_in, 16)
                pool.dma_start(fw2, layer("hy_f_w2").rearrange("a p n -> (a p) n")).then_inc(prm_in, 16)
                pool.dma_start(fw3, layer("hy_f_w3").rearrange("a p n -> (a p) n")).then_inc(prm_in, 16)
                pool.dma_start(feats, i["feats"]).then_inc(prm_in, 16)
                pool.dma_start(dbias, layer("hy_bias")).then_inc(prm_in, 16)
                pool.dma_start(wsT[:, :, :], layer("ws_t").rearrange("a p (h n) -> (a p) h n", h=GH)).then_inc(prm_in, 16)
                pool.dma_start(rw[:, :, :], layer("router_w").rearrange("a (p c) n -> (a p) c n", p=P)).then_inc(prm_in, 16)
                pool.dma_start(ck[:, :], i["cache_k"][0, bass.ds(l, 1)].rearrange("a p h d -> (a p) (h d)")).then_inc(prm_in, 16)
                pool.dma_start(cv[:, :], i["cache_v"][0, bass.ds(l, 1)].rearrange("a p h d -> (a p) (h d)")).then_inc(prm_in, 16)
                pool.dma_start(win, i["window"].rearrange("(t p) n -> p t n", p=P)).then_inc(fil_in, 16)
                pool.dma_start(filc, i["fil_cos"].rearrange("(a p) k -> p a k", p=P)).then_inc(fil_in, 16)
                pool.dma_start(fils, i["fil_sin"].rearrange("(a p) k -> p a k", p=P)).then_inc(fil_in, 16)
                pool.dma_start(filcx, i["filx_cos"]).then_inc(fil_in, 16)
                pool.dma_start(filsx, i["filx_sin"]).then_inc(fil_in, 16)
                hold(pool, spec_mm, l * 5 + 5, const_in)
                pool.wait_ge(x_copied, 32)
                pool.dma_start(zt[:, :, 0:D], x_res.rearrange("(t p) d -> p t d", p=P)).then_inc(x_in, 16)
                hold(pool, used[1], l * ROUNDS + 3, const_in)
                pool.memset(qT[0][HD:P, :, :], 0.0).then_inc(q_zero, 1)
                pool.memset(qT[1][0:HD, :, :], 0.0).then_inc(q_zero, 1)
                s, per, n = taken(proj_at("kv", NT - 1))
                hold(pool, s, l * per + n, const_in)
                for name, a in (("new_k", 512), ("new_v", 640)):
                    pool.dma_start(o[name][0, bass.ds(l, 1)].rearrange("a p h d -> (a p) (h d)"),
                                   zt[:, NT - 1, a:a + KVW]).then_inc(kv_out, 16)
                for t in range(NT):
                    hold(pool, mx_mm, l * NT + t + 1, const_in)
                    if t == NT - 1:
                        hold(pool, kv_out, l * 32 + 32, const_in)
                    pool.dma_start(zt[:, t, 0:D], x_res[t * P:(t + 1) * P]).then_inc(xr_in[t], 16)
                for t in range(NT):
                    hold(pool, x1_done, l * NT + t + 1, const_in)
                    pool.dma_start(x_res[t * P:(t + 1) * P], zt[:, t, 0:D]).then_inc(x1_out, 16)
                    hold(pool, xn2, l * NT + t + 1, const_in)
                    pool.dma_start(xn_dram[t * P:(t + 1) * P], xn[:, t, :]).then_inc(xn_out, 16)
                hold(pool, x1_out, l * 80 + 80, const_in)
                hold(pool, xn_out, l * 80 + 80, const_in)

                def gather(u):
                    pool.indirect_dma_start(xe[u], None, xn_dram,
                                            bass.IndirectOffsetOnAxis(ap=icur[u][:, :], axis=0))\
                        .then_inc(xe_in[u], 16)

                def scatter(u, e):
                    hold(pool, ye_done, e + 1, const_in)
                    pool.indirect_dma_start(x_res, bass.IndirectOffsetOnAxis(ap=iscat[u][:, :], axis=0),
                                            ye[u], None, compute_op=ALU.add).then_inc(scattered, 16)
                    pool.wait_ge(scattered, e * 16 + 16)
                    pool.sem_inc(rows_free, 1)

                hold(pool, icur_done, l * (EXPERTS + 1) + 2, const_in)
                gather(0)
                gather(1)
                with pool.Fori(0, PAIRS - 1) as k:
                    for u in range(2):
                        e = k * 2 + u
                        hold(pool, icur_done, l * (EXPERTS + 1) + e + 3, const_in)
                        hold(pool, xeT_mm, l * EXPERTS + e + 1, const_in)
                        gather(u)
                        scatter(u, l * EXPERTS + e)
                scatter(0, l * EXPERTS + EXPERTS - 2)
                scatter(1, l * EXPERTS + EXPERTS - 1)

            pool.dma_start(zt[:, :, 0:D], x_res.rearrange("(t p) d -> p t d", p=P)).then_inc(fin_in, 16)
            pool.dma_start(final_g, i["final_g"].rearrange("(a d) -> a d", a=1).broadcast_to([P, D])).then_inc(fin_in, 16)
            pool.wait_ge(y_out_done, 1)
            pool.dma_start(o["y_sample"].rearrange("a (t p) d -> p (a t) d", p=P), zt[:, 0:4, 0:D]).then_inc(y_out, 16)
            pool.dma_start(o["y_prompt"].rearrange("a p d -> (a p) d"), zt[:, 4, 0:D]).then_inc(y_out, 16)
            pool.wait_ge(y_out, 32)
            pool.wait_ge(kv_out, 32 * DEPTH)

        @block.tensor
        def _(pe):
            pe.sem_inc(chunk_used, AHEAD)
            pe.sem_inc(achunk_used, ASPLIT)
            pe.wait_ge(const_in, 32)
            pe.wait_ge(cs_parts, 2)

            with pe.Fori(0, DEPTH) as l:
                def ada(j):
                    if j >= 2:
                        pe.wait_ge(mrow_done, l * ADA + j - 1)
                    out = [bank[2 * (j % 2) + n][0:4, :] for n in range(2)]
                    for c in range(KC):
                        k = c - SPLIT0
                        if c % HALF == 0:
                            pe.wait_ge(ada_in[j % SLOTS][c // HALF], l * 32 + 16 * (j // SLOTS + 1))
                        if 0 <= k < ASPLIT:
                            pe.wait_ge(alow_ready, (l * ADA + j) * ASPLIT + k + 1)
                            parts = ((cs_r, ahigh[k]), (cs_r, slot_r[j % SLOTS][:, c, :]))
                        else:
                            parts = ((cs, slot[j % SLOTS][:, c, :]),)
                        for part, (x, w) in enumerate(parts):
                            for n in range(2):
                                mm = pe.matmul(out[n], x[:, c, :], w[:, n * 512:(n + 1) * 512],
                                               start=(c == 0 and part == 0), stop=(c == KC - 1))
                        if 0 <= k < ASPLIT:
                            mm.then_inc(achunk_used, 1)
                    mm.then_inc(used[j % SLOTS], 1)

                def mod_step(q):
                    j, what = MOD[q]
                    if q:
                        pe.wait_ge(mod_out, l * len(MOD) + q)
                    if j == 0:
                        pe.wait_ge(bias_in, l * 32 + 32)
                    hold(pe, mrow_done, l * ADA + j + 1, const_in)
                    if what == "col":
                        for k in range(KC):
                            mm = pe.matmul(bank[4][:, 2 * k:2 * k + 2], mrow[j % 2][:, k:D:KC], join,
                                           start=True, stop=True)
                    else:
                        a, m = {"lat": (0, P), "ctx": (P, P), "cap": (2 * P, CAP)}[what]
                        for n in range(2):
                            mm = pe.matmul(bank[4 + n][0:m, :], sel[:, a:a + m],
                                           mrow[j % 2][:, n * 512:(n + 1) * 512], start=True, stop=True)
                    mm.then_inc(mod_mm, 1)

                def filter_layer(n):
                    if n == 0:
                        hold(pe, prm_in, l * 160 + 160, const_in)
                    else:
                        hold(pe, f_sin, l * 2 + 1, const_in)
                    w, x = (fw1, feats) if n == 0 else (fw2, hid)
                    pe.matmul(bank[6][0:FH, :], w, x[:, 0:LAT], start=True, stop=True)
                    pe.matmul(bank[7][0:FH, 0:CTX], w, x[:, LAT:TOK], start=True, stop=True).then_inc(f_mm, 1)

                def filter_taps(t):
                    if t >= 2:
                        pe.wait_ge(f3_out, l * NT + t - 1)
                    pe.matmul(bank[6 + t % 2][:, :], hid[:, t * P:(t + 1) * P], fw3, start=True, stop=True)\
                        .then_inc(f3_mm, 1)

                def filter_spectrum():
                    pe.wait_ge(f3_out, l * NT + NT)
                    pe.wait_ge(fil_in, l * 80 + 80)
                    for n in range(4):
                        if n >= 2:
                            pe.wait_ge(spec_out, l * 5 + n - 1)
                        table, taps = (filc, fsum) if n < 2 else (fils, fdif)
                        for j in range(2):
                            jj = 2 * (n % 2) + j
                            for a in range(4):
                                mm = pe.matmul(bank[6 + n % 2][:, j * HY:(j + 1) * HY],
                                               table[:, a, jj * P:(jj + 1) * P], taps[:, a, :],
                                               start=(a == 0), stop=(a == 3))
                        mm.then_inc(spec_mm, 1)
                    pe.wait_ge(spec_out, l * 5 + 3)
                    pe.matmul(bank[6][:, 0:HY], filcx, fsum[:, 4, :], start=True, stop=True)
                    pe.matmul(bank[6][:, HY:2 * HY], filsx, fdif[:, 4, :], start=True, stop=True).then_inc(spec_mm, 1)

                ada(0)
                filter_layer(0)
                ada(1)
                mod_step(0)
                filter_layer(1)
                ada(2)
                mod_step(1)
                pe.wait_ge(f_sin, l * 2 + 2)
                filter_taps(0)
                filter_taps(1)
                ada(3)
                mod_step(2)
                mod_step(3)
                filter_taps(2)
                filter_taps(3)
                ada(4)
                mod_step(4)
                filter_taps(4)
                filter_spectrum()
                ada(5)
                mod_step(5)
                mod_step(6)

                pe.wait_ge(mod_out, l * len(MOD) + len(MOD))
                pe.wait_ge(spec_out, l * 5 + 5)
                pe.wait_ge(mrow_done, l * ADA + ADA)
                for t in range(NT):
                    pe.wait_ge(xn1, l * NT + t + 1)
                    if t == 4:
                        pe.wait_ge(h1_v, l * NT + 1)
                        pe.wait_ge(h1_a, l * NT + 1)
                    for k in range(KC):
                        mm = pe.transpose(bank[2 * (t % 4) + k // 4][:, (k % 4) * P:(k % 4 + 1) * P],
                                          zt[:, t, k:D:KC], ident)
                    mm.then_inc(t1_mm, 1)

                for n, (kind, t, _) in enumerate(proj):
                    if n >= 8:
                        s, per, v = taken(n - 8)
                        pe.wait_ge(s, l * per + v)
                    out = bank[(n + 2) % 8]
                    g = max(x for x in range(4) if GROUPS[x] <= n)
                    if n < NT:
                        pe.wait_ge(h_lo, l * NT + n + 1)
                    for c in range(KC):
                        if n in GROUPS and c % 2 == 0:
                            pe.wait_ge(w_lo, l * 16 + g * 4 + c // 2 + 1)
                        for part in range(3):
                            if kind == "zh":
                                m, half = t
                                a, b = token_half(half)
                                x = h_low[:, c, a * P:b * P] if part == 1 else high_of(c, a, b)
                                col = 768 + m * P if m < 2 else (m - 2) * P
                                w = (slot_r[g // 2] if part == 2 else slot_r[2])[:, c, col:col + P]
                                pe_out, lhsT, rhs = out[:, 0:(b - a) * P], w, x
                            else:
                                col, m = {"q": (0, 512), "kv": (512, 256), "zg": (512, 512)}[kind]
                                x = h_low[:, c, t * P:(t + 1) * P] if part == 1 else \
                                    high_of(c, t, t + 1) if c < 4 else h_high_z[:, t, 768 + (c - 4) * P:768 + (c - 3) * P]
                                w = (slot_r[g // 2] if part == 2 else slot_r[2])[:, c, col:col + m]
                                if kind == "q":
                                    w = w.rearrange("p (g i d) -> p i g d", g=KV, i=4)
                                pe_out, lhsT, rhs = out[:, 0:m], x, w
                            mm = pe.matmul(pe_out, lhsT, rhs, start=(c == 0 and part == 0),
                                           stop=(c == KC - 1 and part == 2))
                    mm.then_inc(multiplied(n)[0], 1)

                for e in "av":
                    s, per, v = taken(max(n for n in range(NP_) if proj[n][2] == e))
                    pe.wait_ge(s, l * per + v)
                pe.wait_ge(prm_in, l * 160 + 160)
                for t in range(NT):
                    for h in range(GH):
                        mm = pe.matmul(bank[t // 2][:, (t % 2) * GM + h * 64:(t % 2) * GM + h * 64 + 64],
                                       wsT[:, h, :], zt[:, t, 1024 + h * 64:1088 + h * 64], start=True, stop=True)
                    if t % 2 or t == NT - 1:
                        mm.then_inc(gm_mm, 1)

                pe.wait_ge(u_done, l + 1)
                for t in range(NT):
                    for m in range(2):
                        mm = pe.transpose(bank[3 + t // 2][:, (t % 2) * HY + m * P:(t % 2) * HY + (m + 1) * P],
                                          uT[:, m, t * P:(t + 1) * P], ident)
                    if t % 2 or t == NT - 1:
                        mm.then_inc(ut_mm, 1)
                pe.wait_ge(dft_in, l * 64 + 64)
                pe.wait_ge(ut_out, l * 3 + 3)
                for n in range(4):
                    if n == 2:
                        pe.wait_ge(gm_out, l * 3 + 3)
                    table = dftc if n < 2 else dfts
                    for j in range(2):
                        jj = 2 * (n % 2) + j
                        for a in range(4):
                            pe.matmul(bank[FWD[n]][:, j * HY:(j + 1) * HY], table[:, a, jj * P:(jj + 1) * P],
                                      utok[:, a, :], start=(a == 0), stop=(a == 3))
                pe.matmul(bank[FWD[4]][:, 0:HY], dftcx, utok[:, 4, :], start=True, stop=True)
                pe.matmul(bank[FWD[4]][:, HY:2 * HY], dftsx, utok[:, 4, :], start=True, stop=True).then_inc(fwd_mm, 1)
                pe.wait_ge(y_done, l + 1)
                for m in range(2):
                    for n in range(8):
                        pe.matmul(bank[3 + m][:, :], prod[0 if n < 4 else 2][:, n % 4, m * P:(m + 1) * P],
                                  (dftc if n < 4 else dfts)[:, n % 4, :], start=(n == 0), stop=(n == 7))
                for m in range(2):
                    for n in range(2):
                        mm = pe.matmul(bank[5][:, m * P:(m + 1) * P], prod[2 * n][:, 4, m * P:(m + 1) * P],
                                       dftsx if n else dftcx, start=(n == 0), stop=(n == 1))
                mm.then_inc(inv_mm, 1)
                pe.wait_ge(ysq_done, l + 1)
                for m in range(2):
                    pe.matmul(bank[6][:, :], ones, ysq[:, m, 0:LAT], start=(m == 0), stop=(m == 1))
                for m in range(2):
                    mm = pe.matmul(bank[7][:, 0:CTX], ones, ysq[:, m, LAT:TOK], start=(m == 0), stop=(m == 1))
                mm.then_inc(yss_mm, 1)

                pe.wait_ge(hy_done, l + 1)
                for t in range(NT):
                    if t < 4:
                        pe.wait_ge(rope_done, l * 4 + t + 1)
                    if t >= 2:
                        pe.wait_ge(qk_a, l * 7 + t - 1)
                    for n in range(4):
                        mm = pe.transpose(bank[t % 2][:, n * P:(n + 1) * P], zt[:, t, n * P:(n + 1) * P], ident)
                    mm.then_inc(qk_mm, 1)
                for t in range(4):
                    mm = pe.transpose(bank[2][:, t * P:(t + 1) * P], zt[:, t, 512:640], ident)
                mm.then_inc(qk_mm, 1)
                pe.transpose(bank[3][:, 0:P], zt[:, 4, 512:640], ident)
                pe.transpose(bank[3][:, P:2 * P], ck[:, :], ident).then_inc(qk_mm, 1)

                pe.wait_ge(qk_a, l * 7 + 7)
                pe.wait_ge(q_zero, l * 2 + 2)
                for n in range(len(att) + 3):
                    if n < len(att):
                        b, h = att[n]
                        if n >= 2:
                            pe.wait_ge(sc_out, l * len(att) + n - 1)
                        at = 0
                        for col, w in keys(b)[0]:
                            mm = pe.matmul(bank[4 + n % 2][:, at:at + w], qT[h // 4][:, h % 4, b * P:(b + 1) * P],
                                           kT[:, col:col + w], start=True, stop=True)
                            at += w
                        mm.then_inc(sc_mm, 1)
                    m = n - 2
                    if 0 <= m < len(att):
                        pe.wait_ge(p_done, l * len(att) + m + 1)
                        if m >= 2:
                            pe.wait_ge(pt_v if m % 2 else pt_a, l * 20 + m // 2)
                        for x in range(width(att[m][0]) // P):
                            mm = pe.transpose(bank[6 + m % 2][:, x * P:(x + 1) * P],
                                              prob[m % 2][:, x * P:(x + 1) * P], ident)
                        mm.then_inc(pt_mm, 1)
                    m = n - 3
                    if 0 <= m < len(att):
                        b, h = att[m]
                        pe.wait_ge(pt_v if m % 2 else pt_a, l * 20 + m // 2 + 1)
                        if b == 4 and h == 0:
                            pe.wait_ge(a_done, l * NT + 1)
                        vs = values(b)
                        for x, v in enumerate(vs):
                            mm = pe.matmul(bank[b % 4][:, h * HD:(h + 1) * HD], probT[m % 2][:, x * P:(x + 1) * P],
                                           v[:, h // 4 * HD:h // 4 * HD + HD],
                                           start=(x == 0), stop=(x == len(vs) - 1))
                        mm.then_inc(pv_mm, 1)

                for t in range(NT):
                    pe.wait_ge(mixn, l * NT + t + 1)
                    if t >= 2:
                        pe.wait_ge(mx_out, l * NT + t - 1)
                    for n in range(6):
                        a = n * P if n < 4 else 768 + (n - 4) * P
                        mm = pe.transpose(bank[4 + 2 * (t % 2) + n // 4][:, (n % 4) * P:(n % 4 + 1) * P],
                                          zt[:, t, a:a + P], ident)
                    mm.then_inc(mx_mm, 1)
                pe.wait_ge(mx_out, l * NT + NT)

                pe.wait_ge(wo_lo, l * 8 + 8)
                for n in range(NT + 3):
                    if n < NT:
                        if n >= 2:
                            pe.wait_ge(x1_done, l * NT + n - 1)
                        pe.wait_ge(m_lo, l * NT + n + 1)
                        tile = slice(n * P, (n + 1) * P)
                        for x in range(2):
                            cols = slice(x * 512, (x + 1) * 512)
                            for c in range(KC):
                                parts = ((mixed_high[:, c, tile], slot_r[1][:, c, cols]),
                                         (mixed_high[:, c, tile], slot_r[2][:, c, cols]),
                                         (h_low[:, c, tile], slot_r[1][:, c, cols]))
                                for part, (m, w) in enumerate(parts):
                                    mm = pe.matmul(bank[2 * (n % 2) + x][:, :], m, w,
                                                   start=(c == 0 and part == 0), stop=(c == KC - 1 and part == 2))
                        mm.then_inc(wo_mm if n < NT - 1 else used[2], 1)
                    t = n - 1
                    if 0 <= t < NT:
                        pe.wait_ge(xn2, l * NT + t + 1)
                        if t:
                            pe.wait_ge(h2_v, l * NT + t)
                            pe.wait_ge(h2_a, l * NT + t)
                        for k in range(KC):
                            mm = pe.transpose(bank[4 + k // 4][:, (k % 4) * P:(k % 4 + 1) * P], xn[:, t, k:D:KC], ident)
                        mm.then_inc(t2_mm, 1)
                    t = n - 2
                    if 0 <= t < NT:
                        pe.wait_ge(h2_v, l * NT + t + 1)
                        pe.wait_ge(h2_a, l * NT + t + 1)
                        if t:
                            pe.wait_ge(aff_done, l * NT + t)
                        for c in range(KC):
                            mm = pe.matmul(bank[6][:, t * EXPERTS:(t + 1) * EXPERTS], hT[:, c, t * P:(t + 1) * P],
                                           rw[:, c, :], start=(c == 0), stop=(c == KC - 1))
                        mm.then_inc(lg_mm, 1)
                    t = n - 3
                    if 0 <= t < NT:
                        affinity_T(pe, l, t)
                hold(pe, top_done, l + 1, const_in)
                pe.transpose(bank[6][0:CAP, 0:EXPERTS], topf[:, :], ident[0:EXPERTS, 0:EXPERTS])
                pe.transpose(bank[6][0:CAP, EXPERTS:2 * EXPERTS], topv[:, :], ident[0:EXPERTS, 0:EXPERTS])\
                    .then_inc(top_mm, 1)

                def product(m, s, out, x, between=(None, None)):
                    for c in range(KC):
                        pe.wait_ge(low_ready, chunks(l, m, c))
                        parts = ((x[0], high[c]), (x[0], slot_r[s][:, c, :]), (x[1], high[c]))
                        for part, (xs, w) in enumerate(parts):
                            for n in range(2):
                                mm = pe.matmul(bank[out + n][0:CAP, :], xs[:, c, :], w[:, n * 512:(n + 1) * 512],
                                               start=(c == 0 and part == 0), stop=(c == KC - 1 and part == 2))
                        mm.then_inc(chunk_used, 1)
                        if c == between[0]:
                            between[1]()

                def rows_T(u, k):
                    pe.wait_ge(xe_in[u], (l * PAIRS + k) * 16 + 16)
                    for c in range(KC):
                        mm = pe.transpose(bank[6 + c // 4][:, (c % 4) * CAP:(c % 4 + 1) * CAP], xe[u][:, c:D:KC],
                                          ident[0:CAP, 0:CAP])
                    mm.then_inc(xeT_mm, 1)

                def hidden_T(e):
                    pe.wait_ge(he_done, l * EXPERTS + e + 1)
                    for c in range(KC):
                        mm = pe.transpose(bank[6 + c // 4][:, (c % 4) * CAP:(c % 4 + 1) * CAP], he[:, c:D:KC],
                                          ident[0:CAP, 0:CAP])
                    mm.then_inc(heT_mm, 1)

                def expert(e, u, k, last=False):
                    product(w3_at(e), 1, 2, xeT[u], (None, None) if last else (1, lambda: rows_T(1 - u, k + u)))
                    if last:
                        hidden_T(e)
                    else:
                        pe.wait_ge(xeT_out, l * EXPERTS + e + 2)
                        product(w1_next_at(e), 0, 0, xeT[1 - u], (3, lambda: hidden_T(e)))
                    pe.wait_ge(heT_out, l * EXPERTS + e + 1)
                    product(w2_at(e), 2, 4, heT)

                pe.wait_ge(top_out, l + 1)
                rows_T(0, 0)
                pe.wait_ge(xeT_out, l * EXPERTS + 1)
                product(0, 0, 0, xeT[0])
                with pe.Fori(0, PAIRS - 1) as k:
                    for u in range(2):
                        expert(k * 2 + u, u, k)
                expert(EXPERTS - 2, 0, PAIRS - 1)
                expert(EXPERTS - 1, 1, PAIRS - 1, last=True)
                pe.wait_ge(ye_done, l * EXPERTS + EXPERTS)

        @block.scalar
        def _(act):
            act.wait_ge(c_in, 32)
            act.activation(cs[:, :, 0:2].rearrange("p k s -> p s k"), cvec[:, :, :], ACT.Silu).then_inc(cs_done, 1)
            act.wait_ge(ada_in[0][0], 16)
            act.dma_start(x_res[0:LAT], i["x_sample"].rearrange("a t d -> (a t) d")).then_inc(x_copied, 16)
            act.dma_start(x_res[LAT:TOK], i["x_prompt"].rearrange("a t d -> (a t) d")).then_inc(x_copied, 16)

            with act.Fori(0, DEPTH) as l:
                link = Chain(act, a_link, "A_LAYER", l * A_LAYER, A_LAYER)

                def ada_rounded(j):
                    for k in range(ASPLIT):
                        c = SPLIT0 + k
                        if k < 2:
                            act.wait_ge(ada_in[j % SLOTS][c // HALF], l * 32 + 16 * (j // SLOTS + 1))
                        act.wait_ge(achunk_used, (l * ADA + j) * ASPLIT + k + 1)
                        act.activation(ahigh[k], slot[j % SLOTS][:, c, :], ACT.Copy).then_inc(ahigh_ready, 1)

                def sine(n):
                    act.wait_ge(f_pre, l * 2 + n + 1)
                    act.activation(hid, pre, ACT.Sin).then_inc(f_sin, 1)

                act.wait_ge(chunk_used, AHEAD + l * (MATS * KC))
                for j in range(5):
                    ada_rounded(j)
                    if j in (1, 2):
                        sine(j - 1)
                for n in range(5):
                    act.wait_ge(spec_mm, l * 5 + n + 1)
                    if n < 4:
                        dst, src = spectrum[:, n // 2, 2 * (n % 2):2 * (n % 2) + 2, :], bank[6 + n % 2][:, :]
                    else:
                        dst, src = spectrum[:, :, 4, :], bank[6][:, :]
                    act.activation(dst, src.rearrange("p (j n) -> p j n", j=2), ACT.Copy,
                                   scale=1.0 / (LAT if n < 4 else CTX)).then_inc(spec_out, 1)

                ada_rounded(5)

                act.wait_ge(x_in, l * 16 + 16)
                act.wait_ge(used[2], l * ROUNDS + 2)
                for t in range(NT):
                    ins = act.activation(junk, zt[:, t, 0:D], ACT.Square, accum_out=ssum[:, t:t + 1])
                    link(ins) if t < NT - 1 else ins.then_inc(sq1, 1)
                act.wait_ge(rec1, l + 1)
                act.activation(sroot[:, 0:NT], srec[:, 0:NT], ACT.Sqrt).then_inc(root1, 1)
                def w_in_rounded(g):
                    act.wait_ge(arrived[g // 2], l * 16 + 16)
                    for c in range(0, KC, 2):
                        w, high_w = w_group(slot, g, c)
                        act.activation(high_w, w, ACT.Copy).then_inc(w_hi, 1)

                w_in_rounded(0)
                act.wait_ge(mod_out, l * len(MOD) + len(MOD))

                def modulated(t, src, s0, done):
                    s = t // 4
                    for k in range(4, KC):
                        ins = act.activation(hT[:, k, t * P:(t + 1) * P], src[:, (k - 4) * P:(k - 3) * P], ACT.Identity,
                                             bias=mod[:, s0, k, s:s + 1], scale=mod[:, s0 + 1, k, s:s + 1])
                    ins.then_inc(done, 1)

                for n in range(NT + 1):
                    if n < NT:
                        act.wait_ge(t1_mm, l * NT + n + 1)
                        modulated(n, bank[2 * (n % 4) + 1], 0, h1_a)
                    t = n - 1
                    if t >= 0:
                        tile = slice(t * P, (t + 1) * P)
                        act.wait_ge(h1_v, l * NT + t + 1)
                        act.activation(h_high[:, :, tile], hT[:, 0:4, tile], ACT.Copy)
                        act.wait_ge(h1_a, l * NT + t + 1)
                        act.activation(h_high_z[:, t, 768:1280].rearrange("p (c n) -> p c n", c=4), hT[:, 4:8, tile],
                                       ACT.Copy).then_inc(h_hi, 1)
                w_in_rounded(1)

                for n, (kind, t, e) in enumerate(proj):
                    if n in (GROUPS[1], GROUPS[2]):
                        s, per, at = multiplied(n - 1)
                        act.wait_ge(s, l * per + at)
                        w_in_rounded(2 if n == GROUPS[1] else 3)
                    if e == "a":
                        s, per, at = multiplied(n)
                        act.wait_ge(s, l * per + at)
                        if kind == "kv":
                            act.activation(zt[:, t, 512:768], bank[(n + 2) % 8][:, 0:256], ACT.Copy).then_inc(z_a, 1)
                        else:
                            act.activation(zt[:, t, 768:1280], bank[(n + 2) % 8][:, :], ACT.Gelu_apprx_tanh).then_inc(z_a, 1)

                for g in range(3):
                    act.wait_ge(ut_mm, l * 3 + g + 1)
                    w = 2 if g < 2 else 1
                    act.activation(utok[:, 2 * g:2 * g + w, :], bank[3 + g][:, 0:w * HY].rearrange("p (t n) -> p t n", t=w),
                                   ACT.Copy).then_inc(ut_out, 1)
                act.wait_ge(gm_out, l * 3 + 3)
                for t in range(NT):
                    ins = act.activation(jk[:, 0:GM], zt[:, t, 768:1024], ACT.Square, accum_out=ssum[:, 5 + t:6 + t])
                    link(ins) if t < NT - 1 else ins.then_inc(gm_sq, 1)
                act.wait_ge(yh_done, l + 1)
                act.activation(ysq, yh, ACT.Square).then_inc(ysq_done, 1)
                act.wait_ge(hrec, l + 1)
                act.activation(hy_y, hrc, ACT.Sqrt).then_inc(hroot, 1)

                for n in range(7):
                    act.wait_ge(qk_mm, l * 7 + n + 1)
                    if n < 5:
                        for g in range(KV):
                            half = slice(g * HD, (g + 1) * HD)
                            ins = act.activation(qT[g][half, :, n * P:(n + 1) * P],
                                                 bank[n % 2][half, :].rearrange("p (i t) -> p i t", i=4), ACT.Copy)
                        ins.then_inc(qk_a, 1)
                    else:
                        dst, src = (kT[:, 0:512], bank[2][:, :]) if n == 5 else (kT[:, 512:768], bank[3][:, 0:256])
                        act.activation(dst, src, ACT.Copy).then_inc(qk_a, 1)

                for n in range(len(att) + 8):
                    if n % 4 == 2 and n < 32:
                        c = n // 4
                        act.wait_ge(arrived[2], l * 16 + 16)
                        act.activation(slot_r[1][:, c, :], slot[2][:, c, :], ACT.Copy).then_inc(wo_hi, 1)
                    if n < len(att):
                        b, h = att[n]
                        act.wait_ge(sc_out, l * len(att) + n + 1)
                        if n >= 2:
                            act.wait_ge(pt_mm, l * len(att) + n - 1)
                        w = width(b)
                        act.activation(prob[n % 2][:, 0:w], sbuf_s[n % 2][:, 0:w], ACT.Exp,
                                       bias=negmax[:, b, h:h + 1], scale=-1.0,
                                       accum_out=rsum[:, b, h:h + 1]).then_inc(p_done, 1)
                    m = n - 2
                    if 0 <= m < len(att) and m % 2 == 0:
                        act.wait_ge(pt_mm, l * len(att) + m + 1)
                        if m >= 2:
                            act.wait_ge(pv_mm, l * len(att) + m - 1)
                        w = width(att[m][0])
                        act.activation(probT[0][:, 0:w], bank[6][:, 0:w], ACT.Copy).then_inc(pt_a, 1)
                    if n >= 8 and n % 8 == 0:
                        b = n // 8 - 1
                        act.wait_ge(es_in, l * NT + b + 1)
                        act.activation(esink[:, b, :], denom[:, b, :], ACT.Exp).then_inc(es_out, 1)
                    if n >= 14 and n % 8 == 6:
                        b = n // 8 - 1
                        act.wait_ge(a_done, l * NT + b + 1)
                        ins = act.activation(jk[:, :], zt[:, b, 0:ATT], ACT.Square, accum_out=ssum[:, b:b + 1])
                        ins.then_inc(a_sq, 1)
                act.wait_ge(mrec, l + 1)
                act.activation(sroot[:, :], srec[:, :], ACT.Sqrt).then_inc(mroot, 1)
                for t in range(NT):
                    act.wait_ge(mx_out, l * NT + t + 1)
                    tile = slice(t * P, (t + 1) * P)
                    act.activation(mixed_high[:, :, tile], hT[:, :, tile], ACT.Copy).then_inc(m_hi, 1)

                for n in range(NT + 2):
                    if n < NT:
                        act.wait_ge(x1_done, l * NT + n + 1)
                        act.activation(junk, zt[:, n, 0:D], ACT.Square, accum_out=ssum[:, n:n + 1]).then_inc(sq2, 1)
                        act.wait_ge(rec2, l * NT + n + 1)
                        act.activation(sroot[:, n:n + 1], srec[:, n:n + 1], ACT.Sqrt).then_inc(root2, 1)
                    t = n - 1
                    if 0 <= t < NT:
                        act.wait_ge(t2_mm, l * NT + t + 1)
                        modulated(t, bank[5], 2, h2_a)
                    t = n - 2
                    if 0 <= t < NT:
                        act.wait_ge(anm_done, l * NT + t + 1)
                        act.activation(aff[:, t, :], bank[6][:, t * EXPERTS:(t + 1) * EXPERTS], ACT.Exp,
                                       bias=anm[:, t:t + 1], accum_out=asum[:, t:t + 1]).then_inc(aexp, 1)

                def rounded(m, s, e, after=(None, None)):
                    for c in range(KC):
                        if c % HALF == 0:
                            act.wait_ge(half_in[s][c // HALF], (l * EXPERTS + e) * 16 + 16)
                        act.wait_ge(chunk_used, AHEAD - KC + chunks(l, m, c))
                        act.activation(high[c], slot[s][:, c, :], ACT.Copy).then_inc(high_ready, 1)
                        if c == after[0]:
                            after[1]()

                def rows(x):
                    act.wait_ge(xt_done, l * EXPERTS + x + 1)
                    act.activation(xeT[x % 2 if isinstance(x, int) else 1 - u][0], xt, ACT.Copy).then_inc(xh_done, 1)

                def hidden(e):
                    act.wait_ge(heT_mm, l * EXPERTS + e + 1)
                    for n in range(2):
                        ins = act.activation(heT[0][:, 4 * n:4 * n + 4, :],
                                             bank[6 + n][:, 0:4 * CAP].rearrange("p (c t) -> p c t", c=4), ACT.Copy)
                    ins.then_inc(hh_done, 1)

                def gated(m, e):
                    act.wait_ge(chunk_used, AHEAD + chunks(l, m, KC - 1))
                    act.activation(he[:, 0:512], bank[0][0:CAP, :], ACT.Silu)
                    act.activation(he[:, 512:D], bank[1][0:CAP, :], ACT.Silu).then_inc(silu, 1)

                act.wait_ge(lg_mm, l * NT + NT)
                act.wait_ge(xn_out, l * 80 + 80)
                act.wait_ge(t2_mm, l * NT + NT)
                rounded(0, 0, 0)
                u = 1
                rows(0)
                rounded(w3_at(0), 1, 0)
                gated(0, 0)

                def prepare(e):
                    rounded(w1_next_at(e), 0, e + 1, (4, lambda: rows(e + 1)))
                    rounded(w2_at(e), 2, e, (5, lambda: hidden(e)))
                    gated(w1_next_at(e), e + 1)
                    rounded(w3_at(e + 1), 1, e + 1)

                with act.Fori(0, PAIRS - 1) as k:
                    for u in range(2):
                        prepare(k * 2 + u)
                u = 0
                prepare(EXPERTS - 2)
                rounded(w2_at(EXPERTS - 1), 2, EXPERTS - 1)
                hidden(EXPERTS - 1)
                link.close()

            act.wait_ge(fin_in, 32)
            for t in range(NT):
                act.activation(arena_u[:, t * D:(t + 1) * D], zt[:, t, 0:D], ACT.Square, accum_out=ssum[:, t:t + 1])\
                    .then_inc(fsq, 1)
            act.wait_ge(frec, 1)
            act.activation(sroot[:, 0:NT], srec[:, 0:NT], ACT.Sqrt).then_inc(froot, 1)

        @block.vector
        def _(v):
            def newton(link, root, ms, tmp):
                link(v.tensor_tensor(tmp, root, root, ALU.mult))
                link(v.tensor_tensor(tmp, tmp, ms, ALU.mult))
                link(v.tensor_scalar(tmp, tmp, -0.5, 1.5, ALU.mult, ALU.add))
                link(v.tensor_tensor(root, root, tmp, ALU.mult))

            v.memset(cs[:, :, 2:4], 0.0).then_inc(cs_zero, 1)
            v.wait_ge(const_in, 32)
            v.wait_ge(cs_done, 1)
            v.wait_ge(cs_zero, 1)
            v.tensor_copy(cs_r[:, :, 0:2], cs[:, :, 0:2]).then_inc(cs_parts, 1)
            v.wait_ge(cs_parts, 1)
            v.tensor_tensor(cs_r[:, :, 2:4], cs[:, :, 0:2], cs_r[:, :, 0:2], ALU.subtract).then_inc(cs_parts, 1)
            with v.Fori(0, DEPTH) as l:
                link = Chain(v, v_link, "V_LAYER", l * V_LAYER, V_LAYER)

                def row(j):
                    v.wait_ge(used[j % SLOTS], l * ROUNDS + j // SLOTS + 1)
                    if j >= 2:
                        v.wait_ge(mod_mm, l * len(MOD) + spread[j - 2])
                    for n in range(2):
                        ins = v.tensor_copy(mrow[j % 2][0:4, n * 512:(n + 1) * 512], bank[2 * (j % 2) + n][0:4, :])
                    ins.then_inc(mrow_done, 1)

                def mod_taken(q):
                    j, what = MOD[q]
                    v.wait_ge(mod_mm, l * len(MOD) + q + 1)
                    cols = bank[4][:, 0:2 * KC].rearrange("p (k s) -> p k s", s=2)
                    if what == "col":
                        n = {0: 0, 1: 1, 3: 2, 4: 3}[j]
                        bias = prm[:, AB + n * KC:AB + (n + 1) * KC].unsqueeze(2).broadcast_to([P, KC, 2])
                        ins = v.tensor_tensor(mod[:, n, :, :], cols, bias, ALU.add)
                        if n % 2 == 0:
                            ins.then_inc(mod_out, 1)
                        else:
                            link(ins)
                            g = prm[:, (G1 if j == 1 else G2):(G1 if j == 1 else G2) + KC]
                            v.scalar_tensor_tensor(out=mod[:, n, :, :], in0=mod[:, n, :, :], scalar=1.0,
                                                   in1=g.unsqueeze(2).broadcast_to([P, KC, 2]),
                                                   op0=ALU.add, op1=ALU.mult).then_inc(mod_out, 1)
                    else:
                        dst, m = {"lat": (gate1[:, 0, :], P), "ctx": (gate1[:, 1, :], P), "cap": (gate2[:, :], CAP)}[what]
                        for n in range(2):
                            ins = v.tensor_copy(dst[:, n * 512:(n + 1) * 512], bank[4 + n][0:m, :])
                        ins.then_inc(mod_out, 1)

                def ada_rest(j):
                    for k in range(ASPLIT):
                        c = SPLIT0 + k
                        v.wait_ge(ahigh_ready, (l * ADA + j) * ASPLIT + k + 1)
                        v.tensor_tensor(slot_r[j % SLOTS][:, c, :], slot[j % SLOTS][:, c, :], ahigh[k],
                                        ALU.subtract).then_inc(alow_ready, 1)

                def phase(n):
                    v.wait_ge(f_mm, l * 2 + n + 1)
                    b1, fq = prm[0:FH, FB1 + n:FB1 + n + 1], prm[0:FH, FQ:FQ + 1]
                    v.tensor_scalar(pre[:, 0:LAT], bank[6][0:FH, :], b1, fq, ALU.add, ALU.mult)
                    link(v.tensor_scalar(pre[:, LAT:TOK], bank[7][0:FH, 0:CTX], b1, fq, ALU.add, ALU.mult))
                    link(v.tensor_scalar(turns, pre, 1.0 / (TWO_PI_HI + TWO_PI_LO), ROUND, ALU.mult, ALU.add))
                    link(v.tensor_scalar(turns, turns, ROUND, None, ALU.subtract))
                    link(v.scalar_tensor_tensor(out=pre, in0=turns, scalar=-TWO_PI_HI, in1=pre, op0=ALU.mult, op1=ALU.add))
                    link(v.scalar_tensor_tensor(out=pre, in0=turns, scalar=-TWO_PI_LO, in1=pre, op0=ALU.mult, op1=ALU.add))
                    v.tensor_scalar(pre, pre, PI_IN, -PI_IN, ALU.min, ALU.max).then_inc(f_pre, 1)

                def taps(t):
                    v.wait_ge(f3_mm, l * NT + t + 1)
                    src = bank[6 + t % 2]
                    v.tensor_tensor(hfw, src[:, 0:HY], win[:, t, :], ALU.mult)
                    link(v.tensor_tensor(hbw, src[:, HY:2 * HY], win[:, t, :], ALU.mult))
                    if t in (0, 4):
                        v.tensor_tensor(hfw[0:1, :], hfw[0:1, :], dbias, ALU.add)
                        link(v.memset(hbw[0:1, :], 0.0))
                    v.tensor_tensor(fsum[:, t, :], hfw, hbw, ALU.add)
                    ins = v.tensor_tensor(fdif[:, t, :], hfw, hbw, ALU.subtract)
                    ins.then_inc(f3_out, 1)
                    v.wait_ge(f3_out, l * NT + t + 1)

                ada_rest(0)
                v.wait_ge(prm_in, l * 160 + 160)
                v.tensor_scalar(nsink[:, :], prm[:, SK:SK + HEADS], -1.0, None, ALU.mult)
                ada_rest(1)
                phase(0)
                row(0)
                ada_rest(2)
                mod_taken(0)
                phase(1)
                row(1)
                v.wait_ge(fil_in, l * 80 + 80)
                ada_rest(3)
                mod_taken(1)
                taps(0)
                taps(1)
                row(2)
                ada_rest(4)
                mod_taken(2)
                mod_taken(3)
                taps(2)
                taps(3)
                row(3)
                mod_taken(4)
                taps(4)
                ada_rest(5)
                row(4)
                row(5)
                mod_taken(5)
                mod_taken(6)

                v.wait_ge(sq1, l + 1)
                link(v.tensor_scalar(sms[:, 0:NT], ssum[:, 0:NT], 1.0 / D, EPS, ALU.mult, ALU.add))
                v.reciprocal(srec[:, 0:NT], sms[:, 0:NT]).then_inc(rec1, 1)
                v.wait_ge(root1, l + 1)
                newton(link, sroot[:, 0:NT], sms[:, 0:NT], stmp[:, 0:NT])
                for t in range(NT):
                    v.tensor_scalar(zt[:, t, 0:D], zt[:, t, 0:D], sroot[:, t:t + 1], None, ALU.mult).then_inc(xn1, 1)

                def modulated(t, src, s0, done):
                    s = t // 4
                    for k in range(4):
                        ins = v.tensor_scalar(hT[:, k, t * P:(t + 1) * P], src[:, k * P:(k + 1) * P],
                                              mod[:, s0 + 1, k, s:s + 1], mod[:, s0, k, s:s + 1], ALU.mult, ALU.add)
                    ins.then_inc(done, 1)

                def w_in_rest(g):
                    for c in range(0, KC, 2):
                        v.wait_ge(w_hi, l * 16 + g * 4 + c // 2 + 1)
                        w, high_w = w_group(slot, g, c)
                        v.tensor_tensor(w_group(slot_r, g, c)[0], w, high_w, ALU.subtract).then_inc(w_lo, 1)

                v.wait_ge(mod_out, l * len(MOD) + len(MOD))
                for n in range(NT + 2):
                    if n < NT:
                        v.wait_ge(t1_mm, l * NT + n + 1)
                        modulated(n, bank[2 * (n % 4)], 0, h1_v)
                    if n == 1:
                        w_in_rest(0)
                    t = n - 2
                    if t >= 0:
                        v.wait_ge(h_hi, l * NT + t + 1)
                        tile = slice(t * P, (t + 1) * P)
                        v.tensor_tensor(h_low[:, 0:4, tile], hT[:, 0:4, tile], h_high[:, :, tile], ALU.subtract)
                        v.tensor_tensor(h_low[:, 4:8, tile], hT[:, 4:8, tile],
                                        h_high_z[:, t, 768:1280].rearrange("p (c n) -> p c n", c=4), ALU.subtract)\
                            .then_inc(h_lo, 1)
                w_in_rest(1)

                for n, (kind, t, e) in enumerate(proj):
                    if n in (GROUPS[1], GROUPS[2]):
                        w_in_rest(2 if n == GROUPS[1] else 3)
                    if e == "v":
                        s, per, at = multiplied(n)
                        v.wait_ge(s, l * per + at)
                        if kind == "q":
                            dst, src = zt[:, t, 0:512], bank[(n + 2) % 8][:, :]
                        else:
                            a, b = token_half(t[1])
                            dst, src = zhT[:, t[0], a * P:b * P], bank[(n + 2) % 8][:, 0:(b - a) * P]
                        v.tensor_copy(dst, src).then_inc(z_v, 1)
                v.wait_ge(z_v, l * Z_V + Z_V)

                for m in range(6):
                    dst = x0c[:, m, :] if m < 2 else uT[:, m - 2, :] if m < 4 else cvt
                    w = [prm[:, CW + 6 * j + m:CW + 6 * j + m + 1] for j in range(TAPS)]
                    link(v.tensor_scalar(dst, zhT[:, m, :], w[1], prm[:, CB + m:CB + m + 1], ALU.mult, ALU.add))
                    for j, (to, fr) in enumerate(((1, 0), (0, 1))):
                        for a, b in ((0, LAT), (LAT, TOK)):
                            ins = v.scalar_tensor_tensor(out=dst[:, a + to:b - fr], in0=zhT[:, m, a + fr:b - to],
                                                         scalar=w[2 * j], in1=dst[:, a + to:b - fr],
                                                         op0=ALU.mult, op1=ALU.add)
                        link(ins)
                    if m >= 4:
                        ins = v.tensor_tensor(uT[:, m - 4, :], uT[:, m - 4, :], cvt, ALU.mult)
                        link(ins) if m == 4 else ins.then_inc(u_done, 1)

                for t in range(4):
                    s, per, n = taken(proj_at("kv", t))
                    v.wait_ge(s, l * per + n)
                    x = zt[:, t, 0:640].rearrange("p (h a b n) -> p h a b n", h=10, a=2, b=2)
                    r = rtmp[:, :].rearrange("p (h a b n) -> p h a b n", h=10, a=2, b=2)
                    sn = sin_t[:, t].unsqueeze(1).broadcast_to([P, 10, 2, 16])
                    v.scalar_tensor_tensor(out=r[:, :, :, 0, :], in0=x[:, :, :, 1, :], scalar=-1.0, in1=sn,
                                           op0=ALU.mult, op1=ALU.mult)
                    link(v.tensor_tensor(r[:, :, :, 1, :], x[:, :, :, 0, :], sn, ALU.mult))
                    x3 = zt[:, t, 0:640].rearrange("p (h d) -> p h d", h=10)
                    link(v.tensor_tensor(x3, x3, cos_t[:, t].unsqueeze(1).broadcast_to([P, 10, 64]), ALU.mult))
                    v.tensor_tensor(zt[:, t, 0:640], zt[:, t, 0:640], rtmp[:, :], ALU.add).then_inc(rope_done, 1)
                    v.wait_ge(rope_done, l * 4 + t + 1)

                for g in range(3):
                    v.wait_ge(gm_mm, l * 3 + g + 1)
                    ts = [t for t in (2 * g, 2 * g + 1) if t < NT]
                    for x, t in enumerate(ts):
                        ins = v.tensor_tensor(zt[:, t, 1024:1280].rearrange("p (h c) -> p h c", h=GH),
                                              bank[g][:, x * GM:(x + 1) * GM].rearrange("p (h c) -> p h c", h=GH),
                                              prm[:, GB:GB + GH].unsqueeze(2).broadcast_to([P, GH, 64]), ALU.add)
                    link(ins)
                    for t in ts:
                        ins = v.tensor_tensor(zt[:, t, 768:1024], zt[:, t, 768:1024], zt[:, t, 1024:1280], ALU.mult)
                    ins.then_inc(gm_out, 1)

                v.wait_ge(fwd_mm, l + 1)
                v.wait_ge(spec_out, l * 5 + 5)
                for n, (x, f) in enumerate(((0, 0), (1, 1), (0, 1), (1, 0))):
                    for j in range(2):
                        v.tensor_tensor(prod[n][:, 2 * j:2 * j + 2, :],
                                        bank[FWD[2 * x + j]][:, :].rearrange("p (j n) -> p j n", j=2),
                                        spectrum[:, f, 2 * j:2 * j + 2, :], ALU.mult)
                    ins = v.tensor_tensor(prod[n][:, 4, :], bank[FWD[4]][:, x * HY:(x + 1) * HY],
                                          spectrum[:, f, 4, :], ALU.mult)
                link(ins)
                v.tensor_tensor(spec[1], spec[1], spec[2], ALU.subtract)
                v.tensor_tensor(spec[3], spec[3], spec[4], ALU.add).then_inc(y_done, 1)

                v.wait_ge(inv_mm, l + 1)
                for m in range(2):
                    v.tensor_tensor(yh[:, m, 0:LAT], bank[3 + m][:, :], x0c[:, m, 0:LAT], ALU.mult)
                v.tensor_tensor(yh[:, :, LAT:TOK], bank[5][:, 0:2 * CTX].rearrange("p (m t) -> p m t", m=2),
                                x0c[:, :, LAT:TOK], ALU.mult).then_inc(yh_done, 1)
                v.wait_ge(yss_mm, l + 1)
                v.tensor_scalar(hms[:, 0:LAT], bank[6][:, :], 1.0 / HY, EPS, ALU.mult, ALU.add)
                link(v.tensor_scalar(hms[:, LAT:TOK], bank[7][:, 0:CTX], 1.0 / HY, EPS, ALU.mult, ALU.add))
                v.reciprocal(hrc, hms).then_inc(hrec, 1)
                v.wait_ge(hroot, l + 1)
                newton(link, hy_y, hms, hya)
                for m in range(2):
                    ins = v.scalar_tensor_tensor(out=hT[:, 4 + m, :], in0=yh[:, m, :], scalar=prm[:, GO + 4 + m:GO + 5 + m],
                                                 in1=hy_y, op0=ALU.mult, op1=ALU.mult)
                ins.then_inc(hy_done, 1)

                for n in range(len(att) + 4):
                    if n % 4 == 3 and n < 32:
                        c = n // 4
                        v.wait_ge(wo_hi, l * 8 + c + 1)
                        v.tensor_tensor(slot_r[2][:, c, :], slot[2][:, c, :], slot_r[1][:, c, :], ALU.subtract)\
                            .then_inc(wo_lo, 1)
                    if n < len(att):
                        b, h = att[n]
                        if n >= 2:
                            v.wait_ge(p_done, l * len(att) + n - 1)
                        hold(v, sc_mm, l * len(att) + n + 1, const_in)
                        w, m0 = width(b), keys(b)[1]
                        v.tensor_tensor_reduce(out=sbuf_s[n % 2][:, 0:w], in0=bank[4 + n % 2][:, 0:w],
                                               in1=mask[:, m0:m0 + w], scale=-SCALE, scalar=nsink[:, h:h + 1],
                                               op0=ALU.add, op1=ALU.min,
                                               accum_out=negmax[:, b, h:h + 1]).then_inc(sc_out, 1)
                    m = n - 2
                    if 0 <= m < len(att) and m % 2:
                        v.wait_ge(pt_mm, l * len(att) + m + 1)
                        if m >= 2:
                            v.wait_ge(pv_mm, l * len(att) + m - 1)
                        w = width(att[m][0])
                        v.tensor_copy(probT[1][:, 0:w], bank[7][:, 0:w]).then_inc(pt_v, 1)
                    if n >= 8 and n % 8 == 0:
                        b = n // 8 - 1
                        v.wait_ge(sc_out, l * len(att) + n)
                        v.tensor_tensor(denom[:, b, :], negmax[:, b, :], nsink[:, :], ALU.subtract).then_inc(es_in, 1)
                    if n >= 11 and n % 8 == 3:
                        b = n // 8 - 1
                        v.wait_ge(es_out, l * NT + b + 1)
                        v.wait_ge(pv_mm, l * len(att) + 8 * b + 8)
                        link(v.tensor_tensor(denom[:, b, :], rsum[:, b, :], esink[:, b, :], ALU.add))
                        link(v.reciprocal(denom[:, b, :], denom[:, b, :]))
                        v.tensor_tensor(zt[:, b, 0:ATT].rearrange("p (h d) -> p h d", h=HEADS),
                                        bank[b % 4][:, :].rearrange("p (h d) -> p h d", h=HEADS),
                                        denom[:, b, :].unsqueeze(2).broadcast_to([P, HEADS, HD]), ALU.mult)\
                            .then_inc(a_done, 1)

                v.wait_ge(a_sq, l * NT + NT)
                v.wait_ge(gm_sq, l + 1)
                v.tensor_scalar(sms[:, 0:5], ssum[:, 0:5], 1.0 / ATT, EPS, ALU.mult, ALU.add)
                link(v.tensor_scalar(sms[:, 5:10], ssum[:, 5:10], 1.0 / GM, EPS, ALU.mult, ALU.add))
                v.reciprocal(srec[:, :], sms[:, :]).then_inc(mrec, 1)
                v.wait_ge(mroot, l + 1)
                newton(link, sroot[:, :], sms[:, :], stmp[:, :])
                v.wait_ge(a_done, l * NT + NT)
                v.wait_ge(gm_out, l * 3 + 3)
                for t in range(NT):
                    v.tensor_scalar(zt[:, t, 0:ATT], zt[:, t, 0:ATT], sroot[:, t:t + 1], None, ALU.mult)
                    v.tensor_scalar(zt[:, t, 768:1024], zt[:, t, 768:1024], sroot[:, 5 + t:6 + t], None, ALU.mult)\
                        .then_inc(mixn, 1)
                def mixed_rest(t):
                    v.wait_ge(m_hi, l * NT + t + 1)
                    tile = slice(t * P, (t + 1) * P)
                    v.tensor_tensor(h_low[:, :, tile], hT[:, :, tile], mixed_high[:, :, tile], ALU.subtract)\
                        .then_inc(m_lo, 1)

                for t in range(NT):
                    v.wait_ge(mx_mm, l * NT + t + 1)
                    for x, (c, w) in enumerate(((0, 4), (6, 2))):
                        ins = v.tensor_tensor(hT[:, c:c + w, t * P:(t + 1) * P],
                                              bank[4 + 2 * (t % 2) + x][:, 0:w * P].rearrange("p (c t) -> p c t", c=w),
                                              prm[:, GO + c:GO + c + w].unsqueeze(2).broadcast_to([P, w, P]), ALU.mult)
                    ins.then_inc(mx_out, 1)
                    if t:
                        mixed_rest(t - 1)
                mixed_rest(NT - 1)

                for n in range(NT + 3):
                    if n < NT:
                        if n < NT - 1:
                            v.wait_ge(wo_mm, l * (NT - 1) + n + 1)
                        else:
                            v.wait_ge(used[2], l * ROUNDS + 3)
                        halves = (rtmp[:, 0:512], jk[:, :])
                        for x in range(2):
                            ins = v.tensor_tensor(halves[x], bank[2 * (n % 2) + x][:, :],
                                                  gate1[:, n // 4, x * 512:(x + 1) * 512], ALU.mult)
                        link(ins)
                        v.wait_ge(xr_in[n], l * 16 + 16)
                        for x in range(2):
                            a = zt[:, n, x * 512:(x + 1) * 512]
                            ins = v.tensor_tensor(a, a, halves[x], ALU.add)
                        ins.then_inc(x1_done, 1)
                        v.wait_ge(sq2, l * NT + n + 1)
                        c = slice(n, n + 1)
                        link(v.tensor_scalar(sms[:, c], ssum[:, c], 1.0 / D, EPS, ALU.mult, ALU.add))
                        v.reciprocal(srec[:, c], sms[:, c]).then_inc(rec2, 1)
                        v.wait_ge(root2, l * NT + n + 1)
                        newton(link, sroot[:, c], sms[:, c], stmp[:, c])
                        v.wait_ge(x1_done, l * NT + n + 1)
                        v.tensor_scalar(xn[:, n, :], zt[:, n, 0:D], sroot[:, c], None, ALU.mult).then_inc(xn2, 1)
                    t = n - 1
                    if 0 <= t < NT:
                        v.wait_ge(t2_mm, l * NT + t + 1)
                        modulated(t, bank[4], 2, h2_v)
                    t = n - 2
                    if 0 <= t < NT:
                        v.wait_ge(lg_mm, l * NT + t + 1)
                        v.tensor_reduce(anm[:, t:t + 1], bank[6][:, t * EXPERTS:(t + 1) * EXPERTS], AX_X, ALU.max,
                                        negate=True).then_inc(anm_done, 1)
                        v.wait_ge(aexp, l * NT + t + 1)
                        link(v.reciprocal(arec[:, t:t + 1], asum[:, t:t + 1]))
                        v.tensor_scalar(aff[:, t, :], aff[:, t, :], arec[:, t:t + 1], None, ALU.mult).then_inc(aff_done, 1)
                    t = n - 3
                    if 0 <= t < NT:
                        v.wait_ge(affT_mm, l * NT + t + 1)
                        v.tensor_copy(affT[:, t * P:(t + 1) * P], bank[7][0:EXPERTS, 0:P]).then_inc(affT_out, 1)
                hold(v, affT_out, l * NT + NT, const_in)
                for a, b, c0, c1 in ((0, LAT, 0, CAP_L), (LAT, TOK, CAP_L, CAP)):
                    for c in range(c0, c1, 8):
                        link.held(v.max(topv[:, c:c + 8], affT[:, a:b]), const_in)
                        link.held(v.max_index(topi[:, c:c + 8], topv[:, c:c + 8], affT[:, a:b]), const_in)
                        if c + 8 < c1:
                            link.held(v.match_replace(affT[:, a:b], topv[:, c:c + 8], affT[:, a:b], -1.0), const_in)
                v.tensor_copy(topf[:, 0:CAP_L], topi[:, 0:CAP_L])
                v.tensor_scalar(topf[:, CAP_L:CAP], topi[:, CAP_L:CAP], float(LAT), None, ALU.add).then_inc(top_done, 1)
                v.wait_ge(top_mm, l + 1)
                link(v.tensor_copy(idxT[:, 0:EXPERTS], bank[6][0:CAP, 0:EXPERTS]))
                v.tensor_copy(idxT[:, EXPERTS:EXPERTS + 1], idxT[:, 0:1])
                v.tensor_copy(icur[0][:, :], idxT[:, 0:1]).then_inc(icur_done, 1)
                v.tensor_copy(icur[1][:, :], idxT[:, 1:2]).then_inc(icur_done, 1)
                v.tensor_copy(gateT[:, :], bank[6][0:CAP, EXPERTS:2 * EXPERTS]).then_inc(top_out, 1)
                for dst, n in ((g2e, 3), (s2e, 2)):
                    v.tensor_copy(dst[:, :, 0:CAP_L], mod[:, n, :, 0:1].broadcast_to([P, KC, CAP_L]))
                    ins = v.tensor_copy(dst[:, :, CAP_L:CAP], mod[:, n, :, 1:2].broadcast_to([P, KC, CAP_C]))
                link(ins)

                def rest(m, s, after={}):
                    for c in range(KC):
                        v.wait_ge(high_ready, chunks(l, m, c))
                        v.tensor_tensor(slot_r[s][:, c, :], slot[s][:, c, :], high[c], ALU.subtract).then_inc(low_ready, 1)
                        if c in after:
                            after[c]()

                def rows(x, u):
                    v.wait_ge(xeT_mm, l * EXPERTS + x + 1)
                    if not (isinstance(x, int) and x == EXPERTS - 1):
                        v.tensor_copy(icur[u][:, :], idxT[:, bass.ds(x + 2, 1)]).then_inc(icur_done, 1)
                    for n in range(2):
                        ins = v.tensor_tensor(xt[:, 4 * n:4 * n + 4, :],
                                              bank[6 + n][:, 0:4 * CAP].rearrange("p (c t) -> p c t", c=4),
                                              g2e[:, 4 * n:4 * n + 4, :], ALU.mult)
                    ins.then_inc(xt_scaled, 1)
                    v.wait_ge(xt_scaled, l * EXPERTS + x + 1)
                    v.tensor_tensor(xt, xt, s2e, ALU.add).then_inc(xt_done, 1)

                def rows_rest(x, u):
                    v.wait_ge(xh_done, l * EXPERTS + x + 1)
                    v.tensor_tensor(xeT[u][1], xt, xeT[u][0], ALU.subtract).then_inc(xeT_out, 1)

                def hidden(e):
                    v.wait_ge(chunk_used, AHEAD + chunks(l, w3_at(e), KC - 1))
                    v.wait_ge(silu, l * EXPERTS + e + 1)
                    for n in range(2):
                        a = he[:, n * 512:(n + 1) * 512]
                        ins = v.tensor_tensor(a, a, bank[2 + n][0:CAP, :], ALU.mult)
                    ins.then_inc(he_done, 1)

                def hidden_rest(e):
                    v.wait_ge(hh_done, l * EXPERTS + e + 1)
                    for n in range(2):
                        c = slice(4 * n, 4 * n + 4)
                        ins = v.tensor_tensor(heT[1][:, c, :], bank[6 + n][:, 0:4 * CAP].rearrange("p (c t) -> p c t", c=4),
                                              heT[0][:, c, :], ALU.subtract)
                    ins.then_inc(heT_out, 1)

                def result(e, u):
                    v.wait_ge(rows_free, l * EXPERTS + e + 1)
                    v.tensor_copy(iscat[u][:, :], idxT[:, bass.ds(e, 1)])
                    v.wait_ge(chunk_used, AHEAD + chunks(l, w2_at(e), KC - 1))
                    for n in range(2):
                        ins = v.scalar_tensor_tensor(out=ye[u][:, n * 512:(n + 1) * 512], in0=bank[4 + n][0:CAP, :],
                                                     scalar=gateT[:, bass.ds(e, 1)],
                                                     in1=gate2[:, n * 512:(n + 1) * 512],
                                                     op0=ALU.mult, op1=ALU.mult)
                    ins.then_inc(ye_done, 1)

                def expert(e, u):
                    rest(w1_next_at(e), 0, {2: lambda: rows(e + 1, 1 - u), 4: lambda: rows_rest(e + 1, 1 - u)})
                    hidden(e)
                    rest(w2_at(e), 2, {6: lambda: hidden_rest(e)})
                    rest(w3_at(e + 1), 1)
                    result(e, u)

                rest(0, 0)
                rows(0, 0)
                rows_rest(0, 0)
                rest(w3_at(0), 1)
                with v.Fori(0, PAIRS - 1) as k:
                    for u in range(2):
                        expert(k * 2 + u, u)
                expert(EXPERTS - 2, 0)
                hidden(EXPERTS - 1)
                rest(w2_at(EXPERTS - 1), 2)
                hidden_rest(EXPERTS - 1)
                result(EXPERTS - 1, 1)
                link.close()

            flink = Chain(v, v_flink, "V_LAST", 0, V_LAST)
            v.wait_ge(fsq, NT)
            flink(v.tensor_scalar(sms[:, 0:NT], ssum[:, 0:NT], 1.0 / D, EPS, ALU.mult, ALU.add))
            v.reciprocal(srec[:, 0:NT], sms[:, 0:NT]).then_inc(frec, 1)
            v.wait_ge(froot, 1)
            newton(flink, sroot[:, 0:NT], sms[:, 0:NT], stmp[:, 0:NT])
            for t in range(NT):
                ins = v.scalar_tensor_tensor(out=zt[:, t, 0:D], in0=zt[:, t, 0:D], scalar=sroot[:, t:t + 1],
                                             in1=final_g, op0=ALU.mult, op1=ALU.mult)
            ins.then_inc(y_out_done, 1)
            flink.close()


def tables():
    import numpy as np

    c = {}
    for name, n in (("", LAT), ("x", CTX)):
        k = np.arange(n, dtype=np.float64)
        half = np.pi / n * np.outer(k + 0.5, k + 0.5)
        whole = np.pi / n * np.outer(k, k + 0.5)
        c[f"dft{name}_cos"], c[f"dft{name}_sin"] = np.cos(half), np.sin(half)
        c[f"fil{name}_cos"], c[f"fil{name}_sin"] = np.cos(whole), np.sin(whole)
    feats, window = [], []
    lo, hi = np.log(1e-2) / 1.5, np.log(1e-2) / 0.3
    deltas = np.abs(np.linspace(lo, hi, HY))
    for n in (LAT, CTX):
        t = np.linspace(0.0, 1.0, n)[:, None]
        bands = (EMB - 1) // 2
        fb = np.linspace(1e-4, bands - 1, bands)[None, :]
        w = 2.0 * np.pi * np.arange(n)[:, None] / n
        feats.append(np.concatenate([t, np.cos(fb * w), -np.sin(fb * w)], axis=-1).T)
        window.append(np.exp(-t * deltas[None, :]))
    c["feats"] = np.concatenate(feats, axis=1)
    c["window"] = np.concatenate(window, axis=0)
    m = np.zeros((P, NCST))
    m[:, C_ID:C_ID + P] = np.eye(P)
    q, j = np.arange(P)[:, None], np.arange(P)[None, :]
    m[:, C_MASK:C_MASK + P] = np.where(j >= q, 0.0, NEG)
    m[:, C_MASK + 3 * P:C_MASK + 4 * P] = np.where(j <= q, 0.0, NEG)
    m[:, C_ONE:C_ONE + P] = 1.0
    inv = 10000.0 ** (-np.arange(16) / 16)
    for t in range(4):
        pos = t * P + np.arange(P)
        for h, at in enumerate((pos // 64, pos % 64)):
            ang = at[:, None] * inv[None, :]
            a = C_COS + t * 64 + h * 32
            m[:, a:a + 16] = m[:, a + 16:a + 32] = np.cos(ang)
            a = C_SIN + t * 32 + h * 16
            m[:, a:a + 16] = np.sin(ang)
    c["consts"] = m
    s = np.zeros((5, 2 * P + CAP + 2))
    s[4, 0:2 * P + CAP] = 1.0
    for n in range(2):
        s[n:4:2, n * P:(n + 1) * P] = s[n:4:2, 2 * P + CAP + n] = 1.0
    s[0:4:2, 2 * P:2 * P + CAP_L] = s[1:4:2, 2 * P + CAP_L:2 * P + CAP] = 1.0
    c["sel"] = s
    return {n: a.astype(np.float32) for n, a in c.items()}


_PLAIN = ["x_prompt", "x_sample", "c", "c_ctx", "cache_k", "cache_v", "ada_w", "ada_b", "w_in", "hy_f_w1", "hy_f_w2",
          "hy_f_w3", "hy_bias", "w_out", "router_w", "exp_w1", "exp_w3", "exp_w2", "final_g"]
_OUTS = [("y_prompt", (1, CTX, D)), ("y_sample", (1, LAT, D)),
         ("new_k", (1, DEPTH, CTX, KV, HD)), ("new_v", (1, DEPTH, CTX, KV, HD))]


def kernel(**inputs):
    import numpy as _np
    import concourse.bacc as _bacc
    from concourse import mybir as _mybir
    from concourse.bass_utils import run_bass_kernel_spmd as _run

    arrays = {n: _np.ascontiguousarray(inputs[n]) for n in _PLAIN}
    arrays.update(tables())
    prm = _np.zeros((DEPTH, P, NPRM), _np.float32)
    prm[:, :, G1:G1 + KC] = _np.asarray(inputs["norm1_g"]).reshape(DEPTH, P, KC)
    prm[:, :, G2:G2 + KC] = _np.asarray(inputs["norm2_g"]).reshape(DEPTH, P, KC)
    prm[:, :, GO:GO + KC] = _np.asarray(inputs["out_norm_g"]).reshape(DEPTH, KC, P).transpose(0, 2, 1)
    prm[:, :, CW:CW + 18] = _np.asarray(inputs["hy_conv_w"]).reshape(DEPTH, 18, P).transpose(0, 2, 1)
    prm[:, :, CB:CB + 6] = _np.asarray(inputs["hy_conv_b"]).reshape(DEPTH, 6, P).transpose(0, 2, 1)
    prm[:, :, GB:GB + GH] = _np.asarray(inputs["gm_b"]).transpose(0, 2, 1)
    prm[:, :, SK:SK + HEADS] = _np.asarray(inputs["attn_sink"])[:, None, :]
    prm[:, 0:FH, FB1] = _np.asarray(inputs["hy_f_b1"])
    prm[:, 0:FH, FB2] = _np.asarray(inputs["hy_f_b2"])
    prm[:, 0:FH, FQ] = _np.asarray(inputs["hy_freq"])
    prm[:, :, AB:AB + 4 * KC] = _np.asarray(inputs["ada_b"]).reshape(DEPTH, ADA, P, KC)[:, [0, 1, 3, 4]]\
        .transpose(0, 2, 1, 3).reshape(DEPTH, P, 4 * KC)
    arrays["params"] = prm
    arrays["ws_t"] = _np.ascontiguousarray(_np.asarray(inputs["gm_ws"]).transpose(0, 3, 1, 2).reshape(DEPTH, P, GH * P))

    nc = _bacc.Bacc("TRN2", target_bir_lowering=False, num_devices=1)
    ins, outs, feed = {}, {}, {}
    for n, a in arrays.items():
        feed[f"in_{n}"] = a
        ins[n] = nc.dram_tensor(f"in_{n}", a.shape, _mybir.dt.from_np(a.dtype), kind="ExternalInput").ap()
    for n, shape in _OUTS:
        outs[n] = nc.dram_tensor(f"out_{n}", shape, _mybir.dt.float32, kind="ExternalOutput").ap()
    hybrid_prefix_diffusion_step(nc, ins, outs)
    r = _run(nc, [feed], core_ids=[0])
    return tuple(r.results[0][f"out_{n}"] for n, _ in _OUTS)
```

```python
from contextlib import ExitStack

import concourse.bass as bass
from concourse import mybir

ALU = mybir.AluOpType
ACT = mybir.ActivationFunctionType
F32 = mybir.dt.float32
F32R = mybir.dt.float32r
U32 = mybir.dt.uint32
AX_X = mybir.AxisListType.X

P = 128
D = 1024
DEPTH = 2
LAT, CTX = 512, 128
NT = (LAT + CTX) // P
TOK = LAT + CTX
KC = D // P
HEADS, KV, HD = 8, 2, 64
ATT, KVW = HEADS * HD, KV * HD
HY, GM = 256, 256
GH = 4
TAPS = 3
EMB, FH = 33, 64
EXPERTS = 16
CAP_L, CAP_C = 2 * LAT // EXPERTS, 2 * CTX // EXPERTS
CAP = CAP_L + CAP_C
EPS = 1e-6
SLOTS = 3
ADA = 6
ROUNDS = ADA // SLOTS + 1
PAIRS = EXPERTS // 2
HALF = KC // 2
ASPLIT = 4
SPLIT0 = HALF - 1
MATS = 3 * EXPERTS
AHEAD = 4 * KC
SCALE = HD ** -0.5
NEG = -1e30
TWO_PI_HI, TWO_PI_LO = 6.28125, 6.283185307179586 - 6.28125
ROUND = 1.5 * 2.0 ** 23
PI_IN = 3.1415925

G1, G2, GO, CW, CB, GB, SK, FB1, FB2, FQ, AB, NPRM = 0, 8, 16, 24, 42, 48, 52, 60, 61, 62, 63, 96
C_ID, C_MASK, C_COS, C_SIN, NCST = 0, 128, 640, 896, 1024

V_LAYER, V_LAST = 120, 5
A_LAYER = 13


def hold(eng, s, value, done):
    value = eng.to_reg(value)
    eng.wait_ge(done, 32)
    eng.wait_ge(s, value)


def w3_at(e):
    return e * 3 + 1


def w1_next_at(e):
    return e * 3 + 2


def w2_at(e):
    return MATS - 1 if isinstance(e, int) and e == EXPERTS - 1 else e * 3 + 3


class Chain:

    def __init__(self, eng, sem, name, base, expect):
        self.eng, self.sem, self.base, self.n, self.expect, self.name = eng, sem, base, 0, expect, name

    def held(self, ins, done):
        self.n += 1
        ins.then_inc(self.sem, 1)
        hold(self.eng, self.sem, self.base + self.n, done)

    def __call__(self, ins):
        self.n += 1
        ins.then_inc(self.sem, 1)
        self.eng.wait_ge(self.sem, self.base + self.n)

    def close(self):
        assert self.n == self.expect, f"{self.name} has {self.n} links"


def hybrid_prefix_diffusion_step(nc, i, o):
    x_res = nc.dram_tensor("x_res", [TOK, D], F32).ap()
    xn_dram = nc.dram_tensor("xn_dram", [TOK, D], F32).ap()

    with ExitStack() as ctx:
        def sb(name, shape, dt=F32):
            return ctx.enter_context(nc.sbuf_tensor(name, shape, dt))

        def sb_twice(name, shape):
            with nc.sbuf_tensor(name, shape, F32) as plain:
                pass
            return plain, sb(name + "_r", shape, F32R)

        def sem(name):
            return ctx.enter_context(nc.semaphore(name))

        bank = [ctx.enter_context(nc.psum_tensor(f"bank{n}", [P, 512], F32)) for n in range(8)]
        ring, ring_r = sb_twice("ring", [P, SLOTS, KC * D])
        slot = [ring[:, s, :].rearrange("p (c n) -> p c n", c=KC) for s in range(SLOTS)]
        slot_r = [ring_r[:, s, :].rearrange("p (c n) -> p c n", c=KC) for s in range(SLOTS)]
        dft = ring[:, 2, :]
        dftc = dft[:, 3840:5888].rearrange("p (a k) -> p a k", a=4)
        dfts = dft[:, 5888:7936].rearrange("p (a k) -> p a k", a=4)
        dftcx, dftsx = dft[:, 7936:8064], dft[:, 8064:8192]
        hy = ring[:, 0, :]
        mixed_high = ring_r[:, 0, 0:KC * TOK].rearrange("p (c t) -> p c t", c=KC)
        arena_h, arena_hr = sb_twice("arena_h", [P, KC * TOK])
        hT = arena_h[:, :].rearrange("p (c t) -> p c t", c=KC)
        h_low = arena_hr[:, :].rearrange("p (c t) -> p c t", c=KC)
        filc = arena_h[:, 0:2048].rearrange("p (a k) -> p a k", a=4)
        fils = arena_h[:, 2048:4096].rearrange("p (a k) -> p a k", a=4)
        filcx, filsx = arena_h[:, 4096:4224], arena_h[:, 4224:4352]
        feats = arena_h[0:EMB, 4352:4992]
        final_g = arena_h[:, 0:D]
        arena_z, arena_zr = sb_twice("arena_z", [P, NT * 1280])
        zt = arena_z[:, :].rearrange("p (t n) -> p t n", t=NT)
        win = arena_z[:, 0:1280].rearrange("p (t n) -> p t n", t=NT)
        fsum = arena_z[:, 1280:2560].rearrange("p (t n) -> p t n", t=NT)
        fdif = arena_z[:, 2560:3840].rearrange("p (t n) -> p t n", t=NT)
        hfw, hbw = arena_z[:, 3840:4096], arena_z[:, 4096:4352]
        pre, turns, hid = (arena_z[0:FH, a:a + TOK] for a in (4352, 4992, 5632))
        fw1, fw2 = arena_z[0:EMB, 6272:6336], arena_z[0:FH, 6336:6400]
        xe = [arena_z[0:CAP, a:a + D] for a in (0, 1024)]
        ye = [arena_z[0:CAP, a:a + D] for a in (2048, 3072)]
        he = arena_z[0:CAP, 4096:5120]
        heT = [arena_zr[:, a:a + KC * CAP].rearrange("p (c t) -> p c t", c=KC) for a in (5120, 5760)]
        arena_u, arena_ur = sb_twice("arena_u", [P, 6400])
        mrow = [arena_u[0:5, a:a + D] for a in (1024, 2048)]
        ahigh = [arena_ur[:, a:a + D] for a in (0, 3072, 4096, 5120)]
        junk = arena_u[:, 5120:6144]
        h_high = arena_ur[:, 0:2560].rearrange("p (c t) -> p c t", c=4)
        h_high_z = arena_zr[:, :].rearrange("p (t n) -> p t n", t=NT)
        zhT = arena_u[:, 2560:6400].rearrange("p (m t) -> p m t", m=6)
        x0c = hy[:, 0:1280].rearrange("p (m t) -> p m t", m=2)
        spec = [hy[:, 1280 * a:1280 * a + 1280] for a in range(5)]
        uT = spec[1].rearrange("p (m t) -> p m t", m=2)
        utok = spec[2].rearrange("p (t n) -> p t n", t=NT)
        cvt = spec[3][:, 0:TOK]
        prod = [spec[n].rearrange("p (j n) -> p j n", j=NT) for n in (1, 2, 3, 4)]
        x0tok = hy[:, 6400:7680].rearrange("p (t n) -> p t n", t=NT)
        qT = [a[:, 0:2560].rearrange("p (i t) -> p i t", i=4) for a in (arena_u, arena_h)]
        kT = arena_u[:, 2560:3328]
        sbuf_s = [arena_u[:, 3328 + 512 * n:3840 + 512 * n] for n in range(2)]
        prob = [arena_u[:, 4352 + 512 * n:4864 + 512 * n] for n in range(2)]
        probT = [arena_u[:, 5376 + 512 * n:5888 + 512 * n] for n in range(2)]
        xn = arena_u[:, 0:5120].rearrange("p (t n) -> p t n", t=NT)
        xeT = [[arena_ur[:, a:a + KC * CAP].rearrange("p (c t) -> p c t", c=KC) for a in (b, b + 640)]
               for b in (0, 1280)]
        high = [arena_hr[:, c * D:(c + 1) * D] if c < 5 else arena_ur[:, 2560 + (c - 5) * D:2560 + (c - 4) * D]
                for c in range(KC)]
        spectrum = sb("spectrum", [P, 2, NT, HY])
        sflat = spectrum[:, :, :, :].rearrange("p a t n -> p (a t n)")
        g2e, s2e, xt = (sflat[:, a:a + KC * CAP].rearrange("p (c t) -> p c t", c=KC) for a in (640, 1280, 1920))
        affT = [sflat[0:EXPERTS, a:a + TOK] for a in (0, 640)]
        gate1 = sb("gate1", [P, 2, D])
        gate2 = sb("gate2", [CAP, D])
        cst = sb("cst", [P, NCST])
        ident = cst[:, C_ID:C_ID + P]
        mask = cst[:, C_MASK:C_MASK + 512]
        cos_t = cst[:, C_COS:C_COS + 256].rearrange("p (t n) -> p t n", t=4)
        sin_t = cst[:, C_SIN:C_SIN + 128].rearrange("p (t h n) -> p t h n", t=4, h=2)
        sel = sb("sel", [5, 2 * P + CAP + 2])
        join = sel[:, 2 * P + CAP:]
        prm = sb("prm", [P, NPRM])
        wsT = sb("wsT", [P, GH, P])
        rw = sb("rw", [P, KC, EXPERTS])
        ck, cv = sb("ck", [P, KVW]), sb("cv", [P, KVW])
        rtmp = sb("rtmp", [P, 640])
        jk = sb("jk", [P, 512])
        dbias = rtmp[0:1, 0:HY]
        fw3 = jk[0:FH, :]
        cvec = sb("cvec", [P, 2, KC])
        cs_r = sb("cs_r", [P, KC, 4], F32R)
        cs = sb("cs", [P, KC, 4])
        mod = sb("mod", [P, 4, KC, 2])
        nsink = sb("nsink", [P, HEADS])
        ssum, sms, srec, sroot, stmp = (sb(n, [P, 15]) for n in ("ssum", "sms", "srec", "sroot", "stmp"))
        negmax, rsum, esink, denom = (sb(n, [P, NT, HEADS]) for n in ("negmax", "rsum", "esink", "denom"))
        aff = sb("aff", [P, NT, EXPERTS])
        anm, asum, arec = (sb(n, [P, NT]) for n in ("anm", "asum", "arec"))
        topv = sb("topv", [EXPERTS, CAP])
        topi = sb("topi", [EXPERTS, CAP], U32)
        topf = sb("topf", [EXPERTS, CAP])
        idxT = sb("idxT", [CAP, EXPERTS + 1], U32)
        gateT = sb("gateT", [CAP, EXPERTS])
        icur = [sb(f"icur{n}", [CAP, 1], U32) for n in range(2)]
        iscat = [sb(f"iscat{n}", [CAP, 1], U32) for n in range(2)]

        arrived = [sem(f"arrived{s}") for s in range(SLOTS)]
        ada_in = [[sem(f"ada_in{n}_{h}") for h in range(2)] for n in range(SLOTS)]
        ahigh_ready = sem("ahigh_ready")
        alow_ready = sem("alow_ready")
        achunk_used = sem("achunk_used")
        used = [sem(f"used{s}") for s in range(SLOTS)]
        dft_in = sem("dft_in")
        const_in = sem("const_in")
        c_in = sem("c_in")
        x_copied = sem("x_copied")
        cs_done = sem("cs_done")
        cs_zero = sem("cs_zero")
        cs_parts = sem("cs_parts")
        prm_in = sem("prm_in")
        fil_in = sem("fil_in")
        bias_in = sem("bias_in")
        mrow_done = sem("mrow_done")
        mod_mm = sem("mod_mm")
        mod_out = sem("mod_out")
        f_mm = sem("f_mm")
        f_pre = sem("f_pre")
        f_sin = sem("f_sin")
        f3_mm = sem("f3_mm")
        f3_out = sem("f3_out")
        spec_mm = sem("spec_mm")
        spec_out = sem("spec_out")
        x_in = sem("x_in")
        sq1 = sem("sq1")
        rec1 = sem("rec1")
        root1 = sem("root1")
        xn1 = sem("xn1")
        t1_mm = sem("t1_mm")
        h1_v, h1_a = sem("h1_v"), sem("h1_a")
        h_hi, h_lo = sem("h_hi"), sem("h_lo")
        w_hi = sem("w_hi")
        w_lo = [sem("w_lo0"), sem("w_lo1")]
        z_mm = sem("z_mm")
        z_v, z_a = sem("z_v"), sem("z_a")
        kv_out = sem("kv_out")
        gm_mm = sem("gm_mm")
        gm_out = sem("gm_out")
        gm_sq = sem("gm_sq")
        u_done = sem("u_done")
        ut_mm = sem("ut_mm")
        ut_out = sem("ut_out")
        fwd_mm = sem("fwd_mm")
        y_done = sem("y_done")
        inv_mm = sem("inv_mm")
        yh_done = sem("yh_done")
        ysq_done = sem("ysq_done")
        x0_done = sem("x0_done")
        x0_mm = sem("x0_mm")
        x0_out = sem("x0_out")
        rope_done = sem("rope_done")
        q_zero = sem("q_zero")
        qk_mm = sem("qk_mm")
        qk_a = sem("qk_a")
        sc_mm = sem("sc_mm")
        sc_out = sem("sc_out")
        p_done = sem("p_done")
        pt_mm = sem("pt_mm")
        pt_v, pt_a = sem("pt_v"), sem("pt_a")
        pv_mm = sem("pv_mm")
        es_in = sem("es_in")
        es_out = sem("es_out")
        a_done = sem("a_done")
        a_sq = sem("a_sq")
        mrec = sem("mrec")
        mroot = sem("mroot")
        mixn = sem("mixn")
        mx_mm = sem("mx_mm")
        mx_out = sem("mx_out")
        wo_hi, wo_lo = sem("wo_hi"), sem("wo_lo")
        m_hi, m_lo = sem("m_hi"), sem("m_lo")
        xr_in = [sem(f"xr_in{t}") for t in range(NT)]
        wo_mm = sem("wo_mm")
        x1_done = sem("x1_done")
        sq2 = sem("sq2")
        rec2 = sem("rec2")
        root2 = sem("root2")
        xn2 = sem("xn2")
        x1_out = sem("x1_out")
        xn_out = sem("xn_out")
        t2_mm = sem("t2_mm")
        h2_v, h2_a = sem("h2_v"), sem("h2_a")
        lg_mm = sem("lg_mm")
        anm_done = sem("anm_done")
        aexp = sem("aexp")
        aff_done = sem("aff_done")
        affT_mm = sem("affT_mm")
        affT_out = sem("affT_out")
        top_done = sem("top_done")
        top_mm = sem("top_mm")
        top_out = sem("top_out")
        half_in = [[sem(f"half_in{n}_{h}") for h in range(2)] for n in range(SLOTS)]
        high_ready = sem("high_ready")
        low_ready = sem("low_ready")
        first_low = sem("first_low")
        chunk_used = sem("chunk_used")
        icur_done = sem("icur_done")
        xe_in = [sem("xe_in0"), sem("xe_in1")]
        xeT_mm = sem("xeT_mm")
        xt_scaled = sem("xt_scaled")
        xt_done = sem("xt_done")
        xh_done = sem("xh_done")
        xeT_out = sem("xeT_out")
        silu = sem("silu")
        he_done = sem("he_done")
        heT_mm = sem("heT_mm")
        hh_done = sem("hh_done")
        heT_out = sem("heT_out")
        ye_done = sem("ye_done")
        scattered = sem("scattered")
        rows_free = sem("rows_free")
        g_in = sem("g_in")
        fin_in = [sem(f"fin_in{t}") for t in range(NT)]
        fsq, frec, froot, y_out_done = sem("fsq"), sem("frec"), sem("froot"), sem("y_out_done")
        y_out = sem("y_out")
        v_link, v_flink, a_link = sem("v_link"), sem("v_flink"), sem("a_link")

        proj = ([("q", t, "v") for t in range(NT)] + [("kv", t, "a") for t in range(NT)]
                + [("zh", (m, half), "v") for m in range(6) for half in range(2)]
                + [("zg", t, "a") for t in range(NT)])
        NP_ = len(proj)
        Z_V, Z_A = (sum(p[2] == e for p in proj) for e in "va")

        def taken(n):
            e = proj[n][2]
            return (z_v if e == "v" else z_a), (Z_V if e == "v" else Z_A), sum(p[2] == e for p in proj[:n + 1])

        def multiplied(n):
            if n in (LAST_SLOT0, NP_ - 1):
                return used[0 if n == LAST_SLOT0 else 1], ROUNDS, 3
            return z_mm, NP_ - 2, n + 1 - (n > LAST_SLOT0)

        def proj_at(kind, t):
            return proj.index(next(p for p in proj if p[:2] == (kind, t)))

        LAST_SLOT0 = proj_at("zh", (1, 1))
        GROUPS = [0, NT, LAST_SLOT0 + 1, proj_at("zg", 0)]

        def w_group(w, g, c):
            cols = slice((g % 2) * 512, (g % 2) * 512 + 512)
            return w[g // 2][:, c:c + 2, cols], slot_r[2][:, c:c + 2, cols]

        def token_half(h):
            return (0, 3) if h == 0 else (3, NT)

        def high_of(c, a, b):
            if c < 4:
                return h_high[:, c, a * P:b * P]
            return h_high_z[:, a:b, 768 + (c - 4) * P:768 + (c - 3) * P]

        att = [(b, h) for b in range(NT) for h in range(HEADS)]

        def keys(b):
            if b == NT - 1:
                return [(LAT, P)], P
            blocks = [((b - 1) * P, P)] if b else []
            blocks += [(TOK, P), (b * P, 2 * P if b < 3 else P)]
            return blocks, 0 if b else P

        def values(b):
            if b == NT - 1:
                return [zt[:, b, 640:768]]
            v = [zt[:, b - 1, 640:768]] if b else []
            v += [cv[:, :], zt[:, b, 640:768]]
            return v + ([zt[:, b + 1, 640:768]] if b < 3 else [])

        MOD = [(0, "col"), (1, "col"), (2, "lat"), (2, "ctx"), (3, "col"), (4, "col"), (5, "cap")]
        spread = [1, 2, 4, 5, 6, 7]
        FWD = [6, 7, 0, 1, 2]

        def width(b):
            return sum(n for _, n in keys(b)[0])

        def chunks(l, m, c):
            return l * (MATS * KC) + m * KC + c + 1

        block = ctx.enter_context(nc.Block())

        @block.sync
        def _(sp):
            sp.dma_start(cvec[:, 0, :], i["c"].rearrange("a (p k) -> (a p) k", k=KC)).then_inc(c_in, 16)
            sp.dma_start(cvec[:, 1, :], i["c_ctx"].rearrange("(p k) -> p k", k=KC)).then_inc(c_in, 16)
            sp.dma_start(sel[:, :], i["sel"]).then_inc(const_in, 16)
            sp.dma_start(cst[:, :], i["consts"]).then_inc(const_in, 16)
            with sp.Fori(0, DEPTH) as l:
                def layer(name):
                    return i[name][bass.ds(l, 1)]

                def small_loads():
                    sp.wait_ge(chunk_used, AHEAD + l * (MATS * KC))
                    for j in (2, 5):
                        sp.dma_start(mrow[j % 2][4:5, :], layer("ada_b")[:, j * D:(j + 1) * D]).then_inc(bias_in, 16)
                    sp.dma_start(prm[:, :], layer("params").rearrange("a p n -> (a p) n")).then_inc(prm_in, 16)
                    sp.dma_start(fw1, layer("hy_f_w1").rearrange("a p n -> (a p) n")).then_inc(prm_in, 16)
                    sp.dma_start(fw2, layer("hy_f_w2").rearrange("a p n -> (a p) n")).then_inc(prm_in, 16)
                    sp.dma_start(fw3, layer("hy_f_w3").rearrange("a p n -> (a p) n")).then_inc(prm_in, 16)
                    sp.dma_start(feats, i["feats"]).then_inc(prm_in, 16)
                    sp.dma_start(dbias, layer("hy_bias")).then_inc(prm_in, 16)
                    sp.dma_start(wsT[:, :, :], layer("ws_t").rearrange("a p (h n) -> (a p) h n", h=GH)).then_inc(prm_in, 16)
                    sp.dma_start(rw[:, :, :], layer("router_w").rearrange("a (p c) n -> (a p) c n", p=P)).then_inc(prm_in, 16)
                    sp.dma_start(ck[:, :], i["cache_k"][0, bass.ds(l, 1)].rearrange("a p h d -> (a p) (h d)")).then_inc(prm_in, 16)
                    sp.dma_start(cv[:, :], i["cache_v"][0, bass.ds(l, 1)].rearrange("a p h d -> (a p) (h d)")).then_inc(prm_in, 16)

                def filter_loads():
                    sp.dma_start(win, i["window"].rearrange("(t p) n -> p t n", p=P)).then_inc(fil_in, 16)
                    sp.dma_start(filc, i["fil_cos"].rearrange("(a p) k -> p a k", p=P)).then_inc(fil_in, 16)
                    sp.dma_start(fils, i["fil_sin"].rearrange("(a p) k -> p a k", p=P)).then_inc(fil_in, 16)
                    sp.dma_start(filcx, i["filx_cos"]).then_inc(fil_in, 16)
                    sp.dma_start(filsx, i["filx_sin"]).then_inc(fil_in, 16)

                for r in range(2):
                    for s in range(SLOTS):
                        j = SLOTS * r + s
                        if j == 2:
                            small_loads()
                        for h in range(2):
                            if r == 0:
                                sp.wait_ge(chunk_used, l * (MATS * KC) + AHEAD - (3, 1, 0)[s] * KC)
                            elif h == 0:
                                sp.wait_ge(achunk_used, ASPLIT + (l * ADA + s) * ASPLIT + 1)
                            else:
                                sp.wait_ge(used[s], l * ROUNDS + 1)
                            sp.dma_start(slot[s][:, h * HALF:(h + 1) * HALF, :],
                                         i["ada_w"][bass.ds(l, 1), :, j * D:(j + 1) * D]
                                         .rearrange("a (p c) n -> (a p) c n", p=P)[:, h * HALF:(h + 1) * HALF, :])\
                                .then_inc(ada_in[s][h], 16)
                        if j == 2:
                            filter_loads()
                for s in range(2):
                    sp.wait_ge(used[s], l * ROUNDS + 2)
                    if s:
                        sp.wait_ge(x_in, l * 16 + 16)
                    sp.dma_start(slot[s], i["w_in"][bass.ds(l, 1), :, s * D:(s + 1) * D]
                                 .rearrange("a (p c) n -> (a p) c n", p=P)).then_inc(arrived[s], 16)
                sp.wait_ge(used[1], l * ROUNDS + 3)
                sp.dma_start(dftc, i["dft_cos"].rearrange("(a p) k -> p a k", p=P)).then_inc(dft_in, 16)
                sp.dma_start(dfts, i["dft_sin"].rearrange("(a p) k -> p a k", p=P)).then_inc(dft_in, 16)
                sp.dma_start(dftcx, i["dftx_cos"]).then_inc(dft_in, 16)
                sp.dma_start(dftsx, i["dftx_sin"]).then_inc(dft_in, 16)
                sp.wait_ge(inv_mm, l + 1)
                sp.dma_start(slot[2], i["w_out"][bass.ds(l, 1)]
                             .rearrange("a (c p) n -> (a p) c n", p=P)).then_inc(arrived[2], 16)

                def fill(s, name, e, before):
                    for h in range(2):
                        if s == 2 and before is None and h:
                            for u in range(2):
                                sp.wait_ge(xe_in[u], l * (PAIRS * 16) + 16)
                        elif before is None:
                            sp.wait_ge(used[2], l * ROUNDS + 3)
                        else:
                            sp.wait_ge(chunk_used, AHEAD + chunks(l, before, h * HALF + HALF - 1))
                        sp.dma_start(slot[s][:, h * HALF:(h + 1) * HALF, :],
                                     i[name][bass.ds(l, 1), bass.ds(e, 1)]
                                     .rearrange("a b (p c) n -> (a b p) c n", p=P)[:, h * HALF:(h + 1) * HALF, :])\
                            .then_inc(half_in[s][h], 16)

                fill(0, "exp_w1", 0, None)
                sp.wait_ge(xn_out, l * 80 + 80)
                fill(1, "exp_w3", 0, None)
                fill(2, "exp_w2", 0, None)
                fill(0, "exp_w1", 1, 0)
                fill(1, "exp_w3", 1, w3_at(0))
                with sp.Fori(1, EXPERTS - 1) as e:
                    fill(0, "exp_w1", e + 1, w1_next_at(e) - 3)
                    fill(2, "exp_w2", e, w2_at(e) - 3)
                    fill(1, "exp_w3", e + 1, w3_at(e))
                fill(2, "exp_w2", EXPERTS - 1, w2_at(EXPERTS - 2))

            sp.wait_ge(chunk_used, AHEAD + DEPTH * MATS * KC)
            sp.dma_start(final_g, i["final_g"].rearrange("(a d) -> a d", a=1).broadcast_to([P, D])).then_inc(g_in, 16)
            sp.wait_ge(scattered, DEPTH * EXPERTS * 16)
            for t in range(NT):
                sp.dma_start(zt[:, t, 0:D], x_res[t * P:(t + 1) * P]).then_inc(fin_in[t], 16)
            for t in range(NT):
                out = o["y_sample"][0, t * P:(t + 1) * P] if t < 4 else o["y_prompt"][0]
                sp.wait_ge(y_out_done, t + 1)
                sp.dma_start(out, zt[:, t, 0:D]).then_inc(y_out, 16)
            sp.wait_ge(y_out, 16 * NT)

        @block.gpsimd
        def _(pool):
            pool.sem_inc(rows_free, 2)
            pool.wait_ge(ada_in[2][0], 32)
            pool.dma_start(x_res[0:LAT], i["x_sample"].rearrange("a t d -> (a t) d")).then_inc(x_copied, 16)
            pool.dma_start(x_res[LAT:TOK], i["x_prompt"].rearrange("a t d -> (a t) d")).then_inc(x_copied, 16)

            with pool.Fori(0, DEPTH) as l:
                def layer(name):
                    return i[name][bass.ds(l, 1)]

                hold(pool, spec_mm, l * 5 + 5, const_in)
                pool.wait_ge(x_copied, 32)
                pool.dma_start(zt[:, :, 0:D], x_res.rearrange("(t p) d -> p t d", p=P)).then_inc(x_in, 16)
                for g in range(2):
                    for c in range(0, KC, 2):
                        pool.wait_ge(w_hi, l * 16 + g * 4 + c // 2 + 1)
                        w, high_w = w_group(slot, g, c)
                        pool.tensor_tensor(w_group(slot_r, g, c)[0], w, high_w, ALU.subtract).then_inc(w_lo[0], 1)
                hold(pool, used[1], l * ROUNDS + 3, const_in)
                pool.memset(qT[0][HD:P, :, :], 0.0).then_inc(q_zero, 1)
                pool.memset(qT[1][0:HD, :, :], 0.0).then_inc(q_zero, 1)
                s, per, n = taken(proj_at("kv", NT - 1))
                hold(pool, s, l * per + n, const_in)
                for name, a in (("new_k", 512), ("new_v", 640)):
                    pool.dma_start(o[name][0, bass.ds(l, 1)].rearrange("a p h d -> (a p) (h d)"),
                                   zt[:, NT - 1, a:a + KVW]).then_inc(kv_out, 16)
                for t in range(NT):
                    hold(pool, mx_mm, l * NT + t + 1, const_in)
                    if t == NT - 1:
                        hold(pool, kv_out, l * 32 + 32, const_in)
                    pool.dma_start(zt[:, t, 0:D], x_res[t * P:(t + 1) * P]).then_inc(xr_in[t], 16)
                for t in range(NT):
                    hold(pool, x1_done, l * NT + t + 1, const_in)
                    pool.dma_start(x_res[t * P:(t + 1) * P], zt[:, t, 0:D]).then_inc(x1_out, 16)
                    hold(pool, xn2, l * NT + t + 1, const_in)
                    pool.dma_start(xn_dram[t * P:(t + 1) * P], xn[:, t, :]).then_inc(xn_out, 16)
                hold(pool, x1_out, l * 80 + 80, const_in)
                hold(pool, xn_out, l * 80 + 80, const_in)

                def gather(u):
                    pool.indirect_dma_start(xe[u], None, xn_dram,
                                            bass.IndirectOffsetOnAxis(ap=icur[u][:, :], axis=0))\
                        .then_inc(xe_in[u], 16)

                def scatter(u, e):
                    hold(pool, ye_done, e + 1, const_in)
                    pool.indirect_dma_start(x_res, bass.IndirectOffsetOnAxis(ap=iscat[u][:, :], axis=0),
                                            ye[u], None, compute_op=ALU.add).then_inc(scattered, 16)
                    pool.wait_ge(scattered, e * 16 + 16)
                    pool.sem_inc(rows_free, 1)

                def first_rest(c):
                    pool.wait_ge(high_ready, chunks(l, 0, c))
                    pool.tensor_tensor(slot_r[0][:, c, :], slot[0][:, c, :], high[c], ALU.subtract)\
                        .then_inc(first_low, 1)

                for c in range(KC - 2):
                    first_rest(c)
                hold(pool, icur_done, l * (EXPERTS + 1) + 2, const_in)
                gather(0)
                gather(1)
                first_rest(KC - 2)
                first_rest(KC - 1)
                with pool.Fori(0, PAIRS - 1) as k:
                    for u in range(2):
                        e = k * 2 + u
                        hold(pool, icur_done, l * (EXPERTS + 1) + e + 3, const_in)
                        hold(pool, xeT_mm, l * EXPERTS + e + 1, const_in)
                        gather(u)
                        scatter(u, l * EXPERTS + e)
                scatter(0, l * EXPERTS + EXPERTS - 2)
                scatter(1, l * EXPERTS + EXPERTS - 1)

            pool.wait_ge(kv_out, 32 * DEPTH)

        @block.tensor
        def _(pe):
            pe.sem_inc(chunk_used, AHEAD)
            pe.sem_inc(achunk_used, ASPLIT)
            pe.wait_ge(const_in, 32)
            pe.wait_ge(cs_parts, 2)

            with pe.Fori(0, DEPTH) as l:
                def ada(j, between={}):
                    if j >= 2:
                        pe.wait_ge(mrow_done, l * ADA + j - 1)
                    out = [bank[2 * (j % 2) + n][0:4, :] for n in range(2)]
                    for c in range(KC):
                        k = c - SPLIT0
                        if c % HALF == 0:
                            pe.wait_ge(ada_in[j % SLOTS][c // HALF], l * 32 + 16 * (j // SLOTS + 1))
                        if 0 <= k < ASPLIT:
                            pe.wait_ge(alow_ready, (l * ADA + j) * ASPLIT + k + 1)
                            parts = ((cs_r, ahigh[k]), (cs_r, slot_r[j % SLOTS][:, c, :]))
                        else:
                            parts = ((cs, slot[j % SLOTS][:, c, :]),)
                        for part, (x, w) in enumerate(parts):
                            for n in range(2):
                                mm = pe.matmul(out[n], x[:, c, :], w[:, n * 512:(n + 1) * 512],
                                               start=(c == 0 and part == 0), stop=(c == KC - 1))
                        if 0 <= k < ASPLIT:
                            mm.then_inc(achunk_used, 1)
                        if c == KC - 1:
                            mm.then_inc(used[j % SLOTS], 1)
                        for step, n in between.get(c, []):
                            step(n)

                def mod_step(q):
                    j, what = MOD[q]
                    if q:
                        pe.wait_ge(mod_out, l * len(MOD) + q)
                    if j == 0:
                        pe.wait_ge(bias_in, l * 32 + 32)
                    hold(pe, mrow_done, l * ADA + j + 1, const_in)
                    if what == "col":
                        for k in range(KC):
                            mm = pe.matmul(bank[4][:, 2 * k:2 * k + 2], mrow[j % 2][:, k:D:KC], join,
                                           start=True, stop=True)
                    else:
                        a, m = {"lat": (0, P), "ctx": (P, P), "cap": (2 * P, CAP)}[what]
                        for n in range(2):
                            mm = pe.matmul(bank[4 + n][0:m, :], sel[:, a:a + m],
                                           mrow[j % 2][:, n * 512:(n + 1) * 512], start=True, stop=True)
                    mm.then_inc(mod_mm, 1)

                def filter_layer(n):
                    if n == 0:
                        hold(pe, prm_in, l * 160 + 160, const_in)
                    else:
                        hold(pe, f_sin, l * 2 + 1, const_in)
                    w, x = (fw1, feats) if n == 0 else (fw2, hid)
                    pe.matmul(bank[6][0:FH, :], w, x[:, 0:LAT], start=True, stop=True)
                    pe.matmul(bank[7][0:FH, 0:CTX], w, x[:, LAT:TOK], start=True, stop=True).then_inc(f_mm, 1)

                def filter_taps(t):
                    if t == 0:
                        pe.wait_ge(f_sin, l * 2 + 2)
                    if t >= 2:
                        pe.wait_ge(f3_out, l * NT + t - 1)
                    pe.matmul(bank[6 + t % 2][:, :], hid[:, t * P:(t + 1) * P], fw3, start=True, stop=True)\
                        .then_inc(f3_mm, 1)

                def filter_spectrum():
                    pe.wait_ge(f3_out, l * NT + NT)
                    pe.wait_ge(fil_in, l * 80 + 80)
                    for n in range(4):
                        if n >= 2:
                            pe.wait_ge(spec_out, l * 5 + n - 1)
                        table, taps = (filc, fsum) if n < 2 else (fils, fdif)
                        for j in range(2):
                            jj = 2 * (n % 2) + j
                            for a in range(4):
                                mm = pe.matmul(bank[6 + n % 2][:, j * HY:(j + 1) * HY],
                                               table[:, a, jj * P:(jj + 1) * P], taps[:, a, :],
                                               start=(a == 0), stop=(a == 3))
                        mm.then_inc(spec_mm, 1)
                    pe.wait_ge(spec_out, l * 5 + 3)
                    pe.matmul(bank[6][:, 0:HY], filcx, fsum[:, 4, :], start=True, stop=True)
                    pe.matmul(bank[6][:, HY:2 * HY], filsx, fdif[:, 4, :], start=True, stop=True).then_inc(spec_mm, 1)

                ada(0)
                filter_layer(0)
                ada(1, {6: [(filter_layer, 1)]})
                ada(2, {1: [(mod_step, 0)], 5: [(filter_taps, 0), (filter_taps, 1)]})
                ada(3, {1: [(mod_step, 1)], 5: [(filter_taps, 2), (filter_taps, 3)]})
                ada(4, {1: [(mod_step, 2)], 2: [(mod_step, 3)], 5: [(filter_taps, 4)]})
                filter_spectrum()
                ada(5, {1: [(mod_step, 4)], 5: [(mod_step, 5)]})
                mod_step(6)

                pe.wait_ge(mod_out, l * len(MOD) + len(MOD))
                pe.wait_ge(spec_out, l * 5 + 5)
                pe.wait_ge(mrow_done, l * ADA + ADA)
                for t in range(NT):
                    pe.wait_ge(xn1, l * NT + t + 1)
                    if t == 4:
                        pe.wait_ge(h1_v, l * NT + 1)
                        pe.wait_ge(h1_a, l * NT + 1)
                    for k in range(KC):
                        mm = pe.transpose(bank[2 * (t % 4) + k // 4][:, (k % 4) * P:(k % 4 + 1) * P],
                                          zt[:, t, k:D:KC], ident)
                    mm.then_inc(t1_mm, 1)

                for n, (kind, t, _) in enumerate(proj):
                    if n >= 8:
                        s, per, v = taken(n - 8)
                        pe.wait_ge(s, l * per + v)
                    out = bank[(n + 2) % 8]
                    g = max(x for x in range(4) if GROUPS[x] <= n)
                    if n < NT:
                        pe.wait_ge(h_lo, l * NT + n + 1)
                    for c in range(KC):
                        if n in GROUPS and c % 2 == 0:
                            pe.wait_ge(w_lo[g // 2], l * 8 + g % 2 * 4 + c // 2 + 1)
                        for part in range(3):
                            if kind == "zh":
                                m, half = t
                                a, b = token_half(half)
                                x = h_low[:, c, a * P:b * P] if part == 1 else high_of(c, a, b)
                                col = 768 + m * P if m < 2 else (m - 2) * P
                                w = (slot_r[g // 2] if part == 2 else slot_r[2])[:, c, col:col + P]
                                pe_out, lhsT, rhs = out[:, 0:(b - a) * P], w, x
                            else:
                                col, m = {"q": (0, 512), "kv": (512, 256), "zg": (512, 512)}[kind]
                                x = h_low[:, c, t * P:(t + 1) * P] if part == 1 else \
                                    high_of(c, t, t + 1) if c < 4 else h_high_z[:, t, 768 + (c - 4) * P:768 + (c - 3) * P]
                                w = (slot_r[g // 2] if part == 2 else slot_r[2])[:, c, col:col + m]
                                if kind == "q":
                                    w = w.rearrange("p (g i d) -> p i g d", g=KV, i=4)
                                pe_out, lhsT, rhs = out[:, 0:m], x, w
                            mm = pe.matmul(pe_out, lhsT, rhs, start=(c == 0 and part == 0),
                                           stop=(c == KC - 1 and part == 2))
                    mm.then_inc(multiplied(n)[0], 1)

                for e in "av":
                    s, per, v = taken(max(n for n in range(NP_) if proj[n][2] == e))
                    pe.wait_ge(s, l * per + v)
                pe.wait_ge(prm_in, l * 160 + 160)
                for t in range(NT):
                    for h in range(GH):
                        mm = pe.matmul(bank[t // 2][:, (t % 2) * GM + h * 64:(t % 2) * GM + h * 64 + 64],
                                       wsT[:, h, :], zt[:, t, 1024 + h * 64:1088 + h * 64], start=True, stop=True)
                    if t % 2 or t == NT - 1:
                        mm.then_inc(gm_mm, 1)

                pe.wait_ge(x0_done, l + 1)
                for t in range(NT):
                    for m in range(2):
                        b, a = ((6, 0), (7, 0), (5, GM))[t // 2]
                        mm = pe.transpose(bank[b][:, a + (t % 2) * HY + m * P:a + (t % 2) * HY + (m + 1) * P],
                                          x0c[:, m, t * P:(t + 1) * P], ident)
                mm.then_inc(x0_mm, 1)
                pe.wait_ge(u_done, l + 1)
                pe.wait_ge(x0_out, l + 1)
                for t in range(NT):
                    for m in range(2):
                        mm = pe.transpose(bank[3 + t // 2][:, (t % 2) * HY + m * P:(t % 2) * HY + (m + 1) * P],
                                          uT[:, m, t * P:(t + 1) * P], ident)
                    if t % 2 or t == NT - 1:
                        mm.then_inc(ut_mm, 1)
                pe.wait_ge(dft_in, l * 64 + 64)
                pe.wait_ge(ut_out, l * 3 + 3)
                for n in range(4):
                    if n == 2:
                        pe.wait_ge(gm_out, l * 3 + 3)
                    table = dftc if n < 2 else dfts
                    for j in range(2):
                        jj = 2 * (n % 2) + j
                        for a in range(4):
                            pe.matmul(bank[FWD[n]][:, j * HY:(j + 1) * HY], table[:, a, jj * P:(jj + 1) * P],
                                      utok[:, a, :], start=(a == 0), stop=(a == 3))
                pe.matmul(bank[FWD[4]][:, 0:HY], dftcx, utok[:, 4, :], start=True, stop=True)
                pe.matmul(bank[FWD[4]][:, HY:2 * HY], dftsx, utok[:, 4, :], start=True, stop=True).then_inc(fwd_mm, 1)
                qk = [[(zt[:, t, n * P:(n + 1) * P], n) for n in range(4)] for t in range(NT)]
                qk += [[(zt[:, t, 512:640], t) for t in range(4)], [(zt[:, 4, 512:640], 0), (ck[:, :], 1)]]
                for j, blocks in enumerate(qk):
                    if j < 4:
                        pe.wait_ge(rope_done, l * 4 + j + 1)
                    if j >= 3:
                        pe.wait_ge(qk_a, l * 7 + j - 2)
                    for x, n in blocks:
                        mm = pe.transpose(bank[3 + j % 3][:, n * P:(n + 1) * P], x, ident)
                    mm.then_inc(qk_mm, 1)
                pe.wait_ge(qk_a, l * 7 + 7)
                pe.wait_ge(y_done, l + 1)
                for t in range(4):
                    for n in range(8):
                        pe.matmul(bank[3 + t // 2][:, (t % 2) * HY:(t % 2 + 1) * HY],
                                  (dftc if n < 4 else dfts)[:, n % 4, t * P:(t + 1) * P],
                                  prod[0 if n < 4 else 2][:, n % 4, :], start=(n == 0), stop=(n == 7))
                for n in range(2):
                    mm = pe.matmul(bank[5][:, 0:HY], dftsx if n else dftcx, prod[2 * n][:, 4, :],
                                   start=(n == 0), stop=(n == 1))
                mm.then_inc(inv_mm, 1)

                pe.wait_ge(yh_done, l + 1)
                pe.wait_ge(q_zero, l * 2 + 2)
                for n in range(len(att) + 3):
                    if n < len(att):
                        b, h = att[n]
                        if n >= 2:
                            pe.wait_ge(sc_out, l * len(att) + n - 1)
                        at = 0
                        for col, w in keys(b)[0]:
                            mm = pe.matmul(bank[4 + n % 2][:, at:at + w], qT[h // 4][:, h % 4, b * P:(b + 1) * P],
                                           kT[:, col:col + w], start=True, stop=True)
                            at += w
                        mm.then_inc(sc_mm, 1)
                    m = n - 2
                    if 0 <= m < len(att):
                        pe.wait_ge(p_done, l * len(att) + m + 1)
                        if m >= 2:
                            pe.wait_ge(pt_v if m % 2 else pt_a, l * 20 + m // 2)
                        for x in range(width(att[m][0]) // P):
                            mm = pe.transpose(bank[6 + m % 2][:, x * P:(x + 1) * P],
                                              prob[m % 2][:, x * P:(x + 1) * P], ident)
                        mm.then_inc(pt_mm, 1)
                    m = n - 3
                    if 0 <= m < len(att):
                        b, h = att[m]
                        pe.wait_ge(pt_v if m % 2 else pt_a, l * 20 + m // 2 + 1)
                        if b == 4 and h == 0:
                            pe.wait_ge(a_done, l * NT + 1)
                        vs = values(b)
                        for x, v in enumerate(vs):
                            mm = pe.matmul(bank[b % 4][:, h * HD:(h + 1) * HD], probT[m % 2][:, x * P:(x + 1) * P],
                                           v[:, h // 4 * HD:h // 4 * HD + HD],
                                           start=(x == 0), stop=(x == len(vs) - 1))
                        mm.then_inc(pv_mm, 1)

                def mixers_T(t):
                    pe.wait_ge(mixn, l * NT + t + 1)
                    if t >= 2:
                        pe.wait_ge(mx_out, l * NT + t - 1)
                    for n in range(KC):
                        a = n * P if n < 4 else (1024 + (n - 4) * P if n < 6 else 768 + (n - 6) * P)
                        mm = pe.transpose(bank[4 + 2 * (t % 2) + n // 4][:, (n % 4) * P:(n % 4 + 1) * P],
                                          zt[:, t, a:a + P], ident)
                    mm.then_inc(mx_mm, 1)

                def keep_clock(n):
                    for _ in range(n):
                        pe.matmul(bank[2][:, :], ident, mask, start=True, stop=True)

                pe.wait_ge(a_done, l * NT + NT - 2)
                keep_clock(5)
                mixers_T(0)
                keep_clock(1)
                mixers_T(1)
                keep_clock(2)
                pe.wait_ge(wo_lo, l * 8 + 8)
                for n in range(NT + 2):
                    if n == 1:
                        for t in range(2, NT):
                            mixers_T(t)
                        pe.wait_ge(mx_out, l * NT + NT)
                    if n < NT:
                        if n >= 2:
                            pe.wait_ge(x1_done, l * NT + n - 1)
                        pe.wait_ge(m_lo, l * NT + n + 1)
                        tile = slice(n * P, (n + 1) * P)
                        for x in range(2):
                            cols = slice(x * 512, (x + 1) * 512)
                            for c in range(KC):
                                parts = ((mixed_high[:, c, tile], slot_r[1][:, c, cols]),
                                         (mixed_high[:, c, tile], slot_r[2][:, c, cols]),
                                         (h_low[:, c, tile], slot_r[1][:, c, cols]))
                                for part, (m, w) in enumerate(parts):
                                    mm = pe.matmul(bank[2 * (n % 2) + x][:, :], m, w,
                                                   start=(c == 0 and part == 0), stop=(c == KC - 1 and part == 2))
                        mm.then_inc(wo_mm if n < NT - 1 else used[2], 1)
                    t = n - 1
                    if 0 <= t < NT:
                        pe.wait_ge(xn2, l * NT + t + 1)
                        if t:
                            pe.wait_ge(h2_v, l * NT + t)
                            pe.wait_ge(h2_a, l * NT + t)
                        for k in range(KC):
                            mm = pe.transpose(bank[4 + k // 4][:, (k % 4) * P:(k % 4 + 1) * P], xn[:, t, k:D:KC], ident)
                        mm.then_inc(t2_mm, 1)
                    t = n - 2
                    if 0 <= t < NT:
                        pe.wait_ge(h2_v, l * NT + t + 1)
                        pe.wait_ge(h2_a, l * NT + t + 1)
                        for c in range(KC):
                            mm = pe.matmul(bank[6][:, t * EXPERTS:(t + 1) * EXPERTS], hT[:, c, t * P:(t + 1) * P],
                                           rw[:, c, :], start=(c == 0), stop=(c == KC - 1))
                        mm.then_inc(lg_mm, 1)
                pe.wait_ge(aff_done, l + 1)
                for t in range(NT):
                    out = bank[7][0:EXPERTS, t * P:(t + 1) * P] if t < 4 else bank[5][0:EXPERTS, 0:P]
                    mm = pe.transpose(out, aff[:, t, :], ident)
                mm.then_inc(affT_mm, 1)
                hold(pe, top_done, l + 1, const_in)
                pe.transpose(bank[6][0:CAP, 0:EXPERTS], topf[:, :], ident[0:EXPERTS, 0:EXPERTS])
                pe.transpose(bank[6][0:CAP, EXPERTS:2 * EXPERTS], topv[:, :], ident[0:EXPERTS, 0:EXPERTS])\
                    .then_inc(top_mm, 1)

                def product(m, s, out, x, between=(None, None)):
                    for c in range(KC):
                        if isinstance(m, int) and m == 0:
                            pe.wait_ge(first_low, l * KC + c + 1)
                        else:
                            pe.wait_ge(low_ready, l * ((MATS - 1) * KC) + m * KC + (c + 1 - KC))
                        parts = ((x[0], high[c]), (x[0], slot_r[s][:, c, :]), (x[1], high[c]))
                        for part, (xs, w) in enumerate(parts):
                            for n in range(2):
                                mm = pe.matmul(bank[out + n][0:CAP, :], xs[:, c, :], w[:, n * 512:(n + 1) * 512],
                                               start=(c == 0 and part == 0), stop=(c == KC - 1 and part == 2))
                        mm.then_inc(chunk_used, 1)
                        if c == between[0]:
                            between[1]()

                def rows_T(u, k):
                    pe.wait_ge(xe_in[u], (l * PAIRS + k) * 16 + 16)
                    for c in range(KC):
                        mm = pe.transpose(bank[6 + c // 4][:, (c % 4) * CAP:(c % 4 + 1) * CAP], xe[u][:, c:D:KC],
                                          ident[0:CAP, 0:CAP])
                    mm.then_inc(xeT_mm, 1)

                def hidden_T(e):
                    pe.wait_ge(he_done, l * EXPERTS + e + 1)
                    for c in range(KC):
                        mm = pe.transpose(bank[6 + c // 4][:, (c % 4) * CAP:(c % 4 + 1) * CAP], he[:, c:D:KC],
                                          ident[0:CAP, 0:CAP])
                    mm.then_inc(heT_mm, 1)

                def expert(e, u, k, last=False):
                    product(w3_at(e), 1, 2, xeT[u], (None, None) if last else (1, lambda: rows_T(1 - u, k + u)))
                    if last:
                        hidden_T(e)
                    else:
                        pe.wait_ge(xeT_out, l * EXPERTS + e + 2)
                        product(w1_next_at(e), 0, 0, xeT[1 - u], (3, lambda: hidden_T(e)))
                    pe.wait_ge(heT_out, l * EXPERTS + e + 1)
                    product(w2_at(e), 2, 4, heT)

                pe.wait_ge(top_out, l + 1)
                keep_clock(3)
                rows_T(0, 0)
                keep_clock(2)
                pe.wait_ge(xeT_out, l * EXPERTS + 1)
                product(0, 0, 0, xeT[0])
                with pe.Fori(0, PAIRS - 1) as k:
                    for u in range(2):
                        expert(k * 2 + u, u, k)
                expert(EXPERTS - 2, 0, PAIRS - 1)
                expert(EXPERTS - 1, 1, PAIRS - 1, last=True)
                pe.wait_ge(ye_done, l * EXPERTS + EXPERTS)

        @block.scalar
        def _(act):
            act.wait_ge(c_in, 32)
            act.activation(cs[:, :, 0:2].rearrange("p k s -> p s k"), cvec[:, :, :], ACT.Silu).then_inc(cs_done, 1)

            with act.Fori(0, DEPTH) as l:
                link = Chain(act, a_link, "A_LAYER", l * A_LAYER, A_LAYER)

                def ada_rounded(j):
                    for k in range(ASPLIT):
                        c = SPLIT0 + k
                        if k < 2:
                            act.wait_ge(ada_in[j % SLOTS][c // HALF], l * 32 + 16 * (j // SLOTS + 1))
                        act.wait_ge(achunk_used, (l * ADA + j) * ASPLIT + k + 1)
                        act.activation(ahigh[k], slot[j % SLOTS][:, c, :], ACT.Copy).then_inc(ahigh_ready, 1)

                def sine(n):
                    act.wait_ge(f_pre, l * 2 + n + 1)
                    act.activation(hid, pre, ACT.Sin).then_inc(f_sin, 1)

                act.wait_ge(chunk_used, AHEAD + l * (MATS * KC))
                for j in range(5):
                    ada_rounded(j)
                    if j in (1, 2):
                        sine(j - 1)
                for n in range(5):
                    act.wait_ge(spec_mm, l * 5 + n + 1)
                    if n < 4:
                        dst, src = spectrum[:, n // 2, 2 * (n % 2):2 * (n % 2) + 2, :], bank[6 + n % 2][:, :]
                    else:
                        dst, src = spectrum[:, :, 4, :], bank[6][:, :]
                    act.activation(dst, src.rearrange("p (j n) -> p j n", j=2), ACT.Copy,
                                   scale=1.0 / (LAT if n < 4 else CTX)).then_inc(spec_out, 1)

                ada_rounded(5)

                act.wait_ge(x_in, l * 16 + 16)
                for t in range(NT):
                    for x in range(2):
                        ins = act.activation(jk[:, :], zt[:, t, x * 512:(x + 1) * 512], ACT.Square,
                                             accum_out=ssum[:, 10 * x + t:10 * x + t + 1])
                        ins.then_inc(sq1, 1) if t == NT - 1 and x else link(ins)
                act.wait_ge(rec1, l + 1)
                act.activation(sroot[:, 0:NT], srec[:, 0:NT], ACT.Sqrt).then_inc(root1, 1)
                def w_in_rounded(g):
                    act.wait_ge(arrived[g // 2], l * 16 + 16)
                    for c in range(0, KC, 2):
                        w, high_w = w_group(slot, g, c)
                        act.activation(high_w, w, ACT.Copy).then_inc(w_hi, 1)

                act.wait_ge(used[2], l * ROUNDS + 2)
                w_in_rounded(0)
                act.wait_ge(mod_out, l * len(MOD) + len(MOD))

                def modulated(t, src, s0, done):
                    s = t // 4
                    for k in range(4, KC):
                        ins = act.activation(hT[:, k, t * P:(t + 1) * P], src[:, (k - 4) * P:(k - 3) * P], ACT.Identity,
                                             bias=mod[:, s0, k, s:s + 1], scale=mod[:, s0 + 1, k, s:s + 1])
                    ins.then_inc(done, 1)

                for n in range(NT + 1):
                    if n < NT:
                        act.wait_ge(t1_mm, l * NT + n + 1)
                        modulated(n, bank[2 * (n % 4) + 1], 0, h1_a)
                    t = n - 1
                    if t >= 0:
                        tile = slice(t * P, (t + 1) * P)
                        act.wait_ge(h1_v, l * NT + t + 1)
                        act.activation(h_high[:, :, tile], hT[:, 0:4, tile], ACT.Copy)
                        act.wait_ge(h1_a, l * NT + t + 1)
                        act.activation(h_high_z[:, t, 768:1280].rearrange("p (c n) -> p c n", c=4), hT[:, 4:8, tile],
                                       ACT.Copy).then_inc(h_hi, 1)
                w_in_rounded(1)

                for n, (kind, t, e) in enumerate(proj):
                    if n in (GROUPS[1], GROUPS[2]):
                        s, per, at = multiplied(n - 1)
                        act.wait_ge(s, l * per + at)
                        w_in_rounded(2 if n == GROUPS[1] else 3)
                    if e == "a":
                        s, per, at = multiplied(n)
                        act.wait_ge(s, l * per + at)
                        if kind == "kv":
                            act.activation(zt[:, t, 512:768], bank[(n + 2) % 8][:, 0:256], ACT.Copy).then_inc(z_a, 1)
                        else:
                            act.activation(zt[:, t, 768:1280], bank[(n + 2) % 8][:, :], ACT.Gelu_apprx_tanh).then_inc(z_a, 1)

                act.wait_ge(x0_mm, l + 1)
                for g, (b, a) in enumerate(((6, 0), (7, 0), (5, GM))):
                    w = 2 if g < 2 else 1
                    ins = act.activation(x0tok[:, 2 * g:2 * g + w, :],
                                         bank[b][:, a:a + w * HY].rearrange("p (t n) -> p t n", t=w), ACT.Copy)
                ins.then_inc(x0_out, 1)
                for g in range(3):
                    act.wait_ge(ut_mm, l * 3 + g + 1)
                    w = 2 if g < 2 else 1
                    act.activation(utok[:, 2 * g:2 * g + w, :], bank[3 + g][:, 0:w * HY].rearrange("p (t n) -> p t n", t=w),
                                   ACT.Copy).then_inc(ut_out, 1)
                act.wait_ge(gm_out, l * 3 + 3)
                for t in range(NT):
                    ins = act.activation(jk[:, 0:GM], zt[:, t, 768:1024], ACT.Square, accum_out=ssum[:, 5 + t:6 + t])
                    link(ins) if t < NT - 1 else ins.then_inc(gm_sq, 1)

                for n in range(7):
                    act.wait_ge(qk_mm, l * 7 + n + 1)
                    src = bank[3 + n % 3]
                    if n < 5:
                        for g in range(KV):
                            half = slice(g * HD, (g + 1) * HD)
                            ins = act.activation(qT[g][half, :, n * P:(n + 1) * P],
                                                 src[half, :].rearrange("p (i t) -> p i t", i=4), ACT.Copy)
                    elif n == 5:
                        ins = act.activation(kT[:, 0:512], src[:, :], ACT.Copy)
                    else:
                        ins = act.activation(kT[:, 512:768], src[:, 0:256], ACT.Copy)
                    ins.then_inc(qk_a, 1)

                for n in range(len(att) + 8):
                    if n % 8 == 4:
                        t = n // 8
                        if t == 0:
                            act.wait_ge(yh_done, l + 1)
                        if t < NT:
                            act.activation(jk[:, GM:2 * GM], zt[:, t, 1024:1280], ACT.Square,
                                           accum_out=ssum[:, 10 + t:11 + t]).then_inc(ysq_done, 1)
                            act.wait_ge(ysq_done, l * NT + t + 1)
                    if n % 4 == 2 and 8 <= n < 40:
                        c = n // 4 - 2
                        act.wait_ge(arrived[2], l * 16 + 16)
                        act.activation(slot_r[1][:, c, :], slot[2][:, c, :], ACT.Copy).then_inc(wo_hi, 1)
                    if n < len(att):
                        b, h = att[n]
                        act.wait_ge(sc_out, l * len(att) + n + 1)
                        if n >= 2:
                            act.wait_ge(pt_mm, l * len(att) + n - 1)
                        w = width(b)
                        act.activation(prob[n % 2][:, 0:w], sbuf_s[n % 2][:, 0:w], ACT.Exp,
                                       bias=negmax[:, b, h:h + 1], scale=-1.0,
                                       accum_out=rsum[:, b, h:h + 1]).then_inc(p_done, 1)
                    m = n - 2
                    if 0 <= m < len(att) and m % 2 == 0:
                        act.wait_ge(pt_mm, l * len(att) + m + 1)
                        if m >= 2:
                            act.wait_ge(pv_mm, l * len(att) + m - 1)
                        w = width(att[m][0])
                        act.activation(probT[0][:, 0:w], bank[6][:, 0:w], ACT.Copy).then_inc(pt_a, 1)
                    if n >= 8 and n % 8 == 0:
                        b = n // 8 - 1
                        act.wait_ge(es_in, l * NT + b + 1)
                        act.activation(esink[:, b, :], denom[:, b, :], ACT.Exp).then_inc(es_out, 1)
                    if n >= 14 and n % 8 == 6:
                        b = n // 8 - 1
                        act.wait_ge(a_done, l * NT + b + 1)
                        ins = act.activation(jk[:, :], zt[:, b, 0:ATT], ACT.Square, accum_out=ssum[:, b:b + 1])
                        ins.then_inc(a_sq, 1)
                act.wait_ge(mrec, l + 1)
                act.activation(sroot[:, :], srec[:, :], ACT.Sqrt).then_inc(mroot, 1)
                for t in range(NT):
                    act.wait_ge(mx_out, l * NT + t + 1)
                    tile = slice(t * P, (t + 1) * P)
                    act.activation(mixed_high[:, :, tile], hT[:, :, tile], ACT.Copy).then_inc(m_hi, 1)

                for n in range(NT + 1):
                    if n < NT:
                        act.wait_ge(x1_done, l * NT + n + 1)
                        act.activation(junk, zt[:, n, 0:D], ACT.Square, accum_out=ssum[:, n:n + 1]).then_inc(sq2, 1)
                        act.wait_ge(rec2, l * NT + n + 1)
                        act.activation(sroot[:, n:n + 1], srec[:, n:n + 1], ACT.Sqrt).then_inc(root2, 1)
                    t = n - 1
                    if 0 <= t < NT:
                        act.wait_ge(t2_mm, l * NT + t + 1)
                        modulated(t, bank[5], 2, h2_a)
                act.wait_ge(anm_done, l + 1)
                for t in range(NT):
                    ins = act.activation(aff[:, t, :], bank[6][:, t * EXPERTS:(t + 1) * EXPERTS], ACT.Exp,
                                         bias=anm[:, t:t + 1], accum_out=asum[:, t:t + 1])
                ins.then_inc(aexp, 1)

                def rounded(m, s, e, after=(None, None)):
                    for c in range(KC):
                        if c % HALF == 0:
                            act.wait_ge(half_in[s][c // HALF], (l * EXPERTS + e) * 16 + 16)
                        act.wait_ge(chunk_used, AHEAD - KC + chunks(l, m, c))
                        act.activation(high[c], slot[s][:, c, :], ACT.Copy).then_inc(high_ready, 1)
                        if c == after[0]:
                            after[1]()

                def rows(x):
                    act.wait_ge(xt_done, l * EXPERTS + x + 1)
                    act.activation(xeT[x % 2 if isinstance(x, int) else 1 - u][0], xt, ACT.Copy).then_inc(xh_done, 1)

                def hidden(e):
                    act.wait_ge(heT_mm, l * EXPERTS + e + 1)
                    for n in range(2):
                        ins = act.activation(heT[0][:, 4 * n:4 * n + 4, :],
                                             bank[6 + n][:, 0:4 * CAP].rearrange("p (c t) -> p c t", c=4), ACT.Copy)
                    ins.then_inc(hh_done, 1)

                def gated(m, e):
                    act.wait_ge(chunk_used, AHEAD + chunks(l, m, KC - 1))
                    act.activation(he[:, 0:512], bank[0][0:CAP, :], ACT.Silu)
                    act.activation(he[:, 512:D], bank[1][0:CAP, :], ACT.Silu).then_inc(silu, 1)

                act.wait_ge(lg_mm, l * NT + NT)
                rounded(0, 0, 0, (4, lambda: act.wait_ge(xn_out, l * 80 + 80)))
                u = 1
                rows(0)
                rounded(w3_at(0), 1, 0)
                gated(0, 0)

                def prepare(e):
                    rounded(w1_next_at(e), 0, e + 1, (4, lambda: rows(e + 1)))
                    rounded(w2_at(e), 2, e, (3, lambda: hidden(e)))
                    gated(w1_next_at(e), e + 1)
                    rounded(w3_at(e + 1), 1, e + 1)

                with act.Fori(0, PAIRS - 1) as k:
                    for u in range(2):
                        prepare(k * 2 + u)
                u = 0
                prepare(EXPERTS - 2)
                rounded(w2_at(EXPERTS - 1), 2, EXPERTS - 1, (3, lambda: hidden(EXPERTS - 1)))
                link.close()

            for t in range(NT):
                act.wait_ge(fin_in[t], 16)
                act.activation(arena_u[:, t * D:(t + 1) * D], zt[:, t, 0:D], ACT.Square, accum_out=ssum[:, t:t + 1])\
                    .then_inc(fsq, 1)
            act.wait_ge(frec, 1)
            act.activation(sroot[:, 0:NT], srec[:, 0:NT], ACT.Sqrt).then_inc(froot, 1)

        @block.vector
        def _(v):
            def newton(link, root, ms, tmp):
                link(v.tensor_tensor(tmp, root, root, ALU.mult))
                link(v.tensor_tensor(tmp, tmp, ms, ALU.mult))
                link(v.tensor_scalar(tmp, tmp, -0.5, 1.5, ALU.mult, ALU.add))
                link(v.tensor_tensor(root, root, tmp, ALU.mult))

            v.memset(cs[:, :, 2:4], 0.0).then_inc(cs_zero, 1)
            v.wait_ge(const_in, 32)
            v.wait_ge(cs_done, 1)
            v.wait_ge(cs_zero, 1)
            v.tensor_copy(cs_r[:, :, 0:2], cs[:, :, 0:2]).then_inc(cs_parts, 1)
            v.wait_ge(cs_parts, 1)
            v.tensor_tensor(cs_r[:, :, 2:4], cs[:, :, 0:2], cs_r[:, :, 0:2], ALU.subtract).then_inc(cs_parts, 1)
            with v.Fori(0, DEPTH) as l:
                link = Chain(v, v_link, "V_LAYER", l * V_LAYER, V_LAYER)

                def row(j):
                    v.wait_ge(used[j % SLOTS], l * ROUNDS + j // SLOTS + 1)
                    if j >= 2:
                        v.wait_ge(mod_mm, l * len(MOD) + spread[j - 2])
                    for n in range(2):
                        ins = v.tensor_copy(mrow[j % 2][0:4, n * 512:(n + 1) * 512], bank[2 * (j % 2) + n][0:4, :])
                    ins.then_inc(mrow_done, 1)

                def mod_taken(q):
                    j, what = MOD[q]
                    v.wait_ge(mod_mm, l * len(MOD) + q + 1)
                    cols = bank[4][:, 0:2 * KC].rearrange("p (k s) -> p k s", s=2)
                    if what == "col":
                        n = {0: 0, 1: 1, 3: 2, 4: 3}[j]
                        bias = prm[:, AB + n * KC:AB + (n + 1) * KC].unsqueeze(2).broadcast_to([P, KC, 2])
                        ins = v.tensor_tensor(mod[:, n, :, :], cols, bias, ALU.add)
                        if n % 2 == 0:
                            ins.then_inc(mod_out, 1)
                        else:
                            link(ins)
                            g = prm[:, (G1 if j == 1 else G2):(G1 if j == 1 else G2) + KC]
                            v.scalar_tensor_tensor(out=mod[:, n, :, :], in0=mod[:, n, :, :], scalar=1.0,
                                                   in1=g.unsqueeze(2).broadcast_to([P, KC, 2]),
                                                   op0=ALU.add, op1=ALU.mult).then_inc(mod_out, 1)
                    else:
                        dst, m = {"lat": (gate1[:, 0, :], P), "ctx": (gate1[:, 1, :], P), "cap": (gate2[:, :], CAP)}[what]
                        for n in range(2):
                            ins = v.tensor_copy(dst[:, n * 512:(n + 1) * 512], bank[4 + n][0:m, :])
                        ins.then_inc(mod_out, 1)

                def ada_rest(j):
                    for k in range(ASPLIT):
                        c = SPLIT0 + k
                        v.wait_ge(ahigh_ready, (l * ADA + j) * ASPLIT + k + 1)
                        v.tensor_tensor(slot_r[j % SLOTS][:, c, :], slot[j % SLOTS][:, c, :], ahigh[k],
                                        ALU.subtract).then_inc(alow_ready, 1)

                def phase(n):
                    v.wait_ge(f_mm, l * 2 + n + 1)
                    b1, fq = prm[0:FH, FB1 + n:FB1 + n + 1], prm[0:FH, FQ:FQ + 1]
                    v.tensor_scalar(pre[:, 0:LAT], bank[6][0:FH, :], b1, fq, ALU.add, ALU.mult)
                    link(v.tensor_scalar(pre[:, LAT:TOK], bank[7][0:FH, 0:CTX], b1, fq, ALU.add, ALU.mult))
                    link(v.tensor_scalar(turns, pre, 1.0 / (TWO_PI_HI + TWO_PI_LO), ROUND, ALU.mult, ALU.add))
                    link(v.tensor_scalar(turns, turns, ROUND, None, ALU.subtract))
                    link(v.scalar_tensor_tensor(out=pre, in0=turns, scalar=-TWO_PI_HI, in1=pre, op0=ALU.mult, op1=ALU.add))
                    link(v.scalar_tensor_tensor(out=pre, in0=turns, scalar=-TWO_PI_LO, in1=pre, op0=ALU.mult, op1=ALU.add))
                    v.tensor_scalar(pre, pre, PI_IN, -PI_IN, ALU.min, ALU.max).then_inc(f_pre, 1)

                def taps(t):
                    v.wait_ge(f3_mm, l * NT + t + 1)
                    src = bank[6 + t % 2]
                    v.tensor_tensor(hfw, src[:, 0:HY], win[:, t, :], ALU.mult)
                    link(v.tensor_tensor(hbw, src[:, HY:2 * HY], win[:, t, :], ALU.mult))
                    if t in (0, 4):
                        v.tensor_tensor(hfw[0:1, :], hfw[0:1, :], dbias, ALU.add)
                        link(v.memset(hbw[0:1, :], 0.0))
                    v.tensor_tensor(fsum[:, t, :], hfw, hbw, ALU.add)
                    ins = v.tensor_tensor(fdif[:, t, :], hfw, hbw, ALU.subtract)
                    ins.then_inc(f3_out, 1)
                    v.wait_ge(f3_out, l * NT + t + 1)

                v.wait_ge(rows_free, l * EXPERTS + 2)
                ada_rest(0)
                v.wait_ge(prm_in, l * 160 + 160)
                v.tensor_scalar(nsink[:, :], prm[:, SK:SK + HEADS], -1.0, None, ALU.mult)
                ada_rest(1)
                phase(0)
                row(0)
                ada_rest(2)
                phase(1)
                mod_taken(0)
                row(1)
                v.wait_ge(fil_in, l * 80 + 80)
                ada_rest(3)
                taps(0)
                taps(1)
                mod_taken(1)
                row(2)
                ada_rest(4)
                taps(2)
                taps(3)
                mod_taken(2)
                mod_taken(3)
                row(3)
                taps(4)
                ada_rest(5)
                mod_taken(4)
                row(4)
                mod_taken(5)
                row(5)
                mod_taken(6)

                v.wait_ge(sq1, l + 1)
                link(v.tensor_tensor(ssum[:, 0:NT], ssum[:, 0:NT], ssum[:, 10:15], ALU.add))
                link(v.tensor_scalar(sms[:, 0:NT], ssum[:, 0:NT], 1.0 / D, EPS, ALU.mult, ALU.add))
                v.reciprocal(srec[:, 0:NT], sms[:, 0:NT]).then_inc(rec1, 1)
                v.wait_ge(root1, l + 1)
                newton(link, sroot[:, 0:NT], sms[:, 0:NT], stmp[:, 0:NT])
                for t in range(NT):
                    v.tensor_scalar(zt[:, t, 0:D], zt[:, t, 0:D], sroot[:, t:t + 1], None, ALU.mult).then_inc(xn1, 1)

                def modulated(t, src, s0, done):
                    s = t // 4
                    for k in range(4):
                        ins = v.tensor_scalar(hT[:, k, t * P:(t + 1) * P], src[:, k * P:(k + 1) * P],
                                              mod[:, s0 + 1, k, s:s + 1], mod[:, s0, k, s:s + 1], ALU.mult, ALU.add)
                    ins.then_inc(done, 1)

                def w_in_rest(g):
                    for c in range(0, KC, 2):
                        v.wait_ge(w_hi, l * 16 + g * 4 + c // 2 + 1)
                        w, high_w = w_group(slot, g, c)
                        v.tensor_tensor(w_group(slot_r, g, c)[0], w, high_w, ALU.subtract).then_inc(w_lo[1], 1)

                v.wait_ge(mod_out, l * len(MOD) + len(MOD))
                for n in range(NT + 2):
                    if n < NT:
                        v.wait_ge(t1_mm, l * NT + n + 1)
                        modulated(n, bank[2 * (n % 4)], 0, h1_v)
                    t = n - 2
                    if t >= 0:
                        v.wait_ge(h_hi, l * NT + t + 1)
                        tile = slice(t * P, (t + 1) * P)
                        v.tensor_tensor(h_low[:, 0:4, tile], hT[:, 0:4, tile], h_high[:, :, tile], ALU.subtract)
                        v.tensor_tensor(h_low[:, 4:8, tile], hT[:, 4:8, tile],
                                        h_high_z[:, t, 768:1280].rearrange("p (c n) -> p c n", c=4), ALU.subtract)\
                            .then_inc(h_lo, 1)

                for n, (kind, t, e) in enumerate(proj):
                    if n in (GROUPS[1], GROUPS[2]):
                        w_in_rest(2 if n == GROUPS[1] else 3)
                    if e == "v":
                        s, per, at = multiplied(n)
                        v.wait_ge(s, l * per + at)
                        if kind == "q":
                            dst, src = zt[:, t, 0:512], bank[(n + 2) % 8][:, :]
                        else:
                            a, b = token_half(t[1])
                            dst, src = zhT[:, t[0], a * P:b * P], bank[(n + 2) % 8][:, 0:(b - a) * P]
                        v.tensor_copy(dst, src).then_inc(z_v, 1)
                v.wait_ge(z_v, l * Z_V + Z_V)

                for m in range(6):
                    dst = x0c[:, m, :] if m < 2 else uT[:, m - 2, :] if m < 4 else cvt
                    w = [prm[:, CW + 6 * j + m:CW + 6 * j + m + 1] for j in range(TAPS)]
                    link(v.tensor_scalar(dst, zhT[:, m, :], w[1], prm[:, CB + m:CB + m + 1], ALU.mult, ALU.add))
                    for j, (to, fr) in enumerate(((1, 0), (0, 1))):
                        for a, b in ((0, LAT), (LAT, TOK)):
                            ins = v.scalar_tensor_tensor(out=dst[:, a + to:b - fr], in0=zhT[:, m, a + fr:b - to],
                                                         scalar=w[2 * j], in1=dst[:, a + to:b - fr],
                                                         op0=ALU.mult, op1=ALU.add)
                        link(ins)
                    if m == 1:
                        v.sem_inc(x0_done, 1)
                    if m >= 4:
                        ins = v.tensor_tensor(uT[:, m - 4, :], uT[:, m - 4, :], cvt, ALU.mult)
                        link(ins) if m == 4 else ins.then_inc(u_done, 1)

                for t in range(4):
                    s, per, n = taken(proj_at("kv", t))
                    v.wait_ge(s, l * per + n)
                    x = zt[:, t, 0:640].rearrange("p (h a b n) -> p h a b n", h=10, a=2, b=2)
                    r = rtmp[:, :].rearrange("p (h a b n) -> p h a b n", h=10, a=2, b=2)
                    sn = sin_t[:, t].unsqueeze(1).broadcast_to([P, 10, 2, 16])
                    v.scalar_tensor_tensor(out=r[:, :, :, 0, :], in0=x[:, :, :, 1, :], scalar=-1.0, in1=sn,
                                           op0=ALU.mult, op1=ALU.mult)
                    link(v.tensor_tensor(r[:, :, :, 1, :], x[:, :, :, 0, :], sn, ALU.mult))
                    x3 = zt[:, t, 0:640].rearrange("p (h d) -> p h d", h=10)
                    link(v.tensor_tensor(x3, x3, cos_t[:, t].unsqueeze(1).broadcast_to([P, 10, 64]), ALU.mult))
                    v.tensor_tensor(zt[:, t, 0:640], zt[:, t, 0:640], rtmp[:, :], ALU.add).then_inc(rope_done, 1)
                    v.wait_ge(rope_done, l * 4 + t + 1)

                for g in range(3):
                    v.wait_ge(gm_mm, l * 3 + g + 1)
                    ts = [t for t in (2 * g, 2 * g + 1) if t < NT]
                    for x, t in enumerate(ts):
                        ins = v.tensor_tensor(zt[:, t, 1024:1280].rearrange("p (h c) -> p h c", h=GH),
                                              bank[g][:, x * GM:(x + 1) * GM].rearrange("p (h c) -> p h c", h=GH),
                                              prm[:, GB:GB + GH].unsqueeze(2).broadcast_to([P, GH, 64]), ALU.add)
                    link(ins)
                    for t in ts:
                        ins = v.tensor_tensor(zt[:, t, 768:1024], zt[:, t, 768:1024], zt[:, t, 1024:1280], ALU.mult)
                    ins.then_inc(gm_out, 1)

                v.wait_ge(fwd_mm, l + 1)
                v.wait_ge(spec_out, l * 5 + 5)
                for n, (x, f) in enumerate(((0, 0), (1, 1), (0, 1), (1, 0))):
                    for j in range(2):
                        v.tensor_tensor(prod[n][:, 2 * j:2 * j + 2, :],
                                        bank[FWD[2 * x + j]][:, :].rearrange("p (j n) -> p j n", j=2),
                                        spectrum[:, f, 2 * j:2 * j + 2, :], ALU.mult)
                    ins = v.tensor_tensor(prod[n][:, 4, :], bank[FWD[4]][:, x * HY:(x + 1) * HY],
                                          spectrum[:, f, 4, :], ALU.mult)
                link(ins)
                v.tensor_tensor(spec[1], spec[1], spec[2], ALU.subtract)
                v.tensor_tensor(spec[3], spec[3], spec[4], ALU.add).then_inc(y_done, 1)

                v.wait_ge(inv_mm, l + 1)
                v.wait_ge(x0_out, l + 1)
                for g in range(3):
                    w = 2 if g < 2 else 1
                    ins = v.tensor_tensor(zt[:, 2 * g:2 * g + w, 1024:1280],
                                          bank[3 + g][:, 0:w * HY].rearrange("p (t n) -> p t n", t=w),
                                          x0tok[:, 2 * g:2 * g + w, :], ALU.mult)
                ins.then_inc(yh_done, 1)

                for n in range(len(att) + 4):
                    if n % 4 == 3 and 8 <= n < 40:
                        c = n // 4 - 2
                        v.wait_ge(wo_hi, l * 8 + c + 1)
                        v.tensor_tensor(slot_r[2][:, c, :], slot[2][:, c, :], slot_r[1][:, c, :], ALU.subtract)\
                            .then_inc(wo_lo, 1)
                    if n < len(att):
                        b, h = att[n]
                        if n >= 2:
                            v.wait_ge(p_done, l * len(att) + n - 1)
                        hold(v, sc_mm, l * len(att) + n + 1, const_in)
                        w, m0 = width(b), keys(b)[1]
                        v.tensor_tensor_reduce(out=sbuf_s[n % 2][:, 0:w], in0=bank[4 + n % 2][:, 0:w],
                                               in1=mask[:, m0:m0 + w], scale=-SCALE, scalar=nsink[:, h:h + 1],
                                               op0=ALU.add, op1=ALU.min,
                                               accum_out=negmax[:, b, h:h + 1]).then_inc(sc_out, 1)
                    m = n - 2
                    if 0 <= m < len(att) and m % 2:
                        v.wait_ge(pt_mm, l * len(att) + m + 1)
                        if m >= 2:
                            v.wait_ge(pv_mm, l * len(att) + m - 1)
                        w = width(att[m][0])
                        v.tensor_copy(probT[1][:, 0:w], bank[7][:, 0:w]).then_inc(pt_v, 1)
                    if n >= 8 and n % 8 == 0:
                        b = n // 8 - 1
                        v.wait_ge(sc_out, l * len(att) + n)
                        v.tensor_tensor(denom[:, b, :], negmax[:, b, :], nsink[:, :], ALU.subtract).then_inc(es_in, 1)
                    if n >= 11 and n % 8 == 3:
                        b = n // 8 - 1
                        v.wait_ge(es_out, l * NT + b + 1)
                        v.wait_ge(pv_mm, l * len(att) + 8 * b + 8)
                        link(v.tensor_tensor(denom[:, b, :], rsum[:, b, :], esink[:, b, :], ALU.add))
                        link(v.reciprocal(denom[:, b, :], denom[:, b, :]))
                        v.tensor_tensor(zt[:, b, 0:ATT].rearrange("p (h d) -> p h d", h=HEADS),
                                        bank[b % 4][:, :].rearrange("p (h d) -> p h d", h=HEADS),
                                        denom[:, b, :].unsqueeze(2).broadcast_to([P, HEADS, HD]), ALU.mult)\
                            .then_inc(a_done, 1)

                v.wait_ge(a_sq, l * NT + NT)
                v.wait_ge(gm_sq, l + 1)
                v.wait_ge(ysq_done, l * NT + NT)
                v.tensor_scalar(sms[:, 0:5], ssum[:, 0:5], 1.0 / ATT, EPS, ALU.mult, ALU.add)
                link(v.tensor_scalar(sms[:, 5:15], ssum[:, 5:15], 1.0 / GM, EPS, ALU.mult, ALU.add))
                v.reciprocal(srec[:, :], sms[:, :]).then_inc(mrec, 1)
                v.wait_ge(mroot, l + 1)
                newton(link, sroot[:, :], sms[:, :], stmp[:, :])
                v.wait_ge(a_done, l * NT + NT)
                v.wait_ge(gm_out, l * 3 + 3)
                def scaled(t):
                    for a, b, c in ((0, ATT, t), (768, 1024, 5 + t), (1024, 1280, 10 + t)):
                        ins = v.tensor_scalar(zt[:, t, a:b], zt[:, t, a:b], sroot[:, c:c + 1], None, ALU.mult)
                    ins.then_inc(mixn, 1)

                def mixed(t):
                    v.wait_ge(mx_mm, l * NT + t + 1)
                    for x in range(2):
                        ins = v.tensor_tensor(hT[:, 4 * x:4 * x + 4, t * P:(t + 1) * P],
                                              bank[4 + 2 * (t % 2) + x][:, :].rearrange("p (c t) -> p c t", c=4),
                                              prm[:, GO + 4 * x:GO + 4 * x + 4].unsqueeze(2).broadcast_to([P, 4, P]),
                                              ALU.mult)
                    ins.then_inc(mx_out, 1)

                def mixed_rest(t):
                    v.wait_ge(m_hi, l * NT + t + 1)
                    tile = slice(t * P, (t + 1) * P)
                    v.tensor_tensor(h_low[:, :, tile], hT[:, :, tile], mixed_high[:, :, tile], ALU.subtract)\
                        .then_inc(m_lo, 1)

                scaled(0)
                scaled(1)
                mixed(0)
                scaled(2)
                mixed_rest(0)
                mixed(1)
                scaled(3)
                mixed_rest(1)
                scaled(4)
                for t in range(2, NT):
                    mixed(t)
                    if t > 2:
                        mixed_rest(t - 1)
                mixed_rest(NT - 1)

                for n in range(NT + 1):
                    if n < NT:
                        if n < NT - 1:
                            v.wait_ge(wo_mm, l * (NT - 1) + n + 1)
                        else:
                            v.wait_ge(used[2], l * ROUNDS + 3)
                        halves = (rtmp[:, 0:512], jk[:, :])
                        for x in range(2):
                            ins = v.tensor_tensor(halves[x], bank[2 * (n % 2) + x][:, :],
                                                  gate1[:, n // 4, x * 512:(x + 1) * 512], ALU.mult)
                        link(ins)
                        v.wait_ge(xr_in[n], l * 16 + 16)
                        for x in range(2):
                            a = zt[:, n, x * 512:(x + 1) * 512]
                            ins = v.tensor_tensor(a, a, halves[x], ALU.add)
                        ins.then_inc(x1_done, 1)
                        v.wait_ge(sq2, l * NT + n + 1)
                        c = slice(n, n + 1)
                        link(v.tensor_scalar(sms[:, c], ssum[:, c], 1.0 / D, EPS, ALU.mult, ALU.add))
                        v.reciprocal(srec[:, c], sms[:, c]).then_inc(rec2, 1)
                        v.wait_ge(root2, l * NT + n + 1)
                        newton(link, sroot[:, c], sms[:, c], stmp[:, c])
                        v.wait_ge(x1_done, l * NT + n + 1)
                        v.tensor_scalar(xn[:, n, :], zt[:, n, 0:D], sroot[:, c], None, ALU.mult).then_inc(xn2, 1)
                    t = n - 1
                    if 0 <= t < NT:
                        v.wait_ge(t2_mm, l * NT + t + 1)
                        modulated(t, bank[4], 2, h2_v)
                v.wait_ge(lg_mm, l * NT + NT)
                v.tensor_reduce(anm[:, :], bank[6][:, 0:NT * EXPERTS].rearrange("p (t e) -> p t e", t=NT), AX_X, ALU.max,
                                negate=True).then_inc(anm_done, 1)
                v.wait_ge(aexp, l + 1)
                link(v.reciprocal(arec[:, :], asum[:, :]))
                v.tensor_tensor(aff[:, :, :], aff[:, :, :], arec[:, :].unsqueeze(2).broadcast_to([P, NT, EXPERTS]),
                                ALU.mult).then_inc(aff_done, 1)
                v.wait_ge(affT_mm, l + 1)
                v.tensor_copy(affT[0][:, 0:LAT], bank[7][0:EXPERTS, :])
                v.tensor_copy(affT[0][:, LAT:TOK], bank[5][0:EXPERTS, 0:P]).then_inc(affT_out, 1)
                hold(v, affT_out, l + 1, const_in)
                for turn in range(CAP_L // 8):
                    now, then = affT[turn % 2], affT[1 - turn % 2]
                    lists = [(a, b, c0 + 8 * turn, c1) for a, b, c0, c1 in ((LAT, TOK, CAP_L, CAP), (0, LAT, 0, CAP_L))
                             if c0 + 8 * turn < c1]
                    for a, b, c, _ in lists:
                        ins = v.max(topv[:, c:c + 8], now[:, a:b])
                    link.held(ins, const_in)
                    for a, b, c, c1 in lists:
                        if c + 8 < c1:
                            v.match_replace(then[:, a:b], topv[:, c:c + 8], now[:, a:b], -1.0)
                        ins = v.max_index(topi[:, c:c + 8], topv[:, c:c + 8], now[:, a:b])
                    link.held(ins, const_in)
                v.tensor_copy(topf[:, 0:CAP_L], topi[:, 0:CAP_L])
                v.tensor_scalar(topf[:, CAP_L:CAP], topi[:, CAP_L:CAP], float(LAT), None, ALU.add).then_inc(top_done, 1)
                v.wait_ge(top_mm, l + 1)
                link(v.tensor_copy(idxT[:, 0:EXPERTS], bank[6][0:CAP, 0:EXPERTS]))
                v.tensor_copy(idxT[:, EXPERTS:EXPERTS + 1], idxT[:, 0:1])
                v.tensor_copy(icur[0][:, :], idxT[:, 0:1]).then_inc(icur_done, 1)
                v.tensor_copy(icur[1][:, :], idxT[:, 1:2]).then_inc(icur_done, 1)
                v.tensor_copy(gateT[:, :], bank[6][0:CAP, EXPERTS:2 * EXPERTS]).then_inc(top_out, 1)
                for dst, n in ((g2e, 3), (s2e, 2)):
                    v.tensor_copy(dst[:, :, 0:CAP_L], mod[:, n, :, 0:1].broadcast_to([P, KC, CAP_L]))
                    ins = v.tensor_copy(dst[:, :, CAP_L:CAP], mod[:, n, :, 1:2].broadcast_to([P, KC, CAP_C]))
                link(ins)

                def rest(m, s, after={}):
                    for c in range(KC):
                        v.wait_ge(high_ready, chunks(l, m, c))
                        v.tensor_tensor(slot_r[s][:, c, :], slot[s][:, c, :], high[c], ALU.subtract).then_inc(low_ready, 1)
                        if c in after:
                            after[c]()

                def rows(x, u):
                    v.wait_ge(xeT_mm, l * EXPERTS + x + 1)
                    if not (isinstance(x, int) and x == EXPERTS - 1):
                        v.tensor_copy(icur[u][:, :], idxT[:, bass.ds(x + 2, 1)]).then_inc(icur_done, 1)
                    for n in range(2):
                        ins = v.tensor_tensor(xt[:, 4 * n:4 * n + 4, :],
                                              bank[6 + n][:, 0:4 * CAP].rearrange("p (c t) -> p c t", c=4),
                                              g2e[:, 4 * n:4 * n + 4, :], ALU.mult)
                    ins.then_inc(xt_scaled, 1)
                    v.wait_ge(xt_scaled, l * EXPERTS + x + 1)
                    v.tensor_tensor(xt, xt, s2e, ALU.add).then_inc(xt_done, 1)

                def rows_rest(x, u):
                    v.wait_ge(xh_done, l * EXPERTS + x + 1)
                    v.tensor_tensor(xeT[u][1], xt, xeT[u][0], ALU.subtract).then_inc(xeT_out, 1)

                def hidden(e):
                    v.wait_ge(chunk_used, AHEAD + chunks(l, w3_at(e), KC - 1))
                    v.wait_ge(silu, l * EXPERTS + e + 1)
                    for n in range(2):
                        a = he[:, n * 512:(n + 1) * 512]
                        ins = v.tensor_tensor(a, a, bank[2 + n][0:CAP, :], ALU.mult)
                    ins.then_inc(he_done, 1)

                def hidden_rest(e):
                    v.wait_ge(hh_done, l * EXPERTS + e + 1)
                    for n in range(2):
                        c = slice(4 * n, 4 * n + 4)
                        ins = v.tensor_tensor(heT[1][:, c, :], bank[6 + n][:, 0:4 * CAP].rearrange("p (c t) -> p c t", c=4),
                                              heT[0][:, c, :], ALU.subtract)
                    ins.then_inc(heT_out, 1)

                def result(e, u):
                    v.wait_ge(rows_free, l * EXPERTS + e + 1)
                    v.tensor_copy(iscat[u][:, :], idxT[:, bass.ds(e, 1)])
                    v.wait_ge(chunk_used, AHEAD + chunks(l, w2_at(e), KC - 1))
                    for n in range(2):
                        ins = v.scalar_tensor_tensor(out=ye[u][:, n * 512:(n + 1) * 512], in0=bank[4 + n][0:CAP, :],
                                                     scalar=gateT[:, bass.ds(e, 1)],
                                                     in1=gate2[:, n * 512:(n + 1) * 512],
                                                     op0=ALU.mult, op1=ALU.mult)
                    ins.then_inc(ye_done, 1)

                def expert(e, u):
                    rest(w1_next_at(e), 0, {2: lambda: rows(e + 1, 1 - u), 3: lambda: rows_rest(e + 1, 1 - u)})
                    hidden(e)
                    rest(w2_at(e), 2, {3: lambda: hidden_rest(e)})
                    rest(w3_at(e + 1), 1)
                    result(e, u)

                rows(0, 0)
                rows_rest(0, 0)
                rest(w3_at(0), 1)
                with v.Fori(0, PAIRS - 1) as k:
                    for u in range(2):
                        expert(k * 2 + u, u)
                expert(EXPERTS - 2, 0)
                rest(w2_at(EXPERTS - 1), 2, {2: lambda: hidden(EXPERTS - 1), 3: lambda: hidden_rest(EXPERTS - 1)})
                result(EXPERTS - 1, 1)
                link.close()

            flink = Chain(v, v_flink, "V_LAST", 0, V_LAST)
            v.wait_ge(fsq, NT)
            flink(v.tensor_scalar(sms[:, 0:NT], ssum[:, 0:NT], 1.0 / D, EPS, ALU.mult, ALU.add))
            v.reciprocal(srec[:, 0:NT], sms[:, 0:NT]).then_inc(frec, 1)
            v.wait_ge(froot, 1)
            newton(flink, sroot[:, 0:NT], sms[:, 0:NT], stmp[:, 0:NT])
            v.wait_ge(g_in, 16)
            for t in range(NT):
                v.scalar_tensor_tensor(out=zt[:, t, 0:D], in0=zt[:, t, 0:D], scalar=sroot[:, t:t + 1],
                                       in1=final_g, op0=ALU.mult, op1=ALU.mult).then_inc(y_out_done, 1)
            flink.close()


def tables():
    import numpy as np

    c = {}
    for name, n in (("", LAT), ("x", CTX)):
        k = np.arange(n, dtype=np.float64)
        half = np.pi / n * np.outer(k + 0.5, k + 0.5)
        whole = np.pi / n * np.outer(k, k + 0.5)
        c[f"dft{name}_cos"], c[f"dft{name}_sin"] = np.cos(half), np.sin(half)
        c[f"fil{name}_cos"], c[f"fil{name}_sin"] = np.cos(whole), np.sin(whole)
    feats, window = [], []
    lo, hi = np.log(1e-2) / 1.5, np.log(1e-2) / 0.3
    deltas = np.abs(np.linspace(lo, hi, HY))
    for n in (LAT, CTX):
        t = np.linspace(0.0, 1.0, n)[:, None]
        bands = (EMB - 1) // 2
        fb = np.linspace(1e-4, bands - 1, bands)[None, :]
        w = 2.0 * np.pi * np.arange(n)[:, None] / n
        feats.append(np.concatenate([t, np.cos(fb * w), -np.sin(fb * w)], axis=-1).T)
        window.append(np.exp(-t * deltas[None, :]))
    c["feats"] = np.concatenate(feats, axis=1)
    c["window"] = np.concatenate(window, axis=0)
    m = np.zeros((P, NCST))
    m[:, C_ID:C_ID + P] = np.eye(P)
    q, j = np.arange(P)[:, None], np.arange(P)[None, :]
    m[:, C_MASK:C_MASK + P] = np.where(j >= q, 0.0, NEG)
    m[:, C_MASK + 3 * P:C_MASK + 4 * P] = np.where(j <= q, 0.0, NEG)
    inv = 10000.0 ** (-np.arange(16) / 16)
    for t in range(4):
        pos = t * P + np.arange(P)
        for h, at in enumerate((pos // 64, pos % 64)):
            ang = at[:, None] * inv[None, :]
            a = C_COS + t * 64 + h * 32
            m[:, a:a + 16] = m[:, a + 16:a + 32] = np.cos(ang)
            a = C_SIN + t * 32 + h * 16
            m[:, a:a + 16] = np.sin(ang)
    c["consts"] = m
    s = np.zeros((5, 2 * P + CAP + 2))
    s[4, 0:2 * P + CAP] = 1.0
    for n in range(2):
        s[n:4:2, n * P:(n + 1) * P] = s[n:4:2, 2 * P + CAP + n] = 1.0
    s[0:4:2, 2 * P:2 * P + CAP_L] = s[1:4:2, 2 * P + CAP_L:2 * P + CAP] = 1.0
    c["sel"] = s
    return {n: a.astype(np.float32) for n, a in c.items()}


_PLAIN = ["x_prompt", "x_sample", "c", "c_ctx", "cache_k", "cache_v", "ada_w", "ada_b", "w_in", "hy_f_w1", "hy_f_w2",
          "hy_f_w3", "hy_bias", "w_out", "router_w", "exp_w1", "exp_w3", "exp_w2", "final_g"]
_OUTS = [("y_prompt", (1, CTX, D)), ("y_sample", (1, LAT, D)),
         ("new_k", (1, DEPTH, CTX, KV, HD)), ("new_v", (1, DEPTH, CTX, KV, HD))]


def kernel(**inputs):
    import numpy as _np
    import concourse.bacc as _bacc
    from concourse import mybir as _mybir
    from concourse.bass_utils import run_bass_kernel_spmd as _run

    arrays = {n: _np.ascontiguousarray(inputs[n]) for n in _PLAIN}
    arrays.update(tables())
    prm = _np.zeros((DEPTH, P, NPRM), _np.float32)
    prm[:, :, G1:G1 + KC] = _np.asarray(inputs["norm1_g"]).reshape(DEPTH, P, KC)
    prm[:, :, G2:G2 + KC] = _np.asarray(inputs["norm2_g"]).reshape(DEPTH, P, KC)
    prm[:, :, GO:GO + KC] = _np.asarray(inputs["out_norm_g"]).reshape(DEPTH, KC, P).transpose(0, 2, 1)
    prm[:, :, CW:CW + 18] = _np.asarray(inputs["hy_conv_w"]).reshape(DEPTH, 18, P).transpose(0, 2, 1)
    prm[:, :, CB:CB + 6] = _np.asarray(inputs["hy_conv_b"]).reshape(DEPTH, 6, P).transpose(0, 2, 1)
    prm[:, :, GB:GB + GH] = _np.asarray(inputs["gm_b"]).transpose(0, 2, 1)
    prm[:, :, SK:SK + HEADS] = _np.asarray(inputs["attn_sink"])[:, None, :]
    prm[:, 0:FH, FB1] = _np.asarray(inputs["hy_f_b1"])
    prm[:, 0:FH, FB2] = _np.asarray(inputs["hy_f_b2"])
    prm[:, 0:FH, FQ] = _np.asarray(inputs["hy_freq"])
    prm[:, :, AB:AB + 4 * KC] = _np.asarray(inputs["ada_b"]).reshape(DEPTH, ADA, P, KC)[:, [0, 1, 3, 4]]\
        .transpose(0, 2, 1, 3).reshape(DEPTH, P, 4 * KC)
    arrays["params"] = prm
    arrays["ws_t"] = _np.ascontiguousarray(_np.asarray(inputs["gm_ws"]).transpose(0, 3, 1, 2).reshape(DEPTH, P, GH * P))

    nc = _bacc.Bacc("TRN2", target_bir_lowering=False, num_devices=1)
    ins, outs, feed = {}, {}, {}
    for n, a in arrays.items():
        feed[f"in_{n}"] = a
        ins[n] = nc.dram_tensor(f"in_{n}", a.shape, _mybir.dt.from_np(a.dtype), kind="ExternalInput").ap()
    for n, shape in _OUTS:
        outs[n] = nc.dram_tensor(f"out_{n}", shape, _mybir.dt.float32, kind="ExternalOutput").ap()
    hybrid_prefix_diffusion_step(nc, ins, outs)
    r = _run(nc, [feed], core_ids=[0])
    return tuple(r.results[0][f"out_{n}"] for n, _ in _OUTS)
```
